# Optimizing a Trainium2 kernel written in Bass

```python
import math
import jax, jax.numpy as jnp
from jax import lax
import numpy as np

D_MODEL = 1024
BATCH = 1
SEQ = 512
DEPTH = 2

N_MEM = 256
HEAD_DIM = 64
ROPE_DIM = HEAD_DIM // 4
ROPE_THETA = 500000.0
RMS_EPS = 1e-6
N_TOK_HEADS = 12
N_MEM_HEADS = 4
MIX_WIDTH = (N_TOK_HEADS + N_MEM_HEADS) * HEAD_DIM
MEM_Q = N_MEM_HEADS * HEAD_DIM
D_FF = ((8 * D_MODEL // 3 + 255) // 256) * 256
Q_BLOCK = 128

DSA_KV_RANK = 128
DSA_NOPE = HEAD_DIM - ROPE_DIM
IDX_HEADS = 8
IDX_DIM = 64
DSA_TOPK_MAX = 256
DSA_COLS = [N_TOK_HEADS * HEAD_DIM, DSA_KV_RANK, ROPE_DIM,
            IDX_HEADS * IDX_DIM, IDX_DIM, IDX_HEADS, MEM_Q]

NSA_GROUPS = 2
NSA_HPG = N_TOK_HEADS // NSA_GROUPS
CMP_LEN = 32
CMP_STRIDE = 16
CMP_HIDDEN = 128
SLC_LEN = 64
SLC_TOP_MAX = 16
WIN = 512
NSA_Q_BLOCK = 64
FORCE_SCORE = 1e9
NSA_KV = NSA_GROUPS * HEAD_DIM
NSA_COLS = [N_TOK_HEADS * HEAD_DIM, NSA_KV, NSA_KV, NSA_KV, NSA_KV, NSA_KV, NSA_KV,
            N_TOK_HEADS * 3, MEM_Q]

N_A = (DEPTH + 1) // 2
N_B = DEPTH // 2


def split_cols(x, sizes):
    return jnp.split(x, np.cumsum(sizes)[:-1].tolist(), axis=-1)

def rmsnorm(x, g):
    xf = x.astype(jnp.float32)
    y = xf * lax.rsqrt(jnp.mean(xf * xf, axis=-1, keepdims=True) + RMS_EPS)
    return (y * g.astype(jnp.float32)).astype(x.dtype)

def rope_tables(S):
    inv = ROPE_THETA ** (-np.arange(0, ROPE_DIM, 2, dtype=np.float64) / ROPE_DIM)
    ang = np.arange(S, dtype=np.float64)[:, None] * inv[None, :]
    return jnp.asarray(np.cos(ang).astype(np.float32)), jnp.asarray(np.sin(ang).astype(np.float32))

def apply_partial_rope(x, cos, sin):
    xr, xp = x[..., :ROPE_DIM], x[..., ROPE_DIM:]
    x1, x2 = xr[..., :ROPE_DIM // 2], xr[..., ROPE_DIM // 2:]
    c, s = cos[:, None, :], sin[:, None, :]
    rot = jnp.concatenate([x1 * c - x2 * s, x1 * s + x2 * c], axis=-1).astype(x.dtype)
    return jnp.concatenate([rot, xp], axis=-1)

def masked_softmax(s, mask):
    s = jnp.where(mask, s.astype(jnp.float32), -jnp.inf)
    m = jnp.max(s, axis=-1, keepdims=True)
    m = jnp.where(jnp.isfinite(m), m, 0.0)
    p = jnp.exp(s - m)
    return p / jnp.maximum(jnp.sum(p, axis=-1, keepdims=True), 1e-30)

def memory_attention(q_mem, mem_n, w_kv_mem):
    B, S, _ = q_mem.shape
    q = q_mem.reshape(B, S, N_MEM_HEADS, HEAD_DIM)
    k, v = jnp.split(mem_n @ w_kv_mem, 2, axis=-1)
    k = k.reshape(B, -1, N_MEM_HEADS, HEAD_DIM)
    v = v.reshape(B, -1, N_MEM_HEADS, HEAD_DIM)
    s = jnp.einsum('bshd,bnhd->bhsn', q, k).astype(jnp.float32) * HEAD_DIM ** -0.5
    p = jax.nn.softmax(s, axis=-1).astype(v.dtype)
    return jnp.einsum('bhsn,bnhd->bshd', p, v).reshape(B, S, MEM_Q)

def dsa_mixer(cols, ckv_norm, w_uk, w_uv, cos, sin):
    q, ckv, k_rope, q_idx, k_idx, w_idx = cols
    B, S, _ = q.shape
    q = apply_partial_rope(q.reshape(B, S, N_TOK_HEADS, HEAD_DIM), cos, sin)
    ckv = rmsnorm(ckv, ckv_norm)
    k_nope = ckv @ w_uk
    v = ckv @ w_uv
    k_r = apply_partial_rope(k_rope[:, :, None, :], cos, sin)[:, :, 0]
    k = jnp.concatenate([k_r, k_nope], axis=-1)
    q_idx = apply_partial_rope(q_idx.reshape(B, S, IDX_HEADS, IDX_DIM), cos, sin)
    k_idx = apply_partial_rope(k_idx[:, :, None, :], cos, sin)[:, :, 0]
    w_idx = w_idx.astype(jnp.float32) * (IDX_HEADS ** -0.5 * IDX_DIM ** -0.5)
    topk = min(DSA_TOPK_MAX, S // 4)
    key_pos = jnp.arange(S)
    gather = jax.vmap(lambda kb, ib: kb[ib])

    def block(i):
        t0 = i * Q_BLOCK
        qpos = t0 + jnp.arange(Q_BLOCK)
        qi = lax.dynamic_slice_in_dim(q, t0, Q_BLOCK, axis=1)
        qii = lax.dynamic_slice_in_dim(q_idx, t0, Q_BLOCK, axis=1)
        wi = lax.dynamic_slice_in_dim(w_idx, t0, Q_BLOCK, axis=1)
        logits = jnp.einsum('bthd,bsd->bths', qii, k_idx).astype(jnp.float32)
        score = jnp.einsum('bths,bth->bts', jax.nn.relu(logits), wi)
        causal = key_pos[None, :] <= qpos[:, None]
        score = jnp.where(causal[None], score, -jnp.inf)
        _, idx = lax.top_k(score, topk)
        k_sel = gather(k, idx)
        v_sel = gather(v, idx)
        valid = idx <= qpos[None, :, None]
        s = jnp.einsum('bthd,btkd->bthk', qi, k_sel) * HEAD_DIM ** -0.5
        p = masked_softmax(s, valid[:, :, None, :]).astype(v.dtype)
        return jnp.einsum('bthk,btkd->bthd', p, v_sel).reshape(B, Q_BLOCK, N_TOK_HEADS * HEAD_DIM)

    out = lax.map(block, jnp.arange(S // Q_BLOCK))
    return out.transpose(1, 0, 2, 3).reshape(B, S, N_TOK_HEADS * HEAD_DIM)

def cmp_to_slc_overlap(n_c, n_slc):
    c0 = np.arange(n_c) * CMP_STRIDE
    s0 = np.arange(n_slc) * SLC_LEN
    ov = np.minimum(c0[:, None] + CMP_LEN, s0[None, :] + SLC_LEN) - np.maximum(c0[:, None], s0[None, :])
    return jnp.asarray((np.clip(ov, 0, None) / CMP_LEN).astype(np.float32))

def compress(kv, pos_emb, w1, w2):
    B, S, G, Dh = kv.shape
    n_c = (S - CMP_LEN) // CMP_STRIDE + 1
    blk = np.arange(n_c)[:, None] * CMP_STRIDE + np.arange(CMP_LEN)[None, :]
    blocks = kv[:, blk] + pos_emb[None, None, :, None, :]
    flat = blocks.transpose(0, 1, 3, 2, 4).reshape(B, n_c, G, CMP_LEN * Dh)
    return jax.nn.gelu(flat @ w1) @ w2

def nsa_mixer(cols, pos_k, pos_v, ck_w1, ck_w2, cv_w1, cv_w2, cos, sin):
    q, kc, vc, ks, vs, kw, vw, gates = cols
    B, S, _ = q.shape
    G, J, Dh = NSA_GROUPS, NSA_HPG, HEAD_DIM
    q = q.reshape(B, S, N_TOK_HEADS, Dh)
    q_rot = apply_partial_rope(q, cos, sin)
    kc, vc = kc.reshape(B, S, G, Dh), vc.reshape(B, S, G, Dh)
    ks = apply_partial_rope(ks.reshape(B, S, G, Dh), cos, sin)
    vs = vs.reshape(B, S, G, Dh)
    kw = apply_partial_rope(kw.reshape(B, S, G, Dh), cos, sin)
    vw = vw.reshape(B, S, G, Dh)
    gates = jax.nn.sigmoid(gates.astype(jnp.float32)).astype(q.dtype).reshape(B, S, G, J, 3)
    scale = Dh ** -0.5

    k_cmp = compress(kc, pos_k, ck_w1, ck_w2)
    v_cmp = compress(vc, pos_v, cv_w1, cv_w2)
    n_c = k_cmp.shape[1]
    cmp_end = jnp.arange(n_c) * CMP_STRIDE + CMP_LEN - 1
    n_slc = S // SLC_LEN
    n_sel = min(SLC_TOP_MAX, n_slc)
    overlap = cmp_to_slc_overlap(n_c, n_slc)
    slc_ids = jnp.arange(n_slc)
    ks_b = ks.reshape(B, n_slc, SLC_LEN, G, Dh).transpose(0, 3, 1, 2, 4)
    vs_b = vs.reshape(B, n_slc, SLC_LEN, G, Dh).transpose(0, 3, 1, 2, 4)
    gather = jax.vmap(jax.vmap(lambda kb, ib: kb[ib]))
    kw_pad = jnp.pad(kw, ((0, 0), (WIN, 0), (0, 0), (0, 0)))
    vw_pad = jnp.pad(vw, ((0, 0), (WIN, 0), (0, 0), (0, 0)))

    def block(i):
        T = NSA_Q_BLOCK
        t0 = i * T
        qpos = t0 + jnp.arange(T)
        qc = lax.dynamic_slice_in_dim(q, t0, T, axis=1).reshape(B, T, G, J, Dh)
        qr = lax.dynamic_slice_in_dim(q_rot, t0, T, axis=1).reshape(B, T, G, J, Dh)
        gi = lax.dynamic_slice_in_dim(gates, t0, T, axis=1)
        s_c = jnp.einsum('btgjd,bcgd->btgjc', qc, k_cmp) * scale
        mask_c = cmp_end[None, :] <= qpos[:, None]
        p_c = masked_softmax(s_c, mask_c[None, :, None, None, :])
        o_c = jnp.einsum('btgjc,bcgd->btgjd', p_c.astype(v_cmp.dtype), v_cmp)
        imp = jnp.einsum('btgjc,cn->btgn', p_c, overlap)
        cur = qpos // SLC_LEN
        forced = (slc_ids[None] == 0) | (slc_ids[None] == cur[:, None]) | (slc_ids[None] == cur[:, None] - 1)
        admissible = slc_ids[None] <= cur[:, None]
        imp = jnp.where(forced[None, :, None, :], FORCE_SCORE, imp)
        imp = jnp.where(admissible[None, :, None, :], imp, -jnp.inf)
        _, sel = lax.top_k(imp, n_sel)
        sel_g = sel.transpose(0, 2, 1, 3)
        k_sel = gather(ks_b, sel_g).reshape(B, G, T, n_sel * SLC_LEN, Dh)
        v_sel = gather(vs_b, sel_g).reshape(B, G, T, n_sel * SLC_LEN, Dh)
        tok_pos = (sel_g[..., None] * SLC_LEN + jnp.arange(SLC_LEN)).reshape(B, G, T, n_sel * SLC_LEN)
        mask_s = tok_pos <= qpos[None, None, :, None]
        s_s = jnp.einsum('btgjd,bgtkd->bgtjk', qr, k_sel) * scale
        p_s = masked_softmax(s_s, mask_s[:, :, :, None, :]).astype(v_sel.dtype)
        o_s = jnp.einsum('bgtjk,bgtkd->btgjd', p_s, v_sel)
        kw_i = lax.dynamic_slice_in_dim(kw_pad, t0, WIN + T, axis=1)
        vw_i = lax.dynamic_slice_in_dim(vw_pad, t0, WIN + T, axis=1)
        kpos = t0 - WIN + jnp.arange(WIN + T)
        mask_w = (kpos[None] <= qpos[:, None]) & (kpos[None] > qpos[:, None] - WIN) & (kpos[None] >= 0)
        s_w = jnp.einsum('btgjd,bkgd->btgjk', qr, kw_i) * scale
        p_w = masked_softmax(s_w, mask_w[None, :, None, None, :]).astype(vw_i.dtype)
        o_w = jnp.einsum('btgjk,bkgd->btgjd', p_w, vw_i)
        o = gi[..., 0:1] * o_c + gi[..., 1:2] * o_s + gi[..., 2:3] * o_w
        return o.reshape(B, T, N_TOK_HEADS * Dh)

    out = lax.map(block, jnp.arange(S // NSA_Q_BLOCK))
    return out.transpose(1, 0, 2, 3).reshape(B, S, N_TOK_HEADS * HEAD_DIM)

def first_inputs(seed: int = 0) -> dict:
    key = jax.random.key(seed)
    ks = jax.random.split(key, 24)

    def w(k, shape, fan_in):
        return jax.random.normal(k, shape, jnp.float32) * fan_in ** -0.5

    def gain(k, shape):
        return 1.0 + 0.02 * jax.random.normal(k, shape, jnp.float32)

    return {
        "x": jax.random.normal(ks[0], (BATCH, SEQ, D_MODEL), jnp.float32),
        "mem": jax.random.normal(ks[1], (BATCH, N_MEM, D_MODEL), jnp.float32),
        "attn_norm": gain(ks[2], (DEPTH, D_MODEL)),
        "mem_norm": gain(ks[3], (DEPTH, D_MODEL)),
        "ffn_norm": gain(ks[4], (DEPTH, D_MODEL)),
        "final_norm": gain(ks[5], (D_MODEL,)),
        "dsa_w_in": w(ks[6], (N_A, D_MODEL, sum(DSA_COLS)), D_MODEL),
        "dsa_ckv_norm": gain(ks[7], (N_A, DSA_KV_RANK)),
        "dsa_w_uk": w(ks[8], (N_A, DSA_KV_RANK, DSA_NOPE), DSA_KV_RANK),
        "dsa_w_uv": w(ks[9], (N_A, DSA_KV_RANK, HEAD_DIM), DSA_KV_RANK),
        "nsa_w_in": w(ks[10], (N_B, D_MODEL, sum(NSA_COLS)), D_MODEL),
        "nsa_cmp_pos_k": 0.1 * jax.random.normal(ks[11], (N_B, CMP_LEN, HEAD_DIM), jnp.float32),
        "nsa_cmp_pos_v": 0.1 * jax.random.normal(ks[12], (N_B, CMP_LEN, HEAD_DIM), jnp.float32),
        "nsa_cmp_k_w1": w(ks[13], (N_B, CMP_LEN * HEAD_DIM, CMP_HIDDEN), CMP_LEN * HEAD_DIM),
        "nsa_cmp_k_w2": w(ks[14], (N_B, CMP_HIDDEN, HEAD_DIM), CMP_HIDDEN),
        "nsa_cmp_v_w1": w(ks[15], (N_B, CMP_LEN * HEAD_DIM, CMP_HIDDEN), CMP_LEN * HEAD_DIM),
        "nsa_cmp_v_w2": w(ks[16], (N_B, CMP_HIDDEN, HEAD_DIM), CMP_HIDDEN),
        "mem_w_kv": w(ks[17], (DEPTH, D_MODEL, 2 * MEM_Q), D_MODEL),
        "w_o": w(ks[18], (DEPTH, MIX_WIDTH, D_MODEL), MIX_WIDTH),
        "ffn_w_in": w(ks[19], (DEPTH, D_MODEL, 2 * D_FF), D_MODEL),
        "ffn_w_down": w(ks[20], (DEPTH, D_FF, D_MODEL), D_FF),
    }

def first_block(x, mem, attn_norm, mem_norm, ffn_norm, final_norm,
              dsa_w_in, dsa_ckv_norm, dsa_w_uk, dsa_w_uv,
              nsa_w_in, nsa_cmp_pos_k, nsa_cmp_pos_v,
              nsa_cmp_k_w1, nsa_cmp_k_w2, nsa_cmp_v_w1, nsa_cmp_v_w2,
              mem_w_kv, w_o, ffn_w_in, ffn_w_down):
    S = x.shape[1]
    cos, sin = rope_tables(S)
    for i in range(DEPTH):
        h = rmsnorm(x, attn_norm[i])
        mem_n = rmsnorm(mem, mem_norm[i])
        if i % 2 == 0:
            a = i // 2
            cols = split_cols(h @ dsa_w_in[a], DSA_COLS)
            q_mem = cols[-1]
            tok = dsa_mixer(cols[:-1], dsa_ckv_norm[a], dsa_w_uk[a], dsa_w_uv[a], cos, sin)
        else:
            b = i // 2
            cols = split_cols(h @ nsa_w_in[b], NSA_COLS)
            q_mem = cols[-1]
            tok = nsa_mixer(cols[:-1], nsa_cmp_pos_k[b], nsa_cmp_pos_v[b],
                            nsa_cmp_k_w1[b], nsa_cmp_k_w2[b], nsa_cmp_v_w1[b], nsa_cmp_v_w2[b],
                            cos, sin)
        o_mem = memory_attention(q_mem, mem_n, mem_w_kv[i])
        x = x + jnp.concatenate([tok, o_mem], axis=-1) @ w_o[i]
        h = rmsnorm(x, ffn_norm[i])
        g, u = jnp.split(h @ ffn_w_in[i], 2, axis=-1)
        x = x + (jax.nn.silu(g) * u) @ ffn_w_down[i]
    return rmsnorm(x, final_norm)


N_MIXERS = 2
N_GLA_LAYERS = (DEPTH + 1) // 2
N_SWA_LAYERS = DEPTH // 2

GLA_HEADS = 4
GLA_DK = D_MODEL // 2
GLA_DV = D_MODEL
GLA_HK = GLA_DK // GLA_HEADS
GLA_HV = GLA_DV // GLA_HEADS
GLA_GATE_RANK = 16
GLA_GATE_NORMALIZER = 16.0
GLA_CHUNK = 64
GLA_IN = 2 * GLA_DK + 2 * GLA_DV + GLA_GATE_RANK

SWA_HEAD_DIM = 64
SWA_Q_HEADS = D_MODEL // SWA_HEAD_DIM
SWA_GROUP = 8
SWA_KV_HEADS = SWA_Q_HEADS // SWA_GROUP
SWA_WINDOW = 128
SWA_BLOCK = SWA_WINDOW
SWA_IN = (SWA_Q_HEADS + 2 * SWA_KV_HEADS) * SWA_HEAD_DIM

D_FF_2 = 4 * D_MODEL
NORM_EPS = 1e-6


def rms_norm(x, w):
    xf = x.astype(jnp.float32)
    y = xf * lax.rsqrt(jnp.mean(xf * xf, axis=-1, keepdims=True) + NORM_EPS)
    return (y * w.astype(jnp.float32)).astype(x.dtype)

def gla_mixer(h, w_in, w_gate_up, b_gate_up, g_norm, w_out):
    B, T, _ = h.shape
    nc = T // GLA_CHUNK
    proj = h @ w_in
    q, k, v, g, glr = jnp.split(
        proj, [GLA_DK, 2 * GLA_DK, 2 * GLA_DK + GLA_DV, 2 * GLA_DK + 2 * GLA_DV], axis=-1)
    log_a = jax.nn.log_sigmoid((glr @ w_gate_up + b_gate_up).astype(jnp.float32)) / GLA_GATE_NORMALIZER

    def chunks(t, d):
        return t.reshape(B, nc, GLA_CHUNK, GLA_HEADS, d).astype(jnp.float32)

    qc = chunks(q, GLA_HK) * (GLA_HK ** -0.5)
    kc = chunks(k, GLA_HK)
    vc = chunks(v, GLA_HV)
    bc = jnp.cumsum(chunks(log_a, GLA_HK), axis=2)
    b_last = bc[:, :, -1:]
    q_dec = qc * jnp.exp(bc)
    k_inv = kc * jnp.exp(-bc)
    k_end = kc * jnp.exp(b_last - bc)

    causal = jnp.tril(jnp.ones((GLA_CHUNK, GLA_CHUNK), dtype=bool))
    att = jnp.einsum('bncha,bnsha->bnhcs', q_dec, k_inv)
    att = jnp.where(causal, att, 0.0)
    o_intra = jnp.einsum('bnhcs,bnshv->bnchv', att, vc)

    dS = jnp.einsum('bncha,bnchv->bnhav', k_end, vc)
    decay = jnp.exp(b_last[:, :, 0])

    def step(S, inp):
        dS_n, dec_n = inp
        return S * dec_n[..., None] + dS_n, S

    S0 = jnp.zeros((B, GLA_HEADS, GLA_HK, GLA_HV), jnp.float32)
    _, S_prev = lax.scan(step, S0, (jnp.moveaxis(dS, 1, 0), jnp.moveaxis(decay, 1, 0)))
    S_prev = jnp.moveaxis(S_prev, 0, 1)
    o_inter = jnp.einsum('bncha,bnhav->bnchv', q_dec, S_prev)

    o = (o_intra + o_inter).reshape(B, T, GLA_HEADS, GLA_HV)
    o = rms_norm(o, g_norm).reshape(B, T, GLA_DV)
    o = o * jax.nn.silu(g.astype(jnp.float32))
    return o.astype(h.dtype) @ w_out

def swa_sink_mixer(h, w_in, b_in, sinks, w_out, b_out):
    B, T, _ = h.shape
    nb = T // SWA_BLOCK
    proj = h @ w_in + b_in
    q, k, v = jnp.split(
        proj, [SWA_Q_HEADS * SWA_HEAD_DIM, (SWA_Q_HEADS + SWA_KV_HEADS) * SWA_HEAD_DIM], axis=-1)
    q = q.reshape(B, nb, SWA_BLOCK, SWA_KV_HEADS, SWA_GROUP, SWA_HEAD_DIM)

    def banded(t):
        t = t.reshape(B, nb, SWA_BLOCK, SWA_KV_HEADS, SWA_HEAD_DIM)
        prev = jnp.pad(t[:, :-1], ((0, 0), (1, 0), (0, 0), (0, 0), (0, 0)))
        return jnp.concatenate([prev, t], axis=2)

    kb, vb = banded(k), banded(v)
    s = jnp.einsum('bnqkgd,bnskd->bnkgqs', q, kb).astype(jnp.float32) * (SWA_HEAD_DIM ** -0.5)
    qi = jnp.arange(SWA_BLOCK)[:, None]
    sj = jnp.arange(2 * SWA_BLOCK)[None, :]
    band = (sj > qi) & (sj <= qi + SWA_WINDOW)
    not_first = jnp.arange(nb)[:, None, None] > 0
    valid = band[None] & (not_first | (sj >= SWA_BLOCK)[None])
    s = jnp.where(valid[None, :, None, None], s, -jnp.inf)

    sink = sinks.astype(jnp.float32).reshape(SWA_KV_HEADS, SWA_GROUP)[None, None, :, :, None, None]
    mx = jnp.maximum(jnp.max(s, axis=-1, keepdims=True), sink)
    e = jnp.exp(s - mx)
    p = e / (jnp.sum(e, axis=-1, keepdims=True) + jnp.exp(sink - mx))
    o = jnp.einsum('bnkgqs,bnskd->bnqkgd', p.astype(vb.dtype), vb)
    return o.reshape(B, T, SWA_Q_HEADS * SWA_HEAD_DIM) @ w_out + b_out

def sq_relu_mlp(h, w_up, w_down):
    return jnp.square(jax.nn.relu(h @ w_up)) @ w_down

def second_inputs(seed: int = 0) -> dict:
    key = jax.random.key(seed)
    ks = jax.random.split(key, 20)

    def dense(k, shape, fan_in):
        return jax.random.normal(k, shape, jnp.float32) * (fan_in ** -0.5)

    def gain(k, shape):
        return 1.0 + 0.05 * jax.random.normal(k, shape, jnp.float32)

    def bias(k, shape):
        return 0.02 * jax.random.normal(k, shape, jnp.float32)

    return {
        "x": jax.random.normal(ks[0], (BATCH, SEQ, D_MODEL), jnp.float32),
        "ln_mix_pre": gain(ks[1], (DEPTH, D_MODEL)),
        "ln_mix_post": gain(ks[2], (DEPTH, D_MODEL)),
        "ln_mlp_pre": gain(ks[3], (DEPTH, D_MODEL)),
        "ln_mlp_post": gain(ks[4], (DEPTH, D_MODEL)),
        "gla_w_in": dense(ks[5], (N_GLA_LAYERS, D_MODEL, GLA_IN), D_MODEL),
        "gla_w_gate_up": dense(ks[6], (N_GLA_LAYERS, GLA_GATE_RANK, GLA_DK), GLA_GATE_RANK),
        "gla_b_gate_up": bias(ks[7], (N_GLA_LAYERS, GLA_DK)),
        "gla_g_norm": gain(ks[8], (N_GLA_LAYERS, GLA_HV)),
        "gla_w_out": dense(ks[9], (N_GLA_LAYERS, GLA_DV, D_MODEL), GLA_DV),
        "swa_w_in": dense(ks[10], (N_SWA_LAYERS, D_MODEL, SWA_IN), D_MODEL),
        "swa_b_in": bias(ks[11], (N_SWA_LAYERS, SWA_IN)),
        "swa_sinks": 0.5 * jax.random.normal(ks[12], (N_SWA_LAYERS, SWA_Q_HEADS), jnp.float32),
        "swa_w_out": dense(ks[13], (N_SWA_LAYERS, SWA_Q_HEADS * SWA_HEAD_DIM, D_MODEL), SWA_Q_HEADS * SWA_HEAD_DIM),
        "swa_b_out": bias(ks[14], (N_SWA_LAYERS, D_MODEL)),
        "mlp_w_up": dense(ks[15], (DEPTH, D_MODEL, D_FF_2), D_MODEL),
        "mlp_w_down": dense(ks[16], (DEPTH, D_FF_2, D_MODEL), D_FF_2),
    }

def second_block(x, ln_mix_pre, ln_mix_post, ln_mlp_pre, ln_mlp_post,
              gla_w_in, gla_w_gate_up, gla_b_gate_up, gla_g_norm, gla_w_out,
              swa_w_in, swa_b_in, swa_sinks, swa_w_out, swa_b_out,
              mlp_w_up, mlp_w_down):
    for i in range(DEPTH):
        j = i // N_MIXERS
        h = rms_norm(x, ln_mix_pre[i])
        if i % N_MIXERS == 0:
            m = gla_mixer(h, gla_w_in[j], gla_w_gate_up[j], gla_b_gate_up[j], gla_g_norm[j], gla_w_out[j])
        else:
            m = swa_sink_mixer(h, swa_w_in[j], swa_b_in[j], swa_sinks[j], swa_w_out[j], swa_b_out[j])
        x = x + rms_norm(m, ln_mix_post[i]).astype(x.dtype)
        h = rms_norm(x, ln_mlp_pre[i])
        f = sq_relu_mlp(h, mlp_w_up[i], mlp_w_down[i])
        x = x + rms_norm(f, ln_mlp_post[i]).astype(x.dtype)
    return x


def setup_inputs(seed=0):
    out = dict(first_inputs(seed))
    for name, value in second_inputs(seed + 1).items():
        if name != "x":
            out[name + "_2"] = value
    return out


def reference(
    x, mem, attn_norm, mem_norm, ffn_norm, final_norm, dsa_w_in, dsa_ckv_norm, dsa_w_uk,
    dsa_w_uv, nsa_w_in, nsa_cmp_pos_k, nsa_cmp_pos_v, nsa_cmp_k_w1, nsa_cmp_k_w2, nsa_cmp_v_w1,
    nsa_cmp_v_w2, mem_w_kv, w_o, ffn_w_in, ffn_w_down, ln_mix_pre_2, ln_mix_post_2,
    ln_mlp_pre_2, ln_mlp_post_2, gla_w_in_2, gla_w_gate_up_2, gla_b_gate_up_2, gla_g_norm_2,
    gla_w_out_2, swa_w_in_2, swa_b_in_2, swa_sinks_2, swa_w_out_2, swa_b_out_2, mlp_w_up_2,
    mlp_w_down_2,
):
    x = first_block(
        x, mem, attn_norm, mem_norm, ffn_norm, final_norm, dsa_w_in, dsa_ckv_norm, dsa_w_uk,
        dsa_w_uv, nsa_w_in, nsa_cmp_pos_k, nsa_cmp_pos_v, nsa_cmp_k_w1, nsa_cmp_k_w2,
        nsa_cmp_v_w1, nsa_cmp_v_w2, mem_w_kv, w_o, ffn_w_in, ffn_w_down,
    )
    return second_block(
        x, ln_mix_pre_2, ln_mix_post_2, ln_mlp_pre_2, ln_mlp_post_2, gla_w_in_2,
        gla_w_gate_up_2, gla_b_gate_up_2, gla_g_norm_2, gla_w_out_2, swa_w_in_2, swa_b_in_2,
        swa_sinks_2, swa_w_out_2, swa_b_out_2, mlp_w_up_2, mlp_w_down_2,
    )


_drawn_inputs = setup_inputs


def setup_inputs(seed=0):
    import zlib

    import numpy as np

    out = dict(_drawn_inputs(seed))
    spreads = {}
    factors = {'mem_norm': 8.0,
     'dsa_ckv_norm': 4.453,
     'nsa_cmp_pos_k': 64.0,
     'gla_b_gate_up_2': 8.0,
     'swa_sinks_2': 8.0,
     'ffn_norm': 3.913,
     'nsa_cmp_pos_v': 5.606,
     'nsa_cmp_k_w1': 4.038,
     'nsa_cmp_k_w2': 3.84}
    for name, (base, spread) in spreads.items():
        noise = np.random.default_rng([zlib.crc32(name.encode()), seed]).standard_normal(out[name].shape)
        drawn = base * np.exp(spread * noise) if base else spread * noise
        out[name] = __import__('jax').numpy.asarray(drawn.astype(out[name].dtype))
    for name, factor in factors.items():
        out[name] = (out[name] * factor).astype(out[name].dtype)
    return out
```

```python
import math
from contextlib import ExitStack

import numpy as np

import concourse.bass as bass
from concourse import mybir

F32 = mybir.dt.float32
F32R = mybir.dt.float32r
BF16 = mybir.dt.bfloat16
I32 = mybir.dt.int32
ALU = mybir.AluOpType
ACT = mybir.ActivationFunctionType
AX = mybir.AxisListType

P = 128
SEQ, D, N_MEM, DEPTH = 512, 1024, 256, 2
KT = D // P
TT = SEQ // P
HD, ROPE = 64, 16
TOK_HEADS, MEM_HEADS = 12, 4
RANK, IDX_HEADS, IDX_DIM, TOPK = 128, 8, 64, 128
D_FF, D_FF2 = 2816, 4096
FT = D_FF // P
HALF_FT = D_FF2 // P // 2
N_CMP = (SEQ - 32) // 16 + 1
CMP_PAIRS = 16
GLA_HEADS, GLA_CHUNK = 4, 64
N_CHUNK = SEQ // GLA_CHUNK
GATE_NORM = 16.0
SWA_PAIRS = 8
EPS = 1e-6
NEG = -1e30
SCALE = HD ** -0.5
RING = 4
RAW = 2
AHEAD = RING - 1

GAINS = ["attn0", "attn1", "ffn0", "ffn1", "final", "mem0", "mem1", "mixpre0", "mixpre1", "mixpost0",
         "mixpost1", "mlppre0", "mlppre1", "mlppost0", "mlppost1", "swa_b_out", "swa_b_q"]
EXTRA = ["ckv", "gla_b0", "gla_b1", "gla_b2", "gla_b3", "gla_n0", "gla_n1", "swa_bk0", "swa_bk1"]
N_COLS = len(GAINS) * KT + len(EXTRA)


def plan():
    jobs = [("memsum", 0)]
    for l in range(DEPTH):
        jobs += [(f"mk{l}.{j}", 1) for j in range(2)] + [(f"mv{l}.{j}", 1) for j in range(2)]
    jobs += [("sum.attn0", 0)]
    jobs += [("ckv", 1), ("ckvsum", 0), ("kidx", 1)] + [(f"qidx{j}", 1) for j in range(4)]
    jobs += [("rope.kidx", 0)] + [(f"rope.qidx{j}", 0) for j in range(4)]
    jobs += [("widx", 1), ("dsa_k", 1), ("dsa_v", 0), ("rope.dsa_k", 0)]
    jobs += [(f"q0.{j}", 1) for j in range(6)] + [(f"rope.q0.{j}", 0) for j in range(6)]
    jobs += [(f"qmem0.{j}", 1) for j in range(2)]
    for l in range(DEPTH):
        if l == 1:
            for s in ("kc", "vc"):
                jobs += [(f"{s}{g}", 1) for g in range(2)]
            jobs += [(f"ks{g}", 1) for g in range(2)] + [(f"kw{g}", 1) for g in range(2)]
            jobs += [("cmp_hk", 0), ("cmp_hv", 0)]
            jobs += [(f"rope.ks{g}", 0) for g in range(2)] + [(f"rope.kw{g}", 0) for g in range(2)]
            jobs += [("cmp_k", 0), ("cmp_v", 0)]
            jobs += [(f"q1.{j}", 1) for j in range(6)]
            jobs += [("vs", 1), ("vw", 1), ("gates", 1)] + [(f"rope.q1.{j}", 0) for j in range(6)]
            jobs += [(f"qmem1.{j}", 1) for j in range(2)]
        jobs += [(f"cat{l}.{j}", 0) for j in range(KT)]
        jobs += [(f"wo{l}.{j}", 1) for j in range(KT)]
        jobs += [(f"sum.ffn{l}", 0)]
        jobs += [(f"up{l}.{j}", 1) for j in range(2 * FT)]
        jobs += [(f"down{l}.{j}", 3) for j in range(KT)]
        jobs += [("sum.attn1" if l == 0 else "sum.final", 0)]
    jobs += [("sum.mixpre0", 0), ("glr", 1)]
    jobs += [(f"gk{h}", 1) for h in range(4)] + [(f"gq{h}", 1) for h in range(4)]
    for h in range(4):
        jobs += [(f"gz{h}", 0), (f"gv{2 * h}", 1), (f"gv{2 * h + 1}", 1)]
    jobs += [(f"gg{j}", 1) for j in range(KT)]
    for h in range(4):
        jobs += [(f"gket{h}", 0), (f"gatt{h}", 0)]
        jobs += [(f"gds{h}.{n}", 0) for n in range(N_CHUNK - 1)]
        jobs += [(f"go{h}.{j}", 0) for j in range(2)] + [(f"gosum{h}", 0)]
    for l in range(DEPTH):
        if l == 1:
            jobs += [("sum.mixpre1", 0)] + [(f"sk{g}", 1) for g in range(2)] + [("sv", 1)]
            jobs += [(f"sq{j}", 1) for j in range(KT)] + [(f"scat.{j}", 0) for j in range(KT)]
        jobs += [(f"mix{l}.{j}", 1) for j in range(KT)]
        jobs += [(f"sum.mixpost{l}", 0), (f"sum.mlppre{l}", 0)]
        for half in range(2):
            jobs += [(f"mup{l}{half}.{j}", 1) for j in range(HALF_FT)]
            jobs += [(f"mdown{l}{half}.{j}", 2) for j in range(KT)]
        jobs += [(f"sum.mlppost{l}", 0)]
    return jobs


JOBS = plan()
JOB, CHUNK, SMALL = {}, {}, {}
_chunks = _small = 0
for _n, (_name, _c) in enumerate(JOBS):
    JOB[_name], CHUNK[_name], SMALL[_name] = _n, _chunks, _small
    _chunks += _c
    _small += _c == 0
N_CHUNKS = _chunks

SUMS = ["mem", "attn0", "ffn0", "attn1", "ffn1", "final", "mixpre0", "mixpost0", "mlppre0", "mlppost0",
        "mixpre1", "mixpost1", "mlppre1", "mlppost1"]
NORMS = ["mem0", "mem1", "attn0", "ffn0", "attn1", "ffn1", "mixpre0", "mlppre0", "mixpre1", "mlppre1"]
UNITS = [("dsa", 48), ("mem0", 16), ("nsa0", 72), ("nsa1", 72), ("mem1", 16), ("swa0", 32), ("swa1", 32)]
UNIT0 = {n: sum(c for _, c in UNITS[:k]) for k, (n, _) in enumerate(UNITS)}
PAIR0 = {"dsa": 0, "mem0": 6, "nsa0": 8, "nsa1": 11, "mem1": 14, "swa0": 16, "swa1": 20}


def attention_unit(kind, u):
    if kind.startswith("nsa"):
        return u // 12, u // 3 % 4, u % 3
    return u // 4, u % 4, 1


def key_tiles(kind, qt, branch):
    if kind.startswith("mem"):
        return list(range(N_MEM // P))
    if kind.startswith("swa"):
        return [qt - 1, qt] if qt else [0]
    return list(range(qt + 1))


def program(nc, A):
    with ExitStack() as ctx:
        def sb(name, shape, dt=F32, where=ctx):
            return where.enter_context(nc.sbuf_tensor(name, shape, dt))

        def sem(name):
            return ctx.enter_context(nc.semaphore(name))

        x = sb("x", [P, KT, SEQ])
        h_hi = sb("h_hi", [P, KT, SEQ], F32R)
        h_lo = sb("h_lo", [P, KT, SEQ], F32R)
        tmp = sb("tmp", [P, 2, SEQ])
        sq = sb("sq", [P, 2, SEQ])
        sqacc = sb("sqacc", [P, SEQ])
        std = sb("std", [P, SEQ])
        rstd = sb("rstd", [P, SEQ])
        w_raw = sb("w_raw", [P, RAW, KT * P])
        w_hi = sb("w_hi", [P, RING, KT * P], F32R)
        w_lo = sb("w_lo", [P, RING, KT * P], F32R)
        ident = sb("ident", [P, P])
        perm = sb("perm", [P, P])
        rope_c = sb("rope_c", [P, SEQ])
        rope_s = sb("rope_s", [P, SEQ])
        masks = sb("masks", [P, 2 * P + TT * 32])
        masks_b = sb("masks_b", [P, 2 * P + TT * 32], BF16)
        ident_b = sb("ident_b", [P, P], BF16)
        ones = sb("ones", [P, P])
        eps = sb("eps", [P, 1])
        cols = sb("cols", [P, N_COLS])
        w_uk = sb("w_uk", [P, P])
        w_uv = sb("w_uv", [P, HD])
        sinks = sb("sinks", [P, 16])
        nsinks = sb("nsinks", [P, 16])
        k_mem = sb("k_mem", [P, DEPTH, 2, N_MEM])
        v_mem = sb("v_mem", [P, DEPTH, 2, 2 * P])
        nmax = sb("nmax", [P, 4])
        rawmax = sb("rawmax", [P, 4])
        psum_p = sb("psum_p", [P, 4])
        sinkexp = sb("sinkexp", [P, 4])
        rinv = sb("rinv", [P, 4])
        oscale = sb("oscale", [P, 4])

        def attention_memory(where, n):
            return (sb(f"qs{n}", [P, SEQ], where=where), sb(f"prob{n}", [P, 2, SEQ], where=where),
                    sb(f"probT{n}", [P, 2, SEQ], where=where), sb(f"o_tok{n}", [P, TT, D], where=where))

        with ExitStack() as s:
            memx = sb("memx", [P, KT, N_MEM], where=s)
            mem_hi = [sb(f"mem_hi{l}", [P, KT, N_MEM], F32R, s) for l in range(DEPTH)]
            mem_lo = [sb(f"mem_lo{l}", [P, KT, N_MEM], F32R, s) for l in range(DEPTH)]
        with ExitStack() as s:
            q0 = sb("q0", [P, 6, SEQ], where=s)
            qmem0 = sb("qmem0", [P, 2, SEQ], where=s)
            ckv = sb("ckv", [P, SEQ], where=s)
            ckv_n = sb("ckv_n", [P, SEQ], where=s)
            dsa_k = sb("dsa_k", [P, SEQ], where=s)
            qidx = sb("qidx", [P, 4, SEQ], where=s)
            kidx = sb("kidx", [P, SEQ], where=s)
            widx = sb("widx", [P, TT, IDX_HEADS], where=s)
            dsa_v = sb("dsa_v", [P, TT, HD], where=s)
            score = sb("score", [P, SEQ], where=s)
            top8 = sb("top8", [P, 8], where=s)
            relu_l = sb("relu_l", [P, 2, SEQ], where=s)
            dsa_mask = sb("dsa_mask", [P, TT, SEQ], BF16, s)
            rope_t0 = sb("rope_t0", [P, 2, SEQ], where=s)
            qs0, prob0, probT0, o_tok0 = attention_memory(s, 0)
        with ExitStack() as s:
            act_hi = sb("act_hi", [P, FT, SEQ], F32R, s)
            act_lo = sb("act_lo", [P, FT, SEQ], F32R, s)
        with ExitStack() as s:
            q1 = sb("q1", [P, 6, SEQ], where=s)
            q1r = sb("q1r", [P, 6, SEQ], where=s)
            qmem1 = sb("qmem1", [P, 2, SEQ], where=s)
            ks = sb("ks", [P, 2, SEQ], where=s)
            kw = sb("kw", [P, 2, SEQ], where=s)
            vs = sb("vs", [P, TT, P], where=s)
            vw = sb("vw", [P, TT, P], where=s)
            gates = sb("gates", [P, TT, 3 * TOK_HEADS], where=s)
            k_cmp = sb("k_cmp", [P, 2 * N_CMP], where=s)
            v_cmp = sb("v_cmp", [N_CMP, 2, HD], where=s)
            rope_t1 = sb("rope_t1", [P, 2, SEQ], where=s)
            qr1 = sb("qr1", [P, SEQ], where=s)
            with ExitStack() as s2:
                cmp_w1 = [sb(f"cmp_w1{c}", [P, CMP_PAIRS, P], where=s2) for c in "kv"]
                cmp_w2k = sb("cmp_w2k", [P, P], where=s2)
                cmp_w2v = sb("cmp_w2v", [P, HD], where=s2)
                cmp_pos = [sb(f"cmp_pos{c}", [P, CMP_PAIRS], where=s2) for c in "kv"]
                cmp_x = [sb(f"cmp_x{c}", [P, CMP_PAIRS, 2, N_CMP], where=s2) for c in "kv"]
                cmp_h = [sb(f"cmp_h{c}", [P, 2 * N_CMP], where=s2) for c in "kv"]
            qs1, prob1, probT1, o_tok1 = attention_memory(s, 1)
        with ExitStack() as s:
            gq = sb("gq", [P, 4, SEQ], where=s)
            gk = sb("gk", [P, 4, SEQ], where=s)
            gv = sb("gv", [P, TT, D], where=s)
            gsilu = sb("gsilu", [P, KT, SEQ], where=s)
            glr = sb("glr", [P, SEQ], where=s)
            w_gate = sb("w_gate", [16, 4 * P], where=s)
            gla_mask = sb("gla_mask", [P, P], I32, s)
            g_ab = sb("g_ab", [P, SEQ], where=s)
            g_la = sb("g_la", [P, SEQ], where=s)
            g_cum = sb("g_cum", [P, SEQ], where=s)
            g_exp = sb("g_exp", [P, SEQ], where=s)
            g_o = sb("g_o", [P, 2, SEQ], where=s)
            g_inv, g_end = g_o[:, 0, :], g_o[:, 1, :]
            g_reset = sb("g_reset", [P, SEQ], where=s)
            k_inv = sb("k_inv", [P, 4, SEQ], where=s)
            decay = sb("decay", [P, 4, N_CHUNK], where=s)
            k_endT = sb("k_endT", [P, TT, P], where=s)
            state = sb("state", [P, N_CHUNK, 2 * P], where=s)
            attT = sb("attT", [P, TT, P], where=s)
        with ExitStack() as s:
            sq_q = sb("sq_q", [P, KT, SEQ], where=s)
            sk = sb("sk", [P, 2, SEQ], where=s)
            sv = sb("sv", [P, TT, P], where=s)
            sv_b = sb("sv_b", [1, P], where=s)
            one_row = sb("one_row", [1, P], where=s)
            qs2, prob2, probT2, o_tok2 = attention_memory(s, 2)
        with ExitStack() as s:
            mact_hi = sb("mact_hi", [P, HALF_FT, SEQ], F32R, s)
            mact_lo = sb("mact_lo", [P, HALF_FT, SEQ], F32R, s)
            m = sb("m", [P, KT, SEQ], where=s)

        bank = [ctx.enter_context(nc.psum_tensor(f"bank{b}", [P, SEQ], F32)) for b in range(8)]
        score_bank, probT_bank, o_bank = bank[2:4], bank[4:6], bank[6:8]

        consts_in, mem_in, x_in = sem("consts_in"), sem("mem_in"), sem("x_in")
        cmp_in, gla_in, swa_in = sem("cmp_in"), sem("gla_in"), sem("swa_in")
        raw_loaded = [sem(f"raw_loaded{b}") for b in range(RAW)]
        hi_ready, lo_ready = sem("hi_ready"), sem("lo_ready")
        chunks_used = sem("chunks_used")
        small_done = sem("small_done")
        evacuated = [sem(f"evacuated{b}") for b in range(2)]
        consts_made = sem("consts_made")
        sq_done, sq_added = sem("sq_done"), sem("sq_added")
        h_made, h_rounded, h_ready = sem("h_made"), sem("h_rounded"), sem("h_ready")
        act_made, act_rounded, act_ready = sem("act_made"), sem("act_rounded"), sem("act_ready")
        x_normed, x_added = sem("x_normed"), sem("x_added")
        ckv_normed, roped = sem("ckv_normed"), sem("roped")
        idx_ready, idx_relu, idx_added, idx_chain = sem("idx_ready"), sem("idx_relu"), sem("idx_added"), sem("idx_chain")
        dsa_masked = sem("dsa_masked")
        q_staged = sem("q_staged")
        scores_ready, max_ready, probs_ready = sem("scores_ready"), sem("max_ready"), sem("probs_ready")
        transposed, pv_done, o_done = sem("transposed"), sem("pv_done"), sem("o_done")
        probT_ready = [sem("probT_ready0"), sem("probT_ready1")]
        rawmax_ready, sum_ready, rinv_ready, sink_ready = sem("rawmax_ready"), sem("sum_ready"), sem("rinv_ready"), sem("sink_ready")
        oscale_ready = sem("oscale_ready")
        cat_rounded = sem("cat_rounded")
        cmp_built, gelu_done = sem("cmp_built"), sem("gelu_done")
        g_absed, g_logged, g_cummed, g_exped, g_ended, g_gated = (sem("g_absed"), sem("g_logged"), sem("g_cummed"),
                                                                  sem("g_exped"), sem("g_ended"), sem("g_gated"))
        g_diffed = sem("g_diffed")
        go_made, go_rounded, go_split = sem("go_made"), sem("go_rounded"), sem("go_split")
        std_ready = sem("std_ready")
        dve_step, act_step = sem("dve_step"), sem("act_step")
        relu_done, stored = sem("relu_done"), sem("stored")

        def col(name, k=0):
            n = GAINS.index(name) * KT + k if name in GAINS else len(GAINS) * KT + EXTRA.index(name)
            return cols[:, n:n + 1]

        def wait_evacuated(eng, name, later=0):
            n = JOB[name]
            eng.wait_ge(evacuated[n % 2], n // 2 + 1 + later)

        def wait_product(eng, name, later=0):
            chunks = dict(JOBS)[name]
            if chunks:
                eng.wait_ge(chunks_used, CHUNK[name] + chunks + later)
            else:
                eng.wait_ge(small_done, SMALL[name] + 1)

        def of(name):
            return bank[JOB[name] % 2]

        ROPES = ["kidx"] + [f"qidx{j}" for j in range(4)] + ["dsa_k"] + [f"q0.{j}" for j in range(6)] + \
                [f"{s}{g}" for s in ("ks", "kw") for g in range(2)] + [f"q1.{j}" for j in range(6)]

        def rope_tile(name):
            if name == "kidx":
                return kidx[:, :], kidx[:, :], rope_t0
            if name.startswith("qidx"):
                t = qidx[:, int(name[4]), :]
                return t, t, rope_t0
            if name == "dsa_k":
                return dsa_k[:, :], dsa_k[:, :], rope_t0
            if name.startswith("q0."):
                t = q0[:, int(name[3]), :]
                return t, t, rope_t0
            if name.startswith("q1."):
                return q1[:, int(name[3]), :], q1r[:, int(name[3]), :], rope_t1
            t = (ks if name[1] == "s" else kw)[:, int(name[2]), :]
            return t, t, rope_t1

        def attention(kind):
            if kind in ("dsa", "mem0"):
                return qs0, prob0, probT0, o_tok0
            if kind in ("nsa0", "nsa1", "mem1"):
                return qs1, prob1, probT1, o_tok1
            return qs2, prob2, probT2, o_tok2

        block = ctx.enter_context(nc.Block())

        @block.sync
        def _(sp):
            def load(t, per=0, i=0):
                if per or t >= RAW:
                    sp.wait_ge(lo_ready, t - RAW + 1 + per * i)
                src = A["weights"][t] if not per else \
                    A["weights"][bass.ds(i * per + t, 1)].rearrange("a p n -> p (a n)")
                sp.dma_start(w_raw[:, t % RAW, :], src).then_inc(raw_loaded[t % RAW], 16)

            for t in range(RAW):
                load(t)
            loops = (N_CHUNKS - RAW) // RAW
            with sp.Fori(0, loops) as i:
                for u in range(RAW):
                    load(RAW + u, RAW, i)
            for t in range(RAW + loops * RAW, N_CHUNKS):
                load(t)

        @block.gpsimd
        def _(pool):
            def rest(t, per=0, i=0):
                pool.wait_ge(hi_ready, t + 1 + per * i)
                nc.gpsimd.tensor_tensor(w_lo[:, t % RING, :], w_raw[:, t % RAW, :],
                                        w_hi[:, t % RING, :].bitcast(F32), ALU.subtract).then_inc(lo_ready, 1)

            loops = N_CHUNKS // RING
            with pool.Fori(0, loops) as i:
                for u in range(RING):
                    rest(u, RING, i)
            for t in range(loops * RING, N_CHUNKS):
                rest(t)

        @block.tensor
        def _(pe):
            def bank_free(n, per=0, i=0):
                if per or n >= 2:
                    pe.wait_ge(evacuated[n % 2], n // 2 + per // 2 * i)

            def chunk_ready(t, per=0, i=0):
                pe.wait_ge(lo_ready, t + 1 + per * i)

            def three(out, w, xs, first, last, swap=False):
                (wh, wl), (xh, xl) = w, xs
                for n, (a, b) in enumerate(((wh, xh), (wh, xl), (wl, xh))):
                    if swap:
                        a, b = b, a
                    r = nc.tensor.matmul(out, a, b, start=first and n == 0, stop=last and n == 2)
                return r

            def slot(t, k, width=P):
                return (w_hi[:, t % RING, k * P:k * P + width], w_lo[:, t % RING, k * P:k * P + width])

            def column_tile(name, hs=(h_hi, h_lo), n=SEQ, last=True):
                t = CHUNK[name]
                bank_free(JOB[name])
                chunk_ready(t)
                for k in range(KT):
                    r = three(of(name)[:, 0:n], slot(t, k), (hs[0][:, k, :], hs[1][:, k, :]), k == 0, last and k == KT - 1)
                if last:
                    r.then_inc(chunks_used, 1)

            def token_tile(name, hs=(h_hi, h_lo), tiles=TT, width=P, bias=None):
                t = CHUNK[name]
                bank_free(JOB[name])
                chunk_ready(t)
                for a in range(tiles):
                    out = of(name)[:, a * width:(a + 1) * width]
                    for k in range(KT):
                        xs = (hs[0][:, k, a * P:(a + 1) * P], hs[1][:, k, a * P:(a + 1) * P])
                        r = three(out, slot(t, k, width), xs, k == 0, bias is None and k == KT - 1, swap=True)
                    if bias is not None:
                        r = nc.tensor.matmul(out, one_row[0:1, :], bias, start=False, stop=True)
                r.then_inc(chunks_used, 1)

            def normed(name):
                pe.wait_ge(h_ready, KT * (NORMS.index(name) + 1))

            def sum_squares(name, n=SEQ):
                job = "memsum" if name == "mem" else f"sum.{name}"
                bank_free(JOB[job])
                pe.wait_ge(sq_added, 9 * (SUMS.index(name) + 1))
                nc.tensor.matmul(of(job)[:, 0:n], ones[:, :], sqacc[:, 0:n], start=True, stop=True).then_inc(small_done, 1)

            def rope(name):
                job = f"rope.{name}"
                bank_free(JOB[job])
                wait_evacuated(pe, name)
                nc.tensor.matmul(of(job)[:, :], perm[:, :], rope_tile(name)[0], start=True, stop=True).then_inc(small_done, 1)

            def index_scores(qt):
                for h in range(IDX_HEADS):
                    n = (qt - 1) * IDX_HEADS + h
                    if n >= 2:
                        pe.wait_ge(idx_relu, n - 1)
                    o = HD * (h % 2)
                    nc.tensor.matmul(score_bank[n % 2][:, 0:(qt + 1) * P], qidx[o:o + HD, h // 2, qt * P:(qt + 1) * P],
                                     kidx[o:o + HD, 0:(qt + 1) * P], start=True, stop=True).then_inc(idx_ready, 1)

            def attend(kind, units, i, pair=0):
                per = units
                g0 = UNIT0[kind] + pair * units
                qs, prob, probT, _ = attention(kind)
                l = int(kind[3]) if kind[3:].isdigit() else 0

                def keys(u):
                    hh, qt, br = attention_unit(kind, u)
                    o = HD * hh
                    kts = key_tiles(kind, qt, br)
                    if kind == "dsa":
                        return dsa_k[o:o + HD, 0:len(kts) * P], len(kts) * P
                    if kind.startswith("mem"):
                        return k_mem[o:o + HD, l, pair, :], N_MEM
                    if kind.startswith("swa"):
                        return sk[o:o + HD, l, kts[0] * P:(qt + 1) * P], len(kts) * P
                    if br == 0:
                        return k_cmp[o:o + HD, l * N_CMP:(l + 1) * N_CMP], N_CMP
                    return (ks if br == 1 else kw)[o:o + HD, l, 0:len(kts) * P], len(kts) * P

                def scores(u):
                    hh, qt, br = attention_unit(kind, u)
                    g = g0 + u
                    o = HD * hh
                    k, n = keys(u)
                    out = score_bank[g % 2]
                    pe.wait_ge(probs_ready, g + 1 + per * i)
                    q = (qr1 if br == 0 else qs)[o:o + HD, qt * P:(qt + 1) * P]
                    mem = kind.startswith("mem")
                    r = nc.tensor.matmul(out[:, 0:n], q, k, start=True, stop=mem)
                    if kind == "dsa":
                        r = nc.tensor.matmul(out[:, 0:n], ident_b[:, :], dsa_mask[:, qt, 0:n], start=False, stop=True)
                    elif kind.startswith("swa"):
                        r = nc.tensor.matmul(out[:, 0:n], ident_b[:, :], masks_b[:, 2 * P - n:2 * P], start=False, stop=True)
                    elif not mem and br == 0:
                        r = nc.tensor.matmul(out[:, 0:n], ident_b[:, :], masks_b[:, 2 * P + qt * 32:2 * P + qt * 32 + n],
                                             start=False, stop=True)
                    elif not mem:
                        r = nc.tensor.matmul(out[:, n - P:n], ident_b[:, :], masks_b[:, P:2 * P], start=False, stop=True)
                    r.then_inc(scores_ready, 1)

                def transposes(u):
                    hh, qt, br = attention_unit(kind, u)
                    g = g0 + u
                    pe.wait_ge(probs_ready, g + 3 + per * i)
                    pe.wait_ge(probT_ready[g % 2], g // 2 + 1 + per // 2 * i)
                    if kind.startswith("nsa") and br == 0:
                        r = nc.tensor.matmul(probT_bank[g % 2][0:N_CMP, 0:P], prob[:, g % 2, 0:N_CMP], ident[:, :],
                                             start=True, stop=True)
                    else:
                        for n in range(len(key_tiles(kind, qt, br))):
                            r = nc.tensor.transpose(probT_bank[g % 2][:, n * P:(n + 1) * P],
                                                    prob[:, g % 2, n * P:(n + 1) * P], ident[:, :])
                    r.then_inc(transposed, 1)

                def values(u):
                    hh, qt, br = attention_unit(kind, u)
                    g = g0 + u
                    out = o_bank[g % 2][:, 0:HD]
                    pe.wait_ge(probT_ready[g % 2], g // 2 + 2 + per // 2 * i)
                    pe.wait_ge(o_done, g + 1 + per * i)
                    if kind.startswith("nsa") and br == 0:
                        r = nc.tensor.matmul(out, probT[0:N_CMP, g % 2, 0:P], v_cmp[:, l, :], start=True, stop=True)
                    else:
                        kts = key_tiles(kind, qt, br)
                        for n, kt in enumerate(kts):
                            if kind == "dsa":
                                v = dsa_v[:, kt, :]
                            elif kind.startswith("mem"):
                                v = v_mem[:, l, kt, (2 * pair + hh) * HD:(2 * pair + hh + 1) * HD]
                            elif kind.startswith("swa"):
                                v = sv[:, kt, l * HD:(l + 1) * HD]
                            else:
                                v = (vs if br == 1 else vw)[:, kt, l * HD:(l + 1) * HD]
                            r = nc.tensor.matmul(out, probT[:, g % 2, n * P:(n + 1) * P], v, start=n == 0, stop=n == len(kts) - 1)
                    r.then_inc(pv_done, 1)

                pe.wait_ge(q_staged, PAIR0[kind] + pair + 1 + i)
                scores(0)
                scores(1)
                transposes(0)
                for u in range(units):
                    if u + 2 < units:
                        scores(u + 2)
                    if u + 1 < units:
                        transposes(u + 1)
                    values(u)

            def concat(prefix, kind, units):
                _, _, _, o_tok = attention(kind)
                pe.wait_ge(o_done, 2 + units)
                for j in range(KT):
                    name = f"{prefix}.{j}"
                    bank_free(JOB[name])
                    for a in range(TT):
                        r = nc.tensor.transpose(of(name)[:, a * P:(a + 1) * P], o_tok[:, a, j * P:(j + 1) * P], ident[:, :])
                    r.then_inc(small_done, 1)

            def up(prefix, tiles):
                n0, t0 = JOB[f"{prefix}.0"], CHUNK[f"{prefix}.0"]
                with pe.Fori(0, tiles // 4) as i:
                    for u in range(4):
                        bank_free(n0 + u, 4, i)
                        chunk_ready(t0 + u, 4, i)
                        for k in range(KT):
                            r = three(bank[(n0 + u) % 2][:, :], slot(t0 + u, k), (h_hi[:, k, :], h_lo[:, k, :]), k == 0, k == KT - 1)
                        r.then_inc(chunks_used, 1)

            def down(prefix, hi, lo, tiles, per_tile, step):
                n0, t0 = JOB[f"{prefix}.0"], CHUNK[f"{prefix}.0"]
                with pe.Fori(0, KT // step) as i:
                    for j in range(step):
                        bank_free(n0 + j, step, i)
                        for c in range(per_tile):
                            t = t0 + j * per_tile + c
                            chunk_ready(t, step * per_tile, i)
                            ks_ = min(KT, tiles - c * KT)
                            for k in range(ks_):
                                f = c * KT + k
                                r = three(bank[(n0 + j) % 2][:, :], slot(t, k), (hi[:, f, :], lo[:, f, :]), f == 0, f == tiles - 1)
                            r.then_inc(chunks_used, 1)

            pe.sem_inc(transposed, 2)
            pe.sem_inc(pv_done, 2)
            pe.wait_ge(consts_made, 1)
            sum_squares("mem", N_MEM)
            for l in range(DEPTH):
                normed(f"mem{l}")
                for j in range(2):
                    column_tile(f"mk{l}.{j}", (mem_hi[l], mem_lo[l]), N_MEM)
                for j in range(2):
                    token_tile(f"mv{l}.{j}", (mem_hi[l], mem_lo[l]), 2)
            sum_squares("attn0")
            normed("attn0")
            column_tile("ckv")
            bank_free(JOB["ckvsum"])
            wait_evacuated(pe, "ckv")
            nc.tensor.matmul(of("ckvsum")[:, :], ones[:, :], sq[:, 0, :], start=True, stop=True).then_inc(small_done, 1)
            column_tile("kidx")
            for j in range(4):
                column_tile(f"qidx{j}")
            rope("kidx")
            for j in range(4):
                rope(f"qidx{j}")
            token_tile("widx", width=IDX_HEADS)
            column_tile("dsa_k", last=False)
            pe.wait_ge(ckv_normed, 1)
            nc.tensor.matmul(of("dsa_k")[:, :], w_uk[:, :], ckv_n[:, :], start=False, stop=True).then_inc(chunks_used, 1)
            bank_free(JOB["dsa_v"])
            for a in range(TT):
                r = nc.tensor.matmul(of("dsa_v")[:, a * HD:(a + 1) * HD], ckv_n[:, a * P:(a + 1) * P], w_uv[:, :], start=True, stop=True)
            r.then_inc(small_done, 1)
            rope("dsa_k")
            pe.wait_ge(roped, 5)
            index_scores(1)
            for j in range(3):
                column_tile(f"q0.{j}")
            index_scores(2)
            for j in range(3, 6):
                column_tile(f"q0.{j}")
            index_scores(3)
            for j in range(6):
                rope(f"q0.{j}")
            for j in range(2):
                column_tile(f"qmem0.{j}")
            pe.wait_ge(roped, 12)
            pe.wait_ge(dsa_masked, TT)
            wait_evacuated(pe, "dsa_v")
            with pe.Fori(0, 6) as i:
                attend("dsa", 8, i)
            for pair in range(2):
                attend("mem0", 8, 0, pair)
            for l in range(DEPTH):
                if l == 1:
                    normed("attn1")
                    for s_ in ("kc", "vc", "ks", "kw"):
                        for g in range(2):
                            column_tile(f"{s_}{g}")
                    for c, name in enumerate(("cmp_hk", "cmp_hv")):
                        bank_free(JOB[name])
                        pe.wait_ge(cmp_built, 4 * (c + 1))
                        for p_ in range(CMP_PAIRS):
                            r = nc.tensor.matmul(of(name)[:, 0:2 * N_CMP], cmp_w1[c][:, p_, :],
                                                 cmp_x[c][:, p_, :, :].rearrange("p g c -> p (g c)"),
                                                 start=p_ == 0, stop=p_ == CMP_PAIRS - 1)
                        r.then_inc(small_done, 1)
                    for s_ in ("ks", "kw"):
                        for g in range(2):
                            rope(f"{s_}{g}")
                    bank_free(JOB["cmp_k"])
                    wait_evacuated(pe, "cmp_hk")
                    nc.tensor.matmul(of("cmp_k")[:, 0:2 * N_CMP], cmp_w2k[:, :], cmp_h[0][:, :], start=True, stop=True).then_inc(small_done, 1)
                    bank_free(JOB["cmp_v"])
                    wait_evacuated(pe, "cmp_hv")
                    for g in range(2):
                        r = nc.tensor.matmul(of("cmp_v")[0:N_CMP, g * HD:(g + 1) * HD], cmp_h[1][:, g * N_CMP:(g + 1) * N_CMP],
                                             cmp_w2v[:, :], start=True, stop=True)
                    r.then_inc(small_done, 1)
                    for j in range(6):
                        column_tile(f"q1.{j}")
                    token_tile("vs")
                    token_tile("vw")
                    token_tile("gates", width=3 * TOK_HEADS)
                    for j in range(6):
                        rope(f"q1.{j}")
                    for j in range(2):
                        column_tile(f"qmem1.{j}")
                    pe.wait_ge(roped, len(ROPES))
                    for name in ("cmp_k", "cmp_v", "vs", "vw"):
                        wait_evacuated(pe, name)
                    for g in range(2):
                        with pe.Fori(0, 3) as i:
                            attend(f"nsa{g}", 24, i)
                    for pair in range(2):
                        attend("mem1", 8, 0, pair)
                concat(f"cat{l}", f"mem{l}", UNIT0[f"mem{l}"] + 16)
                wait_evacuated(pe, f"cat{l}.{KT - 2}")
                wait_evacuated(pe, f"cat{l}.{KT - 1}")
                for j in range(KT):
                    column_tile(f"wo{l}.{j}")
                sum_squares(f"ffn{l}")
                normed(f"ffn{l}")
                up(f"up{l}", 2 * FT)
                pe.wait_ge(act_ready, FT * (l + 1))
                down(f"down{l}", act_hi, act_lo, FT, 3, 4)
                sum_squares("attn1" if l == 0 else "final")
            sum_squares("mixpre0")
            normed("mixpre0")
            column_tile("glr")
            for h in range(4):
                column_tile(f"gk{h}")
            for h in range(4):
                column_tile(f"gq{h}")
            pe.wait_ge(gla_in, 32)
            for h in range(4):
                bank_free(JOB[f"gz{h}"])
                wait_evacuated(pe, "glr")
                nc.tensor.matmul(of(f"gz{h}")[:, :], w_gate[:, h * P:(h + 1) * P], glr[0:16, :], start=True, stop=True).then_inc(small_done, 1)
                token_tile(f"gv{2 * h}")
                token_tile(f"gv{2 * h + 1}")
            for j in range(KT):
                column_tile(f"gg{j}")
            for h in range(4):
                name = f"gket{h}"
                bank_free(JOB[name])
                pe.wait_ge(g_gated, 3 * (h + 1))
                for a in range(TT):
                    r = nc.tensor.transpose(of(name)[:, a * P:(a + 1) * P], gk[:, h, a * P:(a + 1) * P], ident[:, :])
                r.then_inc(small_done, 1)
                name = f"gatt{h}"
                bank_free(JOB[name])
                for a in range(TT):
                    r = nc.tensor.matmul(of(name)[:, a * P:(a + 1) * P], k_inv[:, h, a * P:(a + 1) * P], gq[:, h, a * P:(a + 1) * P],
                                         start=True, stop=True)
                r.then_inc(small_done, 1)
                wait_evacuated(pe, f"gket{h}")
                for n in range(N_CHUNK - 1):
                    name = f"gds{h}.{n}"
                    bank_free(JOB[name])
                    o = GLA_CHUNK * (n % 2)
                    nc.tensor.matmul(of(name)[:, 0:2 * P], k_endT[o:o + GLA_CHUNK, n // 2, :],
                                     gv[o:o + GLA_CHUNK, n // 2, h * 2 * P:(h + 1) * 2 * P], start=True, stop=True).then_inc(small_done, 1)
                wait_evacuated(pe, f"gatt{h}")
                wait_evacuated(pe, f"gds{h}.{N_CHUNK - 2}")
                for j in range(2):
                    name = f"go{h}.{j}"
                    bank_free(JOB[name])
                    for a in range(TT):
                        c0 = h * 2 * P + j * P
                        r = nc.tensor.matmul(of(name)[:, a * P:(a + 1) * P], gv[:, a, c0:c0 + P], attT[:, a, :], start=True, stop=False)
                        for n in (2 * a, 2 * a + 1):
                            if n:
                                r = nc.tensor.matmul(of(name)[:, n * GLA_CHUNK:(n + 1) * GLA_CHUNK], state[:, n, j * P:(j + 1) * P],
                                                     gq[:, h, n * GLA_CHUNK:(n + 1) * GLA_CHUNK], start=False, stop=n % 2 == 1)
                    r.then_inc(small_done, 1)
                name = f"gosum{h}"
                bank_free(JOB[name])
                for j in range(2):
                    wait_evacuated(pe, f"go{h}.{j}")
                    r = nc.tensor.matmul(of(name)[:, :], ones[:, :], sq[:, j, :], start=j == 0, stop=j == 1)
                r.then_inc(small_done, 1)
            pe.wait_ge(go_split, KT)
            for l in range(DEPTH):
                if l == 1:
                    sum_squares("mixpre1")
                    normed("mixpre1")
                    for g in range(2):
                        column_tile(f"sk{g}")
                    pe.wait_ge(swa_in, 16)
                    token_tile("sv", bias=sv_b[0:1, :])
                    for j in range(KT):
                        column_tile(f"sq{j}")
                    for name in ("sk0", "sk1", "sv"):
                        wait_evacuated(pe, name)
                    for g in range(2):
                        with pe.Fori(0, 4) as i:
                            attend(f"swa{g}", 8, i)
                    concat("scat", "swa1", UNIT0["swa1"] + 32)
                    wait_evacuated(pe, f"scat.{KT - 2}")
                    wait_evacuated(pe, f"scat.{KT - 1}")
                for j in range(KT):
                    column_tile(f"mix{l}.{j}")
                sum_squares(f"mixpost{l}")
                sum_squares(f"mlppre{l}")
                normed(f"mlppre{l}")
                for half in range(2):
                    up(f"mup{l}{half}", HALF_FT)
                    pe.wait_ge(act_ready, 2 * FT + HALF_FT * (2 * l + half + 1))
                    down(f"mdown{l}{half}", mact_hi, mact_lo, HALF_FT, 2, 2)
                sum_squares(f"mlppost{l}")

        @block.scalar
        def _(act):
            following = [0]

            def split(t, per=0, i=0):
                act.wait_ge(raw_loaded[t % RAW], 16 * (t // RAW + 1) + 16 * per // RAW * i)
                if per or t >= RING:
                    act.wait_ge(chunks_used, t - RING + 1 + per * i)
                nc.scalar.activation(w_hi[:, t % RING, :], w_raw[:, t % RAW, :], ACT.Copy).then_inc(hi_ready, 1)

            def split_ahead(t):
                while following[0] <= min(t + AHEAD, N_CHUNKS - 1):
                    split(following[0])
                    following[0] += 1

            def product(name, c=None):
                n = dict(JOBS)[name]
                if n:
                    split_ahead(CHUNK[name] + n - 1)
                wait_product(act, name)

            def move(name, out, src=None, func=ACT.Copy, **how):
                product(name)
                nc.scalar.activation(out, of(name)[:, 0:SEQ] if src is None else src, func, **how).then_inc(evacuated[JOB[name] % 2], 1)

            def square(k, name, src, n=SEQ, ready=None, later=0):
                b = 9 * SUMS.index(name)
                if b or k >= 2:
                    act.wait_ge(sq_added, b + k if k >= 2 else b)
                nc.scalar.activation(sq[:, k % 2, 0:n], src, ACT.Square).then_inc(sq_done, 1)

            def deviation(job, n=SEQ):
                product(job)
                nc.scalar.activation(std[:, 0:n], of(job)[:, 0:n], ACT.Sqrt, bias=eps[:, 0:1]).then_inc(evacuated[JOB[job] % 2], 1)

            def round_norm(name, hi, n=SEQ):
                for k in range(KT):
                    act.wait_ge(h_made, KT * NORMS.index(name) + k + 1)
                    nc.scalar.activation(hi[:, k, :], tmp[:, k % 2, 0:n], ACT.Copy).then_inc(h_rounded, 1)

            def index_relu(qt):
                n_ = (qt + 1) * P
                for h in range(IDX_HEADS):
                    n = (qt - 1) * IDX_HEADS + h
                    act.wait_ge(idx_ready, n + 1)
                    if n >= 2:
                        act.wait_ge(idx_added, n - 1)
                    nc.scalar.activation(relu_l[:, n % 2, 0:n_], score_bank[n % 2][:, 0:n_], ACT.Relu).then_inc(idx_relu, 1)

            def attend(kind, units, i, pair=0):
                per = units
                g0 = UNIT0[kind] + pair * units
                _, prob, probT, _ = attention(kind)

                def width(u):
                    _, qt, br = attention_unit(kind, u)
                    return N_CMP if kind.startswith("nsa") and br == 0 else P * len(key_tiles(kind, qt, br))

                def exponentials(u):
                    g, n = g0 + u, width(u)
                    act.wait_ge(max_ready, g + 1 + per * i)
                    act.wait_ge(transposed, g + 1 + per * i)
                    nc.scalar.activation(prob[:, g % 2, 0:n], score_bank[g % 2][:, 0:n], ACT.Exp, bias=nmax[:, g % 4:g % 4 + 1],
                                         accum_out=psum_p[:, g % 4:g % 4 + 1]).then_inc(probs_ready, 1)
                    if kind.startswith("swa"):
                        head = (8 * int(kind[3]) + u // 4) + 2 * i
                        nc.scalar.activation(sinkexp[:, g % 4:g % 4 + 1], sinks[:, bass.ds(head, 1)], ACT.Exp,
                                             bias=nmax[:, g % 4:g % 4 + 1]).then_inc(sink_ready, 1)

                def move_transposed(u):
                    g, n = g0 + u, width(u)
                    rows, n = (N_CMP, P) if n == N_CMP else (P, n)
                    act.wait_ge(transposed, g + 3 + per * i)
                    act.wait_ge(pv_done, g + 1 + per * i)
                    nc.scalar.activation(probT[0:rows, g % 2, 0:n], probT_bank[g % 2][0:rows, 0:n], ACT.Copy).then_inc(probT_ready[g % 2], 1)

                exponentials(0)
                for u in range(units):
                    if u + 1 < units:
                        exponentials(u + 1)
                    if u % 2 == 0:
                        move_transposed(u)

            def concat(prefix, n):
                for j in range(KT):
                    name = f"{prefix}.{j}"
                    product(name)
                    nc.scalar.activation(h_hi[:, j, :], of(name)[:, :], ACT.Copy).then_inc(cat_rounded, 1)

            def loop(t0, steps, per, body):
                split_ahead(t0 - 1)
                over = t0 + per * steps + AHEAD > N_CHUNKS
                with act.Fori(0, steps - over) as i:
                    body(i, lambda u: split(t0 + u + AHEAD, per, i))
                following[0] = t0 + per * (steps - over) + AHEAD
                if over:
                    last = steps - 1
                    body(last, lambda u: split_ahead(t0 + per * last + u))

            def up_gated(l):
                n0, t0 = JOB[f"up{l}.0"], CHUNK[f"up{l}.0"]

                def body(i, ahead):
                    for f in range(2):
                        b = n0 + 2 * f
                        ahead(2 * f)
                        act.wait_ge(chunks_used, t0 + 2 * f + 1 + 4 * i)
                        if FT * l or f == 0:
                            pass
                        act.wait_ge(act_made, FT * l + f + 2 * i)
                        nc.scalar.activation(sq[:, f, :], bank[b % 2][:, :], ACT.Silu).then_inc(evacuated[b % 2], 1)
                        ahead(2 * f + 1)
                        act.wait_ge(act_made, FT * l + f + 1 + 2 * i)
                        nc.scalar.activation(act_hi[:, bass.ds(2 * i + f, 1), :].rearrange("p a n -> p (a n)"), tmp[:, f, :], ACT.Copy).then_inc(act_rounded, 1)

                loop(t0, FT // 2, 4, body)

            def up_relu(l, half):
                t0, n0 = CHUNK[f"mup{l}{half}.0"], JOB[f"mup{l}{half}.0"]
                c0 = 2 * FT + HALF_FT * (2 * l + half)

                def body(i, ahead):
                    for f in range(4):
                        ahead(f)
                        act.wait_ge(chunks_used, t0 + f + 1 + 4 * i)
                        act.wait_ge(act_made, c0 + f - 1 + 4 * i)
                        nc.scalar.activation(sq[:, f % 2, :], bank[(n0 + f) % 2][:, :], ACT.Relu).then_inc(relu_done, 1)
                        act.wait_ge(act_made, c0 + f + 1 + 4 * i)
                        nc.scalar.activation(mact_hi[:, bass.ds(4 * i + f, 1), :].rearrange("p a n -> p (a n)"), tmp[:, f % 2, :], ACT.Copy).then_inc(act_rounded, 1)

                loop(t0, HALF_FT // 4, 4, body)

            def down(prefix, per_tile, step, name, dst):
                t0, n0 = CHUNK[f"{prefix}.0"], JOB[f"{prefix}.0"]

                def body(i, ahead):
                    for j in range(step):
                        for c in range(per_tile):
                            ahead(j * per_tile + c)
                        if name:
                            act.wait_ge(evacuated[(n0 + j) % 2], (n0 + j) // 2 + 1 + step // 2 * i)
                            act.wait_ge(sq_added, 9 * SUMS.index(name) + j + step * i)
                            nc.scalar.activation(sq[:, j % 2, :], dst[:, bass.ds(step * i + j, 1), :].rearrange("p a n -> p (a n)"),
                                                 ACT.Square).then_inc(sq_done, 1)

                loop(t0, KT // step, step * per_tile, body)

            act.sem_inc(probs_ready, 2)
            act.sem_inc(probT_ready[0], 1)
            act.dma_start(memx[:, :, :], A["memT"]).then_inc(mem_in, 16)
            for dst, src in ((cols[:, :], A["cols"]), (ident[:, :], A["ident"]), (perm[:, :], A["perm"]), (rope_c[:, :], A["rope_c"]),
                             (rope_s[:, :], A["rope_s"]), (masks[:, :], A["masks"]),
                             (w_uk[:, :], A["w_uk"]), (w_uv[:, :], A["w_uv"]), (sinks[:, :], A["sinks"])):
                act.dma_start(dst, src).then_inc(consts_in, 16)
            act.dma_start(x[:, :, :], A["xT"]).then_inc(x_in, 16)
            act.wait_ge(consts_made, 1)
            act.wait_ge(mem_in, 16)
            for k in range(KT):
                square(k, "mem", memx[:, k, :], N_MEM)
            deviation("memsum", N_MEM)
            split_ahead(-1)
            round_norm("mem0", mem_hi[0], N_MEM)
            round_norm("mem1", mem_hi[1], N_MEM)
            act.wait_ge(x_in, 16)
            for k in range(KT):
                square(k, "attn0", x[:, k, :])
            for l in range(DEPTH):
                for j in range(2):
                    move(f"mk{l}.{j}", k_mem[:, l, j, :], of(f"mk{l}.{j}")[:, 0:N_MEM])
                for j in range(2):
                    move(f"mv{l}.{j}", v_mem[:, l, :, j * P:(j + 1) * P], of(f"mv{l}.{j}")[:, 0:2 * P].rearrange("p (a n) -> p a n", a=2))
            deviation("sum.attn0")
            round_norm("attn0", h_hi)
            product("ckv")
            nc.scalar.activation(ckv[:, :], of("ckv")[:, :], ACT.Copy).then_inc(act_step, 1)
            act.wait_ge(sq_added, 9 * (SUMS.index("attn0") + 1))
            nc.scalar.activation(sq[:, 0, :], of("ckv")[:, :], ACT.Square, scale=math.sqrt(D // RANK) if math.sqrt(D // RANK).is_integer() else 1.0).then_inc(evacuated[JOB["ckv"] % 2], 1)
            product("ckvsum")
            nc.scalar.activation(std[:, :], of("ckvsum")[:, :], ACT.Sqrt, scale=float(D // RANK), bias=eps[:, 0:1]).then_inc(evacuated[JOB["ckvsum"] % 2], 1)
            move("kidx", kidx[:, :])
            for j in range(4):
                move(f"qidx{j}", qidx[:, j, :])
            move("widx", widx[:, :, :], of("widx")[:, 0:TT * IDX_HEADS].rearrange("p (a n) -> p a n", a=TT),
                 scale=IDX_HEADS ** -0.5 * IDX_DIM ** -0.5)
            move("dsa_k", dsa_k[:, :])
            move("dsa_v", dsa_v[:, :, :], of("dsa_v")[:, 0:TT * HD].rearrange("p (a n) -> p a n", a=TT))
            index_relu(1)
            for j in range(3):
                move(f"q0.{j}", q0[:, j, :], scale=SCALE)
            index_relu(2)
            for j in range(3, 6):
                move(f"q0.{j}", q0[:, j, :], scale=SCALE)
            index_relu(3)
            for j in range(2):
                move(f"qmem0.{j}", qmem0[:, j, :], scale=SCALE)
            with act.Fori(0, 6) as i:
                attend("dsa", 8, i)
            for pair in range(2):
                attend("mem0", 8, 0, pair)
            for l in range(DEPTH):
                if l == 1:
                    wait_product(act, f"down0.{KT - 1}")
                    for c in range(2):
                        act.dma_start(cmp_w1[c][:, :, :], A["cmp_w1"][c]).then_inc(cmp_in, 16)
                        act.dma_start(cmp_pos[c][:, :], A["cmp_pos"][c]).then_inc(cmp_in, 16)
                    act.dma_start(cmp_w2k[:, :], A["cmp_w2k"]).then_inc(cmp_in, 16)
                    act.dma_start(cmp_w2v[:, :], A["cmp_w2v"]).then_inc(cmp_in, 16)
                    deviation("sum.attn1")
                    round_norm("attn1", h_hi)
                    for name in ("kc0", "kc1", "vc0", "vc1"):
                        split_ahead(CHUNK[name])
                    for g in range(2):
                        move(f"ks{g}", ks[:, g, :])
                    for g in range(2):
                        move(f"kw{g}", kw[:, g, :])
                    for c, name in enumerate(("cmp_hk", "cmp_hv")):
                        move(name, cmp_h[c][:, :], of(name)[:, 0:2 * N_CMP], ACT.Gelu_apprx_tanh)
                    move("cmp_k", k_cmp[:, :], of("cmp_k")[:, 0:2 * N_CMP])
                    move("cmp_v", v_cmp[:, :, :], of("cmp_v")[0:N_CMP, 0:2 * HD].rearrange("p (a n) -> p a n", a=2))
                    for j in range(6):
                        move(f"q1.{j}", q1[:, j, :], scale=SCALE)
                    for name, dst in (("vs", vs), ("vw", vw)):
                        move(name, dst[:, :, :], of(name)[:, :].rearrange("p (a n) -> p a n", a=TT))
                    move("gates", gates[:, :, :], of("gates")[:, 0:TT * 3 * TOK_HEADS].rearrange("p (a n) -> p a n", a=TT), ACT.Sigmoid)
                    for j in range(2):
                        move(f"qmem1.{j}", qmem1[:, j, :], scale=SCALE)
                    for g in range(2):
                        with act.Fori(0, 3) as i:
                            attend(f"nsa{g}", 24, i)
                    for pair in range(2):
                        attend("mem1", 8, 0, pair)
                concat(f"cat{l}", l)
                for j in range(KT):
                    split_ahead(CHUNK[f"wo{l}.{j}"])
                    wait_evacuated(act, f"wo{l}.{j}")
                    square(j, f"ffn{l}", x[:, j, :])
                deviation(f"sum.ffn{l}")
                round_norm(f"ffn{l}", h_hi)
                up_gated(l)
                down(f"down{l}", 3, 4, "attn1" if l == 0 else "final", x)
            deviation("sum.final")
            for k in range(KT):
                act.wait_ge(x_normed, k + 1)
                square(k, "mixpre0", x[:, k, :])
            act.dma_start(w_gate[:, :], A["w_gate"]).then_inc(gla_in, 16)
            act.dma_start(gla_mask[:, :], A["gla_mask"]).then_inc(gla_in, 16)
            deviation("sum.mixpre0")
            round_norm("mixpre0", h_hi)
            move("glr", glr[:, :])
            for h in range(4):
                move(f"gk{h}", gk[:, h, :])
            for h in range(4):
                move(f"gq{h}", gq[:, h, :])
            for h in range(4):
                product(f"gz{h}")
                if h:
                    act.wait_ge(g_cummed, 2 * h)
                nc.scalar.activation(g_ab[:, :], of(f"gz{h}")[:, :], ACT.Abs, bias=col(f"gla_b{h}")).then_inc(g_absed, 1)
                act.wait_ge(g_absed, h + 1)
                nc.scalar.activation(g_ab[:, :], g_ab[:, :], ACT.Exp, scale=-1.0).then_inc(act_step, 1)
                act.wait_ge(act_step, 2 + h)
                nc.scalar.activation(g_ab[:, :], g_ab[:, :], ACT.Ln, bias=1.0).then_inc(g_logged, 1)
                name = f"gv{2 * h}"
                move(name, gv[:, :, 2 * h * P:(2 * h + 1) * P], of(name)[:, :].rearrange("p (a n) -> p a n", a=TT))
                act.wait_ge(g_cummed, 2 * h + 2)
                act.wait_ge(g_gated, 3 * h)
                nc.scalar.activation(g_exp[:, :], g_cum[:, :], ACT.Exp, scale=1.0 / GATE_NORM).then_inc(g_exped, 1)
                nc.scalar.activation(g_inv, g_cum[:, :], ACT.Exp, scale=-1.0 / GATE_NORM).then_inc(g_exped, 1)
                act.wait_ge(g_diffed, h + 1)
                nc.scalar.activation(g_end, g_end, ACT.Exp, scale=1.0 / GATE_NORM).then_inc(g_exped, 1)
                name = f"gv{2 * h + 1}"
                move(name, gv[:, :, (2 * h + 1) * P:(2 * h + 2) * P], of(name)[:, :].rearrange("p (a n) -> p a n", a=TT))
            for j in range(KT):
                move(f"gg{j}", gsilu[:, j, :], func=ACT.Silu)
            for h in range(4):
                name = f"gket{h}"
                move(name, k_endT[:, :, :], of(name)[:, :].rearrange("p (a n) -> p a n", a=TT))
                for j in range(2):
                    name = f"go{h}.{j}"
                    product(name)
                    if h:
                        act.wait_ge(go_made, 2 * (h - 1) + j + 1)
                        wait_product(act, f"gosum{h - 1}")
                    nc.scalar.activation(g_o[:, j, :], of(name)[:, :], ACT.Copy).then_inc(act_step, 1)
                    nc.scalar.activation(sq[:, j, :], of(name)[:, :], ACT.Square).then_inc(evacuated[JOB[name] % 2], 1)
                name = f"gosum{h}"
                product(name)
                nc.scalar.activation(std[:, :], of(name)[:, :], ACT.Sqrt, scale=float(KT // 2), bias=eps[:, 0:1]).then_inc(evacuated[JOB[name] % 2], 1)
                for j in range(2):
                    act.wait_ge(go_made, 2 * h + j + 1)
                    nc.scalar.activation(h_hi[:, 2 * h + j, :], tmp[:, j, :], ACT.Copy).then_inc(go_rounded, 1)
            for l in range(DEPTH):
                if l == 1:
                    act.dma_start(sv_b[0:1, :], A["sv_b"]).then_inc(swa_in, 16)
                    deviation("sum.mixpre1")
                    round_norm("mixpre1", h_hi)
                    for g in range(2):
                        move(f"sk{g}", sk[:, g, :], func=ACT.Identity, bias=col(f"swa_bk{g}"))
                    move("sv", sv[:, :, :], of("sv")[:, :].rearrange("p (a n) -> p a n", a=TT))
                    for j in range(KT):
                        split_ahead(CHUNK[f"sq{j}"])
                        wait_evacuated(act, f"sq{j}")
                    for g in range(2):
                        with act.Fori(0, 4) as i:
                            attend(f"swa{g}", 8, i)
                    concat("scat", 2)
                for j in range(KT):
                    split_ahead(CHUNK[f"mix{l}.{j}"])
                    wait_evacuated(act, f"mix{l}.{j}")
                    square(j, f"mixpost{l}", m[:, j, :])
                deviation(f"sum.mixpost{l}")
                for k in range(KT):
                    act.wait_ge(x_added, KT * 2 * l + k + 1)
                    square(k, f"mlppre{l}", x[:, k, :])
                deviation(f"sum.mlppre{l}")
                round_norm(f"mlppre{l}", h_hi)
                for half in range(2):
                    up_relu(l, half)
                    down(f"mdown{l}{half}", 2, 2, f"mlppost{l}" if half else None, m)
                deviation(f"sum.mlppost{l}")
                for k in range(KT):
                    act.wait_ge(x_added, KT * (2 * l + 1) + k + 1)
                    if l == 0:
                        square(k, "mixpre1", x[:, k, :])
                    else:
                        act.dma_start(A["out"][k], x[:, k, :]).then_inc(stored, 16)
            act.wait_ge(stored, 16 * KT)

        @block.vector
        def _(dve):
            steps = [0]

            def step(ins):
                steps[0] += 1
                ins.then_inc(dve_step, 1)
                dve.wait_ge(dve_step, steps[0])

            def zero_sum(name):
                nc.vector.memset(sqacc[:, :], 0.0).then_inc(sq_added, 1)

            def add_square(k, name, n=SEQ, per=0, i=0):
                b = SUMS.index(name)
                dve.wait_ge(sq_done, KT * b + k + 1 + per * i)
                dve.wait_ge(sq_added, 9 * b + k + 1 + per * i)
                nc.vector.tensor_tensor(sqacc[:, 0:n], sqacc[:, 0:n], sq[:, k % 2, 0:n], ALU.add).then_inc(sq_added, 1)

            def inverse(job, n=SEQ):
                wait_evacuated(dve, job)
                step(nc.vector.reciprocal(rstd[:, 0:n], std[:, 0:n]))

            def norm(name, src, hi, lo, n=SEQ):
                b = KT * NORMS.index(name)

                def whole(k):
                    nc.vector.scalar_tensor_tensor(tmp[:, k % 2, 0:n], src[:, k, :], col(name, k), rstd[:, 0:n],
                                                   ALU.mult, ALU.mult).then_inc(h_made, 1)

                if b:
                    dve.wait_ge(h_ready, b)
                whole(0)
                whole(1)
                for k in range(KT):
                    dve.wait_ge(h_rounded, b + k + 1)
                    nc.vector.tensor_tensor(lo[:, k, :], tmp[:, k % 2, 0:n], hi[:, k, :].bitcast(F32), ALU.subtract).then_inc(h_ready, 1)
                    if k + 2 < KT:
                        dve.wait_ge(h_ready, b + k + 1)
                        whole(k + 2)

            def rope(name):
                raw, out, t = rope_tile(name)
                wait_evacuated(dve, name)
                if ROPES.index(name):
                    dve.wait_ge(roped, ROPES.index(name))
                nc.vector.tensor_tensor(t[:, 0, :], raw, rope_c[:, :], ALU.mult).then_inc(dve_step, 1)
                steps[0] += 1
                job = f"rope.{name}"
                wait_product(dve, job)
                nc.vector.tensor_tensor(t[:, 1, :], of(job)[:, :], rope_s[:, :], ALU.mult).then_inc(evacuated[JOB[job] % 2], 1)
                dve.wait_ge(dve_step, steps[0])
                wait_evacuated(dve, job)
                nc.vector.tensor_tensor(out, t[:, 0, :], t[:, 1, :], ALU.add).then_inc(roped, 1)

            def index_mask(qt):
                n = (qt + 1) * P
                if qt:
                    dve.wait_ge(dsa_masked, qt)
                    step(nc.vector.memset(score[:, 0:qt * P], 0.0))
                    nc.vector.tensor_copy(score[:, qt * P:n], masks[:, P:2 * P]).then_inc(idx_chain, 1)
                    dve.wait_ge(idx_chain, qt)
                    for h in range(IDX_HEADS):
                        c = (qt - 1) * IDX_HEADS + h
                        dve.wait_ge(idx_relu, c + 1)
                        if h:
                            dve.wait_ge(idx_added, c)
                        nc.vector.scalar_tensor_tensor(score[:, 0:n], relu_l[:, c % 2, 0:n], widx[:, qt, h:h + 1], score[:, 0:n],
                                                       ALU.mult, ALU.add).then_inc(idx_added, 1)
                    dve.wait_ge(idx_added, qt * IDX_HEADS)

            def index_top(qt):
                n = (qt + 1) * P
                if qt:
                    for _ in range(TOPK // 8):
                        step(nc.vector.max(top8[:, :], score[:, 0:n]))
                        step(nc.vector.match_replace(score[:, 0:n], top8[:, :], score[:, 0:n], -3e38))
                    nc.vector.tensor_scalar(dsa_mask[:, qt, 0:n], score[:, 0:n], -2e38, NEG, ALU.is_gt, ALU.mult).then_inc(dsa_masked, 1)
                else:
                    nc.vector.tensor_copy(dsa_mask[:, 0, 0:P], masks[:, P:2 * P]).then_inc(dsa_masked, 1)

            def attend(kind, units, i, pair=0):
                per = units
                g0 = UNIT0[kind] + pair * units
                qs, prob, probT, o_tok = attention(kind)
                nsa, swa, mem = (kind.startswith(s_) for s_ in ("nsa", "swa", "mem"))
                group = int(kind[3]) if nsa or swa else 0

                def width(u):
                    _, qt, br = attention_unit(kind, u)
                    return N_CMP if nsa and br == 0 else P * len(key_tiles(kind, qt, br))

                def stage():
                    dve.wait_ge(scores_ready, g0 + per * i)
                    if mem:
                        nc.vector.tensor_copy(qs[:, :], (qmem0 if kind == "mem0" else qmem1)[:, pair, :]).then_inc(q_staged, 1)
                        return
                    src = {"dsa": q0, "nsa": q1r, "swa": sq_q}[kind[0:3]]
                    j = bass.ds(i + (3 if nsa else 4) * group, 1)
                    if nsa:
                        nc.vector.tensor_copy(qr1[:, :], q1[:, j, :].rearrange("p a n -> p (a n)"))
                    nc.vector.tensor_copy(qs[:, :], src[:, j, :].rearrange("p a n -> p (a n)")).then_inc(q_staged, 1)

                def maximum(u):
                    g, n, s4 = g0 + u, width(u), (g0 + u) % 4
                    _, qt, br = attention_unit(kind, u)
                    dve.wait_ge(scores_ready, g + 1 + per * i)
                    src = score_bank[g % 2][:, 0:n]
                    if swa:
                        r0 = g - UNIT0["swa0"] + 48
                        nc.vector.tensor_reduce(rawmax[:, s4:s4 + 1], src, AX.X, ALU.max, negate=True).then_inc(rawmax_ready, 1)
                        dve.wait_ge(rawmax_ready, r0 + 1 + per * i)
                        head = 8 * group + u // 4 + 2 * i
                        nc.vector.tensor_tensor(nmax[:, s4:s4 + 1], rawmax[:, s4:s4 + 1], nsinks[:, bass.ds(head, 1)], ALU.min).then_inc(max_ready, 1)
                    elif nsa and br == 0:
                        r0 = (g - UNIT0["nsa0"]) // 3
                        nc.vector.tensor_reduce(rawmax[:, s4:s4 + 1], src, AX.X, ALU.max, negate=True).then_inc(rawmax_ready, 1)
                        dve.wait_ge(rawmax_ready, r0 + 1 + per // 3 * i)
                        nc.vector.tensor_scalar(nmax[:, s4:s4 + 1], rawmax[:, s4:s4 + 1], -NEG / 10, None, ALU.min).then_inc(max_ready, 1)
                    else:
                        nc.vector.tensor_reduce(nmax[:, s4:s4 + 1], src, AX.X, ALU.max, negate=True).then_inc(max_ready, 1)

                def move_transposed(u):
                    g, n = g0 + u, width(u)
                    rows, n = (N_CMP, P) if n == N_CMP else (P, n)
                    dve.wait_ge(transposed, g + 3 + per * i)
                    dve.wait_ge(pv_done, g + 1 + per * i)
                    nc.vector.tensor_copy(probT[0:rows, g % 2, 0:n], probT_bank[g % 2][0:rows, 0:n]).then_inc(probT_ready[g % 2], 1)

                def output(u):
                    hh, qt, br = attention_unit(kind, u)
                    g, s4 = g0 + u, (g0 + u) % 4
                    den = psum_p[:, s4:s4 + 1]
                    dve.wait_ge(probs_ready, g + 3 + per * i)
                    if swa:
                        r0 = g - UNIT0["swa0"]
                        dve.wait_ge(sink_ready, r0 + 1 + per * i)
                        nc.vector.tensor_tensor(oscale[:, s4:s4 + 1], den, sinkexp[:, s4:s4 + 1], ALU.add).then_inc(sum_ready, 1)
                        den = oscale[:, s4:s4 + 1]
                        dve.wait_ge(sum_ready, 48 + r0 + 1 + per * i)
                    elif nsa and br == 0:
                        r0 = (g - UNIT0["nsa0"]) // 3
                        nc.vector.tensor_scalar(oscale[:, s4:s4 + 1], den, 1e-30, None, ALU.max).then_inc(sum_ready, 1)
                        den = oscale[:, s4:s4 + 1]
                        dve.wait_ge(sum_ready, r0 + 1 + per // 3 * i)
                    nc.vector.reciprocal(rinv[:, s4:s4 + 1], den).then_inc(rinv_ready, 1)
                    dve.wait_ge(rinv_ready, g + 1 + per * i)
                    factor = rinv[:, s4:s4 + 1]
                    if nsa:
                        c = (6 * group + hh) * 3 + br + 6 * i
                        nc.vector.tensor_tensor(oscale[:, s4:s4 + 1], factor, gates[:, qt, bass.ds(c, 1)], ALU.mult).then_inc(oscale_ready, 1)
                        dve.wait_ge(oscale_ready, g - UNIT0["nsa0"] + 1 + per * i)
                        factor = oscale[:, s4:s4 + 1]
                    dve.wait_ge(pv_done, g + 3 + per * i)
                    o = o_bank[g % 2][:, 0:HD]
                    if mem:
                        c = (TOK_HEADS + 2 * pair + hh) * HD
                        dst = o_tok[:, qt, c:c + HD]
                    else:
                        dst = o_tok[:, qt, bass.ds(((6 if nsa else 8) * group + hh) * HD + P * i, HD)]
                    if nsa and br:
                        dve.wait_ge(o_done, g + 2 + per * i)
                        nc.vector.scalar_tensor_tensor(dst, o, factor, dst, ALU.mult, ALU.add).then_inc(o_done, 1)
                    else:
                        nc.vector.tensor_scalar(dst, o, factor, None, ALU.mult).then_inc(o_done, 1)

                stage()
                maximum(0)
                maximum(1)
                for u in range(units):
                    if u % 2:
                        move_transposed(u)
                    if u + 2 < units:
                        maximum(u + 2)
                    output(u)

            def concat(prefix, n):
                for j in range(KT):
                    name = f"{prefix}.{j}"
                    dve.wait_ge(cat_rounded, KT * n + j + 1)
                    nc.vector.tensor_tensor(h_lo[:, j, :], of(name)[:, :], h_hi[:, j, :].bitcast(F32), ALU.subtract).then_inc(evacuated[JOB[name] % 2], 1)

            def up_gated(l):
                n0, t0 = JOB[f"up{l}.0"], CHUNK[f"up{l}.0"]
                with dve.Fori(0, FT // 2) as i:
                    for f in range(2):
                        c = FT * l + f
                        b = n0 + 2 * f + 1
                        dve.wait_ge(chunks_used, t0 + 2 * f + 2 + 4 * i)
                        dve.wait_ge(evacuated[(b - 1) % 2], (b - 1) // 2 + 1 + 2 * i)
                        nc.vector.tensor_tensor(tmp[:, f, :], sq[:, f, :], bank[b % 2][:, :], ALU.mult).then_inc(act_made, 1)
                        dve.wait_ge(act_made, c + 1 + 2 * i)
                        dve.sem_inc(evacuated[b % 2], 1)
                        dve.wait_ge(act_rounded, c + 1 + 2 * i)
                        j = bass.ds(2 * i + f, 1)
                        nc.vector.tensor_tensor(act_lo[:, j, :].rearrange("p a n -> p (a n)"), tmp[:, f, :],
                                                act_hi[:, j, :].rearrange("p a n -> p (a n)").bitcast(F32), ALU.subtract).then_inc(act_ready, 1)

            def up_relu(l, half):
                n0, t0 = JOB[f"mup{l}{half}.0"], CHUNK[f"mup{l}{half}.0"]
                c0, r0 = 2 * FT + HALF_FT * (2 * l + half), HALF_FT * (2 * l + half)
                with dve.Fori(0, HALF_FT // 4) as i:
                    for f in range(4):
                        b = n0 + f
                        dve.wait_ge(relu_done, r0 + f + 1 + 4 * i)
                        nc.vector.tensor_tensor(tmp[:, f % 2, :], sq[:, f % 2, :], bank[b % 2][:, :], ALU.mult).then_inc(act_made, 1)
                        dve.wait_ge(act_made, c0 + f + 1 + 4 * i)
                        dve.sem_inc(evacuated[b % 2], 1)
                        dve.wait_ge(act_rounded, c0 + f + 1 + 4 * i)
                        j = bass.ds(4 * i + f, 1)
                        nc.vector.tensor_tensor(mact_lo[:, j, :].rearrange("p a n -> p (a n)"), tmp[:, f % 2, :],
                                                mact_hi[:, j, :].rearrange("p a n -> p (a n)").bitcast(F32), ALU.subtract).then_inc(act_ready, 1)

            def down(prefix, per_tile, step_, name, dst, add):
                n0, t0 = JOB[f"{prefix}.0"], CHUNK[f"{prefix}.0"]
                if name:
                    zero_sum(name)
                with dve.Fori(0, KT // step_) as i:
                    for j in range(step_):
                        b = bank[(n0 + j) % 2][:, :]
                        d = dst[:, bass.ds(step_ * i + j, 1), :].rearrange("p a n -> p (a n)")
                        dve.wait_ge(chunks_used, t0 + (j + 1) * per_tile + step_ * per_tile * i)
                        ins = nc.vector.tensor_tensor(d, d, b, ALU.add) if add else nc.vector.tensor_copy(d, b)
                        ins.then_inc(evacuated[(n0 + j) % 2], 1)
                        if name:
                            add_square(j, name, per=step_, i=i)

            dve.sem_inc(o_done, 2)
            dve.sem_inc(probT_ready[1], 1)
            nc.vector.memset(ones[:, :], 1.0 / D)
            nc.vector.memset(eps[:, :], EPS)
            dve.wait_ge(consts_in, 144)
            nc.vector.tensor_copy(ident_b[:, :], ident[:, :])
            nc.vector.tensor_copy(masks_b[:, :], masks[:, :])
            nc.vector.tensor_scalar(nsinks[:, :], sinks[:, :], -1.0, None, ALU.mult).then_inc(consts_made, 1)
            zero_sum("mem")
            for k in range(KT):
                add_square(k, "mem", N_MEM)
            inverse("memsum", N_MEM)
            for l in range(DEPTH):
                norm(f"mem{l}", memx, mem_hi[l], mem_lo[l], N_MEM)
            zero_sum("attn0")
            for k in range(KT):
                add_square(k, "attn0")
            inverse("sum.attn0")
            norm("attn0", x, h_hi, h_lo)
            inverse("ckvsum")
            nc.vector.scalar_tensor_tensor(ckv_n[:, :], ckv[:, :], col("ckv"), rstd[:, :], ALU.mult, ALU.mult).then_inc(ckv_normed, 1)
            index_top(0)
            for name in ROPES[0:6]:
                rope(name)
            wait_evacuated(dve, "widx")
            index_mask(1)
            index_top(1)
            index_mask(2)
            index_top(2)
            index_mask(3)
            for name in ROPES[6:12]:
                rope(name)
            index_top(3)
            dve.wait_ge(roped, 12)
            with dve.Fori(0, 6) as i:
                attend("dsa", 8, i)
            for j in range(2):
                wait_evacuated(dve, f"qmem0.{j}")
            for pair in range(2):
                attend("mem0", 8, 0, pair)
            for l in range(DEPTH):
                if l == 1:
                    inverse("sum.attn1")
                    norm("attn1", x, h_hi, h_lo)
                    dve.wait_ge(cmp_in, 96)
                    for c, s_ in enumerate("kv"):
                        for g in range(2):
                            name = f"{s_}c{g}"
                            wait_product(dve, name)
                            src = of(name)
                            for half in range(2):
                                rows = slice(HD * half, HD * half + HD)
                                tok = src[rows, half:half + 16 * (N_CMP - 1) + 2 * (CMP_PAIRS - 1) + 1]
                                out = cmp_x[c][rows, :, g, :]
                                pos = cmp_pos[c][rows, :].unsqueeze(2).to_broadcast([HD, CMP_PAIRS, N_CMP])
                                win = bass.AP(tok.tensor, tok.offset, [tok.ap[0], [2, CMP_PAIRS], [16, N_CMP]])
                                ins = nc.vector.tensor_tensor(out, win, pos, ALU.add)
                                ins.then_inc(cmp_built, 1)
                            dve.wait_ge(cmp_built, 4 * c + 2 * g + 2)
                            dve.sem_inc(evacuated[JOB[name] % 2], 1)
                    for name in ROPES[12:]:
                        rope(name)
                    wait_evacuated(dve, "gates")
                    dve.wait_ge(roped, len(ROPES))
                    for g in range(2):
                        with dve.Fori(0, 3) as i:
                            attend(f"nsa{g}", 24, i)
                    for j in range(2):
                        wait_evacuated(dve, f"qmem1.{j}")
                    for pair in range(2):
                        attend("mem1", 8, 0, pair)
                concat(f"cat{l}", l)
                zero_sum(f"ffn{l}")
                for j in range(KT):
                    name = f"wo{l}.{j}"
                    wait_product(dve, name)
                    nc.vector.tensor_tensor(x[:, j, :], x[:, j, :], of(name)[:, :], ALU.add).then_inc(evacuated[JOB[name] % 2], 1)
                    add_square(j, f"ffn{l}")
                inverse(f"sum.ffn{l}")
                norm(f"ffn{l}", x, h_hi, h_lo)
                up_gated(l)
                down(f"down{l}", 3, 4, "attn1" if l == 0 else "final", x, True)
            inverse("sum.final")
            zero_sum("mixpre0")
            for k in range(KT):
                nc.vector.scalar_tensor_tensor(x[:, k, :], x[:, k, :], col("final", k), rstd[:, :], ALU.mult, ALU.mult).then_inc(x_normed, 1)
                add_square(k, "mixpre0")
            inverse("sum.mixpre0")
            norm("mixpre0", x, h_hi, h_lo)
            nc.vector.memset(attT[:, :, :], 0.0)
            step(nc.vector.memset(g_reset[:, :], 1.0))
            step(nc.vector.memset(g_reset[:, :].rearrange("p (n c) -> p n c", c=GLA_CHUNK)[:, :, 0:1], 0.0))
            for h in range(4):
                name = f"gz{h}"
                dve.wait_ge(g_absed, h + 1)
                nc.vector.tensor_scalar(g_la[:, :], of(name)[:, :], col(f"gla_b{h}"), 0.0, ALU.add, ALU.min).then_inc(evacuated[JOB[name] % 2], 1)
                wait_evacuated(dve, name)
                dve.wait_ge(g_logged, h + 1)
                nc.vector.tensor_tensor(g_la[:, :], g_la[:, :], g_ab[:, :], ALU.subtract).then_inc(g_cummed, 1)
                dve.wait_ge(g_cummed, 2 * h + 1)
                nc.vector.tensor_tensor_scan(g_cum[:, :], g_reset[:, :], g_la[:, :], 0.0, ALU.mult, ALU.add).then_inc(g_cummed, 1)
                dve.wait_ge(g_cummed, 2 * h + 2)
                cum = g_cum[:, :].rearrange("p (n c) -> p n c", c=GLA_CHUNK)
                last = cum[:, :, GLA_CHUNK - 1:GLA_CHUNK].to_broadcast([P, N_CHUNK, GLA_CHUNK])
                nc.vector.tensor_tensor(g_end.rearrange("p (n c) -> p n c", c=GLA_CHUNK), last, cum, ALU.subtract).then_inc(g_diffed, 1)
                dve.wait_ge(g_exped, 3 * h + 2)
                wait_evacuated(dve, f"gq{h}")
                nc.vector.tensor_copy(decay[:, h, :], g_exp[:, :].rearrange("p (n c) -> p n c", c=GLA_CHUNK)[:, :, GLA_CHUNK - 1])
                nc.vector.scalar_tensor_tensor(gq[:, h, :], gq[:, h, :], float(P) ** -0.5, g_exp[:, :], ALU.mult, ALU.mult).then_inc(g_gated, 1)
                nc.vector.tensor_tensor(k_inv[:, h, :], gk[:, h, :], g_inv, ALU.mult).then_inc(g_gated, 1)
                dve.wait_ge(g_exped, 3 * h + 3)
                nc.vector.tensor_tensor(gk[:, h, :], gk[:, h, :], g_end, ALU.mult).then_inc(g_gated, 1)
            dve.wait_ge(g_gated, 12)
            dve.wait_ge(gla_in, 32)
            for h in range(4):
                name = f"gatt{h}"
                wait_product(dve, name)
                nc.vector.copy_predicated(attT[:, :, :], gla_mask[:, :].unsqueeze(1).to_broadcast([P, TT, P]),
                                          of(name)[:, :].rearrange("p (a n) -> p a n", a=TT)).then_inc(evacuated[JOB[name] % 2], 1)
                for n in range(N_CHUNK - 1):
                    name = f"gds{h}.{n}"
                    wait_product(dve, name)
                    src = of(name)[:, 0:2 * P]
                    if n:
                        wait_evacuated(dve, f"gds{h}.{n - 1}")
                        ins = nc.vector.scalar_tensor_tensor(state[:, n + 1, :], state[:, n, :], decay[:, h, n:n + 1], src, ALU.mult, ALU.add)
                    else:
                        ins = nc.vector.tensor_copy(state[:, 1, :], src)
                    ins.then_inc(evacuated[JOB[name] % 2], 1)
                inverse(f"gosum{h}")
                for j in range(2):
                    step(nc.vector.scalar_tensor_tensor(tmp[:, j, :], g_o[:, j, :], col(f"gla_n{j}"), rstd[:, :], ALU.mult, ALU.mult))
                    wait_evacuated(dve, f"gg{2 * h + j}")
                    nc.vector.tensor_tensor(tmp[:, j, :], tmp[:, j, :], gsilu[:, 2 * h + j, :], ALU.mult).then_inc(go_made, 1)
                for j in range(2):
                    k = 2 * h + j
                    dve.wait_ge(go_rounded, k + 1)
                    nc.vector.tensor_tensor(h_lo[:, k, :], tmp[:, j, :], h_hi[:, k, :].bitcast(F32), ALU.subtract).then_inc(go_split, 1)
            for l in range(DEPTH):
                if l == 1:
                    inverse("sum.mixpre1")
                    nc.vector.memset(one_row[:, :], 1.0)
                    norm("mixpre1", x, h_hi, h_lo)
                    for j in range(KT):
                        name = f"sq{j}"
                        wait_product(dve, name)
                        nc.vector.tensor_scalar(sq_q[:, j, :], of(name)[:, :], col("swa_b_q", j), SCALE, ALU.add, ALU.mult).then_inc(evacuated[JOB[name] % 2], 1)
                    for j in (KT - 2, KT - 1):
                        wait_evacuated(dve, f"sq{j}")
                    for g in range(2):
                        with dve.Fori(0, 4) as i:
                            attend(f"swa{g}", 8, i)
                    concat("scat", 2)
                zero_sum(f"mixpost{l}")
                for j in range(KT):
                    name = f"mix{l}.{j}"
                    wait_product(dve, name)
                    if l == 0:
                        ins = nc.vector.tensor_copy(m[:, j, :], of(name)[:, :])
                    else:
                        ins = nc.vector.tensor_scalar(m[:, j, :], of(name)[:, :], col("swa_b_out", j), None, ALU.add)
                    ins.then_inc(evacuated[JOB[name] % 2], 1)
                    add_square(j, f"mixpost{l}")

                def add_normed(name):
                    for k in range(KT):
                        step(nc.vector.scalar_tensor_tensor(tmp[:, k % 2, :], m[:, k, :], col(name, k), rstd[:, :], ALU.mult, ALU.mult))
                        nc.vector.tensor_tensor(x[:, k, :], x[:, k, :], tmp[:, k % 2, :], ALU.add).then_inc(x_added, 1)

                inverse(f"sum.mixpost{l}")
                zero_sum(f"mlppre{l}")
                add_normed(f"mixpost{l}")
                for k in range(KT):
                    add_square(k, f"mlppre{l}")
                inverse(f"sum.mlppre{l}")
                norm(f"mlppre{l}", x, h_hi, h_lo)
                for half in range(2):
                    up_relu(l, half)
                    down(f"mdown{l}{half}", 2, 2, f"mlppost{l}" if half else None, m, half == 1)
                inverse(f"sum.mlppost{l}")
                if l == 0:
                    zero_sum("mixpre1")
                add_normed(f"mlppost{l}")
                if l == 0:
                    for k in range(KT):
                        add_square(k, "mixpre1")


def by_columns(w):
    k, n = w.shape
    pad = -n % P
    if pad:
        w = np.concatenate([w, np.zeros((k, pad), w.dtype)], 1)
    n = (n + pad) // P
    return w.reshape(k // P, P, n, P).transpose(2, 1, 0, 3).reshape(n, P, k)


def by_rows_of(w, per_tile):
    f, n = w.shape
    pad = per_tile * D - f
    if pad:
        w = np.concatenate([w, np.zeros((pad, n), w.dtype)], 0)
    return w.reshape(per_tile, KT, P, n // P, P).transpose(3, 0, 2, 1, 4).reshape(-1, P, D)


def interleave(a, b):
    return np.stack([a, b], 1).reshape(-1, *a.shape[1:])


def twice(w):
    return np.concatenate([w, w], 1)


def weight_stream(v):
    out = []
    for l in range(DEPTH):
        out.append(by_columns(v["mem_w_kv"][l]))
    w = v["dsa_w_in"][0]
    q, ckv, k_rope, q_idx, k_idx, w_idx, q_mem = np.split(w, np.cumsum([768, 128, 16, 512, 64, 8]).tolist(), 1)
    gap = np.zeros((D, HD - ROPE), w.dtype)
    out += [by_columns(a) for a in (ckv, twice(k_idx), q_idx, w_idx, twice(np.concatenate([k_rope, gap], 1)), q, q_mem)]
    for l in range(DEPTH):
        if l == 1:
            w = v["nsa_w_in"][0]
            q, kc, vc, ks, vs, kw, vw, gates, q_mem = np.split(w, np.cumsum([768] + [128] * 6 + [36]).tolist(), 1)
            for a in (kc, vc, ks, kw):
                out += [by_columns(twice(a[:, 0:HD])), by_columns(twice(a[:, HD:]))]
            out += [by_columns(a) for a in (q, vs, vw, gates, q_mem)]
        out.append(by_columns(v["w_o"][l]))
        gate, upw = np.split(v["ffn_w_in"][l], 2, 1)
        out.append(interleave(by_columns(gate), by_columns(upw)))
        out.append(by_rows_of(v["ffn_w_down"][l], 3))
    w = v["gla_w_in_2"][0]
    q, k, vv, g, glr = np.split(w, np.cumsum([512, 512, 1024, 1024]).tolist(), 1)
    out += [by_columns(a) for a in (glr, k, q, vv, g)]
    for l in range(DEPTH):
        if l == 1:
            w = v["swa_w_in_2"][0]
            q, k, vv = np.split(w, [1024, 1152], 1)
            out += [by_columns(twice(k[:, 0:HD])), by_columns(twice(k[:, HD:])), by_columns(vv), by_columns(q)]
        out.append(by_columns(v["gla_w_out_2"][0] if l == 0 else v["swa_w_out_2"][0]))
        upw, downw = v["mlp_w_up_2"][l], v["mlp_w_down_2"][l]
        for half in range(2):
            f = slice(half * D_FF2 // 2, (half + 1) * D_FF2 // 2)
            out += [by_columns(upw[:, f]), by_rows_of(downw[f], 2)]
    return np.concatenate(out, 0)


def shape_constants():
    inv = 500000.0 ** (-np.arange(0, ROPE, 2, dtype=np.float64) / ROPE)
    ang = np.arange(SEQ, dtype=np.float64)[:, None] * inv[None, :]
    cos, sin = np.cos(ang).astype(np.float32).T, np.sin(ang).astype(np.float32).T
    c, s, perm = np.ones((P, SEQ), np.float32), np.zeros((P, SEQ), np.float32), np.zeros((P, P), np.float32)
    half = ROPE // 2
    for o in (0, HD):
        for d in range(half):
            c[o + d] = c[o + half + d] = cos[d]
            s[o + d] = s[o + half + d] = sin[d]
            perm[o + half + d, o + d] = -1.0
            perm[o + d, o + half + d] = 1.0
    a = np.arange(P)
    prev = np.where(a[None, :] > a[:, None], 0.0, NEG)
    own = np.where(a[None, :] <= a[:, None], 0.0, NEG)
    blocks = np.arange(32)
    cmp_ = [np.where((blocks * 16 + 31)[None, :] <= (t * P + a)[:, None], 0.0, NEG) for t in range(TT)]
    masks = np.concatenate([prev, own] + cmp_, 1).astype(np.float32)
    same = (a[:, None] // GLA_CHUNK == a[None, :] // GLA_CHUNK) & (a[:, None] <= a[None, :])
    return {"ident": np.eye(P, dtype=np.float32), "perm": perm, "rope_c": c, "rope_s": s, "masks": masks, "gla_mask": same.astype(np.int32)}


def lay_out(v):
    f = {n: np.asarray(a) for n, a in v.items()}
    vec = {"final": f["final_norm"], "swa_b_out": f["swa_b_out_2"][0], "swa_b_q": f["swa_b_in_2"][0][0:D]}
    for l in range(DEPTH):
        for name, src in (("attn", "attn_norm"), ("ffn", "ffn_norm"), ("mem", "mem_norm"), ("mixpre", "ln_mix_pre_2"),
                          ("mixpost", "ln_mix_post_2"), ("mlppre", "ln_mlp_pre_2"), ("mlppost", "ln_mlp_post_2")):
            vec[f"{name}{l}"] = f[src][l]
    bk = f["swa_b_in_2"][0][D:D + 2 * HD].reshape(2, HD)
    columns = [vec[n].reshape(KT, P).T for n in GAINS] + [f["dsa_ckv_norm"][0][:, None], f["gla_b_gate_up_2"][0].reshape(4, P).T,
               f["gla_g_norm_2"][0].reshape(2, P).T] + [np.concatenate([b, b])[:, None] for b in bk]
    gap = np.zeros((P, ROPE), np.float32)
    uk = f["dsa_w_uk"][0]
    pairs = lambda a: a.reshape(CMP_PAIRS, P, -1).transpose(1, 0, 2)
    out = {
        "weights": weight_stream(f),
        "memT": f["mem"][0].T.reshape(KT, P, N_MEM).transpose(1, 0, 2),
        "xT": f["x"][0].T.reshape(KT, P, SEQ).transpose(1, 0, 2),
        "cols": np.concatenate(columns, 1),
        "w_uk": np.concatenate([gap, uk, gap, uk], 1),
        "w_uv": f["dsa_w_uv"][0],
        "sinks": np.broadcast_to(f["swa_sinks_2"][0][None, :], (P, 16)),
        "cmp_w1": np.stack([pairs(f["nsa_cmp_k_w1"][0]), pairs(f["nsa_cmp_v_w1"][0])]),
        "cmp_pos": np.stack([f[f"nsa_cmp_pos_{c}"][0].reshape(CMP_PAIRS, P).T for c in "kv"]),
        "cmp_w2k": twice(f["nsa_cmp_k_w2"][0]),
        "cmp_w2v": f["nsa_cmp_v_w2"][0],
        "w_gate": f["gla_w_gate_up_2"][0],
        "sv_b": f["swa_b_in_2"][0][None, D + 2 * HD:],
    }
    out.update(shape_constants())
    return {"in_" + n: np.ascontiguousarray(a) for n, a in out.items()}


def build(nc, arrays):
    A = {n[3:]: nc.dram_tensor(n, a.shape, mybir.dt.from_np(a.dtype), kind="ExternalInput").ap() for n, a in arrays.items()}
    A["out"] = nc.dram_tensor("out", (KT, P, SEQ), F32, kind="ExternalOutput").ap()
    program(nc, A)


def kernel(**inputs):
    import concourse.bacc as bacc
    from concourse.bass_utils import run_bass_kernel_spmd

    arrays = lay_out(inputs)
    nc = bacc.Bacc("TRN2", target_bir_lowering=False, num_devices=1)
    build(nc, arrays)
    r = run_bass_kernel_spmd(nc, [arrays], core_ids=[0])
    return np.ascontiguousarray(r.results[0]["out"].reshape(D, SEQ).T)[None]
```

```python
import math
from contextlib import ExitStack

import numpy as np

import concourse.bass as bass
from concourse import mybir

F32 = mybir.dt.float32
F32R = mybir.dt.float32r
BF16 = mybir.dt.bfloat16
I32 = mybir.dt.int32
ALU = mybir.AluOpType
ACT = mybir.ActivationFunctionType
AX = mybir.AxisListType

P = 128
SEQ, D, N_MEM, DEPTH = 512, 1024, 256, 2
KT = D // P
TT = SEQ // P
HD, ROPE = 64, 16
TOK_HEADS, MEM_HEADS = 12, 4
RANK, IDX_HEADS, IDX_DIM, TOPK = 128, 8, 64, 128
D_FF, D_FF2 = 2816, 4096
FT = D_FF // P
HALF_FT = D_FF2 // P // 2
N_CMP = (SEQ - 32) // 16 + 1
CMP_PAIRS = 16
GLA_HEADS, GLA_CHUNK = 4, 64
N_CHUNK = SEQ // GLA_CHUNK
GATE_NORM = 16.0
SWA_PAIRS = 8
EPS = 1e-6
NEG = -1e30
SCALE = HD ** -0.5
RING = 4
RAW = 2
AHEAD = RING - 1

GAINS = ["attn0", "attn1", "ffn0", "ffn1", "final", "mem0", "mem1", "mixpre0", "mixpre1", "mixpost0",
         "mixpost1", "mlppre0", "mlppre1", "mlppost0", "mlppost1", "swa_b_out", "swa_b_q"]
EXTRA = ["ckv", "gla_b0", "gla_b1", "gla_b2", "gla_b3", "gla_n0", "gla_n1", "swa_bk0", "swa_bk1"]
N_COLS = len(GAINS) * KT + len(EXTRA)


def inverse_of(job):
    return job.replace("sum", "inv")


def plan():
    jobs = [("memsum", 0)]
    for l in range(DEPTH):
        jobs += [(f"mk{l}.{j}", 1) for j in range(2)] + [(f"mv{l}", 2)]
    jobs += [("sum.attn0", 0)]
    jobs += [("ckv", 1), ("ckvsum", 0), ("kidx", 1)] + [(f"qidx{j}", 1) for j in range(4)]
    jobs += [("rope.kidx", 0)] + [(f"rope.qidx{j}", 0) for j in range(4)]
    jobs += [("widx", 1), ("dsa_k", 1), ("dsa_v", 0), ("rope.dsa_k", 0)]
    jobs += [(f"q0.{j}", 1) for j in range(6)] + [(f"rope.q0.{j}", 0) for j in range(6)]
    jobs += [(f"qmem0.{j}", 1) for j in range(2)]
    for l in range(DEPTH):
        if l == 1:
            for s in ("kc", "vc"):
                jobs += [(f"{s}{g}", 1) for g in range(2)]
            jobs += [(f"ks{g}", 1) for g in range(2)] + [(f"kw{g}", 1) for g in range(2)]
            jobs += [("cmp_hk", 0), ("cmp_hv", 0)]
            jobs += [(f"rope.ks{g}", 0) for g in range(2)] + [(f"rope.kw{g}", 0) for g in range(2)]
            jobs += [("cmp_k", 0), ("cmp_v", 0)]
            jobs += [("q1.0", 1)]
            for j in range(1, 6):
                jobs += [(f"q1.{j}", 1), (f"rope.q1.{j - 1}", 0)]
            jobs += [("vsw.a", 0), ("vsw.b", 2), ("rope.q1.5", 0), ("gates", 1)]
            jobs += [(f"qmem1.{j}", 1) for j in range(2)]
        jobs += [(f"cat{l}.{j}", 0) for j in range(KT)]
        jobs += [(f"wo{l}.{j}", 1) for j in range(KT)]
        jobs += [(f"sum.ffn{l}", 0)]
        jobs += [(f"up{l}.{j}", 1) for j in range(2 * FT)]
        jobs += [(f"down{l}.{j}", 3) for j in range(KT)]
        jobs += [("sum.attn1" if l == 0 else "sum.final", 0)]
    jobs += [("sum.mixpre0", 0), ("glr", 1)]
    jobs += [(f"gk{h}", 1) for h in range(4)] + [(f"gq{h}", 1) for h in range(4)]
    for h in range(4):
        jobs += [(f"gz{h}", 0), (f"gv{h}.a", 0), (f"gv{h}.b", 2)]
    jobs += [(f"gg{j}", 1) for j in range(KT)]
    for h in range(4):
        jobs += [(f"gket{h}", 0), (f"gatt{h}", 0)]
        jobs += [(f"gds{h}.{n}", 0) for n in range(N_CHUNK - 1)]
        jobs += [(f"go{h}.{j}", 0) for j in range(2)] + [(f"gosum{h}", 0)]
    for l in range(DEPTH):
        if l == 1:
            jobs += [("sum.mixpre1", 0)] + [(f"sk{g}", 1) for g in range(2)] + [("sv", 1)]
            jobs += [(f"sq{j}", 1) for j in range(KT)] + [(f"scat.{j}", 0) for j in range(KT)]
        jobs += [(f"mix{l}.{j}", 1) for j in range(KT)]
        jobs += [(f"sum.mixpost{l}", 0), (f"sum.mlppre{l}", 0)]
        for half in range(2):
            jobs += [(f"mup{l}{half}.{j}", 1) for j in range(HALF_FT)]
            jobs += [(f"mdown{l}{half}.{j}", 2) for j in range(KT)]
        jobs += [(f"sum.mlppost{l}", 0)]
    return [j for job in jobs for j in ([job, (inverse_of(job[0]), 0)] if "sum" in job[0] else [job])]


JOBS = plan()
JOB, CHUNK, SMALL = {}, {}, {}
_chunks = _small = 0
for _n, (_name, _c) in enumerate(JOBS):
    JOB[_name], CHUNK[_name], SMALL[_name] = _n, _chunks, _small
    _chunks += _c
    _small += _c == 0
N_CHUNKS = _chunks

ROOTS = [name for name, _ in JOBS if "sum" in name]
BURSTS = {"mixpre0": "glr", "mlppre0": "mup00.0", "mixpre1": "sk0", "mlppre1": "mup10.0"}
FIRST = {"mem0": "mk0.0", "mem1": "mk1.0", "attn0": "ckv", "ffn0": "up0.0", "attn1": "kc0", "ffn1": "up1.0", "mixpre0": "glr",
         "mlppre0": "mup00.0", "mixpre1": "sk0", "mlppre1": "mup10.0"}
SUMS = ["mem", "attn0", "ffn0", "attn1", "ffn1", "final", "mixpre0", "mixpost0", "mlppre0", "mlppost0",
        "mixpre1", "mixpost1", "mlppre1", "mlppost1"]
SUMMED = ["mixpost0", "mlppost0", "mixpost1", "mlppost1"]
NORMS = ["mem0", "mem1", "attn0", "ffn0", "attn1", "ffn1", "mixpre0", "mlppre0", "mixpre1", "mlppre1"]
UNITS = [("dsa", 48), ("mem0", 16), ("nsa0", 54), ("nsa1", 54), ("mem1", 16), ("swa0", 32), ("swa1", 32)]
UNIT0 = {n: sum(c for _, c in UNITS[:k]) for k, (n, _) in enumerate(UNITS)}
STAGED = {"dsa": 0, "mem0": 12, "nsa0": 16, "nsa1": 22, "mem1": 28, "swa0": 32, "swa1": 40}


PER_PAIR = {n: 18 if n.startswith("nsa") else 8 for n, _ in UNITS}
STREAMS = [[("dsa", 6, 0), ("mem0", 1, 0), ("mem0", 1, 1)],
           [("nsa0", 3, 0), ("nsa1", 3, 0), ("mem1", 1, 0), ("mem1", 1, 1)],
           [("swa0", 4, 0), ("swa1", 4, 0)]]


def attention_unit(kind, u):
    if kind.startswith("nsa"):
        hh, r = divmod(u, 9)
        return (hh, (r - 1) // 2, 1 + (r - 1) % 2) if r else (hh, 0, 0)
    return u // 4, u % 4, 1


def compressed(kind, u):
    return kind.startswith("nsa") and u % 9 == 0


def slot_of(kind, u):
    return u % (9 if kind.startswith("nsa") else 8)


def bank_of(kind, u):
    return u % (3 if kind.startswith("nsa") else 4)


def attention_stream(eng, passes, begin, pair_of_heads):
    for n, (kind, pairs, pair) in enumerate(passes):
        per = PER_PAIR[kind]
        follow = passes[n + 1] if n + 1 < len(passes) else None
        if n == 0:
            begin(lambda u: (kind, pair, u, 0))
        if pairs > 1:
            with eng.Fori(0, pairs - 1) as i:
                pair_of_heads(per, lambda u: (kind, pair, u, i) if u < per else (kind, pair, u - per, i + 1))

        def at(u):
            if u < per:
                return kind, pair, u, pairs - 1
            return (follow[0], follow[2], u - per, 0) if follow else None

        pair_of_heads(per, at)


def key_tiles(kind, qt, branch):
    if kind.startswith("mem"):
        return list(range(N_MEM // P))
    if kind.startswith("swa"):
        return [qt - 1, qt] if qt else [0]
    return list(range(qt + 1))


def program(nc, A):
    with ExitStack() as ctx:
        def sb(name, shape, dt=F32, where=ctx):
            return where.enter_context(nc.sbuf_tensor(name, shape, dt))

        def sem(name):
            return ctx.enter_context(nc.semaphore(name))

        x = sb("x", [P, KT, SEQ])
        h_hi = sb("h_hi", [P, KT, SEQ], F32R)
        h_lo = sb("h_lo", [P, KT, SEQ], F32R)
        tmp = sb("tmp", [P, 2, SEQ])
        sq = sb("sq", [P, 2, SEQ])
        sqacc = sb("sqacc", [P, SEQ])
        diag = sb("diag", [P, SEQ])
        spare = sb("spare", [P, SEQ])
        w_raw = sb("w_raw", [P, RAW, KT * P])
        w_hi = sb("w_hi", [P, RING, KT * P], F32R)
        w_lo = sb("w_lo", [P, RING, KT * P], F32R)
        ident = sb("ident", [P, P])
        perm = sb("perm", [P, P])
        rope_c = sb("rope_c", [P, SEQ])
        rope_s = sb("rope_s", [P, SEQ])
        masks = sb("masks", [P, 2 * P + TT * 32])
        masks_b = sb("masks_b", [P, 2 * P + TT * 32], BF16)
        ident_b = sb("ident_b", [P, P], BF16)
        ones = sb("ones", [P, P])
        eps = sb("eps", [P, 1])
        cols = sb("cols", [P, N_COLS])
        w_uk = sb("w_uk", [P, P])
        w_uv = sb("w_uv", [P, HD])
        sinks = sb("sinks", [P, 16])
        nsinks = sb("nsinks", [P, 16])
        k_mem = sb("k_mem", [P, DEPTH, 2, N_MEM])
        v_mem = sb("v_mem", [P, DEPTH, 2, 2 * P])
        nmax = sb("nmax", [P, 9])
        psum_p = sb("psum_p", [P, 9])
        rinv = sb("rinv", [P, 9])
        oscale = sb("oscale", [P, 9])

        root, inv_root = rinv[:, 0:TT], oscale[:, 0:TT]

        def norm_tile(k):
            return (tmp, sq)[k // 2 % 2][:, k % 2, :]

        prob, probT = tmp, sq
        q_plain, q_pos0 = diag, spare

        with ExitStack() as s:
            memx = sb("memx", [P, KT, N_MEM], where=s)
            mem_hi = [sb(f"mem_hi{l}", [P, KT, N_MEM], F32R, s) for l in range(DEPTH)]
            mem_lo = [sb(f"mem_lo{l}", [P, KT, N_MEM], F32R, s) for l in range(DEPTH)]
        with ExitStack() as s:
            q_dsa = sb("q_dsa", [P, TOK_HEADS, SEQ], F32R, s)
            k_dsa = [sb(f"k_dsa_{part}", [P, SEQ], F32R, s) for part in ("hi", "lo")]
            dsa_v = sb("dsa_v", [P, TT, HD], where=s)
            dsa_mask = sb("dsa_mask", [P, TT, SEQ], BF16, s)
            qmem0 = sb("qmem0", [P, 2, SEQ], where=s)
            with ExitStack() as s2:
                q0 = sb("q0", [P, 6, SEQ], where=s2)
                ckv = sb("ckv", [P, SEQ], where=s2)
                ckv_n = sb("ckv_n", [P, SEQ], where=s2)
                dsa_k = sb("dsa_k", [P, SEQ], where=s2)
                qidx = sb("qidx", [P, 4, SEQ], where=s2)
                kidx = sb("kidx", [P, SEQ], where=s2)
                widx = sb("widx", [P, TT, IDX_HEADS], where=s2)
                score = sb("score", [P, SEQ], where=s2)
                top8 = sb("top8", [P, 8], where=s2)
                relu_l = sb("relu_l", [P, 2, SEQ], where=s2)
                rope_t0 = sb("rope_t0", [P, 2, SEQ], where=s2)
            q_stage0 = sb("q_stage0", [P, 2, SEQ], F32R, s)
            o_tok0 = sb("o_tok0", [P, TT, D], where=s)
        with ExitStack() as s:
            act_hi = sb("act_hi", [P, FT, SEQ], F32R, s)
            act_lo = sb("act_lo", [P, FT, SEQ], F32R, s)
        with ExitStack() as s:
            q1 = sb("q1", [P, 6, SEQ], where=s)
            qmem1 = sb("qmem1", [P, 2, SEQ], where=s)
            k_nsa = [sb(f"k_nsa_{part}", [P, 4, SEQ], F32R, s) for part in ("hi", "lo")]
            v_nsa = sb("v_nsa", [P, TT, 2 * P], where=s)
            gates = sb("gates", [P, TT, 3 * TOK_HEADS], where=s)
            k_cmp = sb("k_cmp", [P, 2 * N_CMP], where=s)
            v_cmp = sb("v_cmp", [P, 2, TT * HD + TT], where=s)
            c_max = sb("c_max", [P, TT, 1], where=s)
            c_shift = sb("c_shift", [P, TT, 32], where=s)
            c_scale = sb("c_scale", [P, TT, 1], where=s)
            cmp_hk = sb("cmp_hk", [P, 2 * N_CMP], where=s)
            cmp_hv = sb("cmp_hv", [P, 2, TT, 32], where=s)
            cmp_w2k = sb("cmp_w2k", [P, P], where=s)
            cmp_w2v = sb("cmp_w2v", [P, HD], where=s)
            cmp_pos = [sb(f"cmp_pos{c}", [P, CMP_PAIRS], where=s) for c in "kv"]
            with ExitStack() as s2:
                q1r = sb("q1r", [P, 2, SEQ], where=s2)
                k_raw = sb("k_raw", [P, 4, SEQ], where=s2)
                rope_t1 = sb("rope_t1", [P, 2, SEQ], where=s2)
            q_stage1 = sb("q_stage1", [P, 2, SEQ], F32R, s)
            o_tok1 = sb("o_tok1", [P, TT, D], where=s)
            with ExitStack() as s2:
                cmp_w1 = [sb(f"cmp_w1{c}", [P, CMP_PAIRS, P], where=s2) for c in "kv"]
                cmp_x = [sb(f"cmp_x{c}", [P, CMP_PAIRS, 2, N_CMP], where=s2) for c in "kv"]
            q_nsa = sb("q_nsa", [P, TOK_HEADS, SEQ], F32R, s)
        with ExitStack() as s:
            gq = sb("gq", [P, 4, SEQ], where=s)
            gk = sb("gk", [P, 4, SEQ], where=s)
            gv = sb("gv", [P, TT, D], where=s)
            gsilu = sb("gsilu", [P, KT, SEQ], where=s)
            glr = sb("glr", [P, SEQ], where=s)
            w_gate = sb("w_gate", [16, 4 * P], where=s)
            gla_mask = sb("gla_mask", [P, P], I32, s)
            g_ab = sb("g_ab", [P, SEQ], where=s)
            g_la = sb("g_la", [P, SEQ], where=s)
            g_cum = sb("g_cum", [P, SEQ], where=s)
            g_exp = sb("g_exp", [P, SEQ], where=s)
            g_o = sb("g_o", [P, 2, SEQ], where=s)
            g_inv, g_end = g_o[:, 0, :], g_o[:, 1, :]
            g_reset = sb("g_reset", [P, SEQ], where=s)
            k_inv = sb("k_inv", [P, 4, SEQ], where=s)
            decay = sb("decay", [P, 4, N_CHUNK], where=s)
            k_endT = sb("k_endT", [P, TT, P], where=s)
            state = sb("state", [P, N_CHUNK, 2 * P], where=s)
            attT = sb("attT", [P, TT, P], where=s)
        with ExitStack() as s:
            sq_q = sb("sq_q", [P, KT, SEQ], where=s)
            sk = sb("sk", [P, 2, SEQ], where=s)
            sv = sb("sv", [P, TT, P], where=s)
            sv_b = sb("sv_b", [1, P], where=s)
            one_row = sb("one_row", [1, P], where=s)
            k_swa = [sb(f"k_swa_{part}", [P, 2, SEQ], F32R, s) for part in ("hi", "lo")]
            q_swa = sb("q_swa", [P, 2 * SWA_PAIRS, SEQ], F32R, s)
            q_stage2 = sb("q_stage2", [P, 2, SEQ], F32R, s)
            rawmax = sb("rawmax", [P, 9], where=s)
            sinkexp = sb("sinkexp", [P, 9], where=s)
            o_tok2 = sb("o_tok2", [P, TT, D], where=s)
        with ExitStack() as s:
            mact_hi = sb("mact_hi", [P, HALF_FT, SEQ], F32R, s)
            mact_lo = sb("mact_lo", [P, HALF_FT, SEQ], F32R, s)
            m = sb("m", [P, KT, SEQ], where=s)

        bank = [ctx.enter_context(nc.psum_tensor(f"bank{b}", [P, SEQ], F32)) for b in range(8)]
        score_bank, probT_bank, o_bank = bank[2:4] + bank[0:2], bank[4:6], bank[6:8]

        consts_in, mem_in, x_in = sem("consts_in"), sem("mem_in"), sem("x_in")
        cmp_in, gla_in, swa_in = sem("cmp_in"), sem("gla_in"), sem("swa_in")
        raw_loaded = [sem(f"raw_loaded{b}") for b in range(RAW)]
        hi_ready, lo_ready = sem("hi_ready"), sem("lo_ready")
        chunks_used = sem("chunks_used")
        small_done = sem("small_done")
        evacuated = [sem(f"evacuated{b}") for b in range(2)]
        consts_made = sem("consts_made")
        sq_done, sq_added = sem("sq_done"), sem("sq_added")
        h_made, h_rounded = sem("h_made"), sem("h_rounded")
        h_ready = [sem("h_ready_even"), sem("h_ready_odd")]
        diag_ready = sem("diag_ready")
        act_made, act_rounded, act_ready = sem("act_made"), sem("act_rounded"), sem("act_ready")
        x_normed, x_added = sem("x_normed"), sem("x_added")
        ckv_normed, roped = sem("ckv_normed"), sem("roped")
        idx_ready, idx_relu, idx_added, idx_chain = sem("idx_ready"), sem("idx_relu"), sem("idx_added"), sem("idx_chain")
        dsa_masked = sem("dsa_masked")
        q_staged, pos0_staged = sem("q_staged"), sem("pos0_staged")
        q_rounded, q_split, k_rounded, k_split = sem("q_rounded"), sem("q_split"), sem("k_rounded"), sem("k_split")
        scores_ready, max_ready, probs_ready = sem("scores_ready"), sem("max_ready"), sem("probs_ready")
        transposed, pv_done, o_done = sem("transposed"), sem("pv_done"), sem("o_done")
        probT_ready = [sem("probT_ready0"), sem("probT_ready1")]
        rawmax_ready, sum_ready, rinv_ready, sink_ready = sem("rawmax_ready"), sem("sum_ready"), sem("rinv_ready"), sem("sink_ready")
        oscale_ready = sem("oscale_ready")
        cat_rounded = sem("cat_rounded")
        cmp_built, gelu_done = sem("cmp_built"), sem("gelu_done")
        g_absed, g_logged, g_cummed, g_exped, g_ended, g_gated = (sem("g_absed"), sem("g_logged"), sem("g_cummed"),
                                                                  sem("g_exped"), sem("g_ended"), sem("g_gated"))
        g_diffed = sem("g_diffed")
        go_made, go_rounded, go_split = sem("go_made"), sem("go_rounded"), sem("go_split")
        std_ready = sem("std_ready")
        dve_step, act_step = sem("dve_step"), sem("act_step")
        relu_done, stored = sem("relu_done"), sem("stored")

        def col(name, k=0):
            n = GAINS.index(name) * KT + k if name in GAINS else len(GAINS) * KT + EXTRA.index(name)
            return cols[:, n:n + 1]

        def wait_evacuated(eng, name, later=0):
            n = JOB[name]
            eng.wait_ge(evacuated[n % 2], n // 2 + 1 + later)

        def wait_product(eng, name, later=0):
            chunks = dict(JOBS)[name]
            if chunks:
                eng.wait_ge(chunks_used, CHUNK[name] + chunks + later)
            else:
                eng.wait_ge(small_done, SMALL[name] + 1)

        def of(name):
            return bank[JOB[name] % 2]

        ROPES = ["kidx"] + [f"qidx{j}" for j in range(4)] + ["dsa_k"] + [f"q0.{j}" for j in range(6)] + \
                [f"{s}{g}" for s in ("ks", "kw") for g in range(2)] + [f"q1.{j}" for j in range(6)]

        def rope_tile(name):
            if name == "kidx":
                return kidx[:, :], kidx[:, :], rope_t0
            if name.startswith("qidx"):
                t = qidx[:, int(name[4]), :]
                return t, t, rope_t0
            if name == "dsa_k":
                return dsa_k[:, :], dsa_k[:, :], rope_t0
            if name.startswith("q0."):
                t = q0[:, int(name[3]), :]
                return t, t, rope_t0
            if name.startswith("q1."):
                return q1[:, int(name[3]), :], q1r[:, int(name[3]) % 2, :], rope_t1
            t = k_raw[:, 2 * (name[1] == "w") + int(name[2]), :]
            return t, t, rope_t1

        def output_of(kind):
            return {"dsa": o_tok0, "mem0": o_tok0, "nsa0": o_tok1, "nsa1": o_tok1, "mem1": o_tok1}.get(kind, o_tok2)

        def split_queries(kind):
            return {"dsa": (q_dsa, 0, 0), "nsa0": (q_nsa, 0, 6), "nsa1": (q_nsa, 6, 6), "swa0": (q_swa, 0, 12), "swa1": (q_swa, 8, 12)}[kind]

        def staged(kind):
            return {"d": q_stage0, "n": q_stage1, "s": q_stage2}[kind[0]]

        def both_heads(kind, j, tile):
            q = split_queries(kind)[0]
            for hh in range(2):
                rows, others = slice(HD * hh, HD * hh + HD), slice(HD - HD * hh, P - HD * hh)
                yield tile[rows, :], q[rows, 2 * j + hh, :], q[others, 2 * j + hh, :]

        block = ctx.enter_context(nc.Block())

        @block.sync
        def _(sp):
            def load(t, per=0, i=0):
                if per or t >= RAW:
                    sp.wait_ge(lo_ready, t - RAW + 1 + per * i)
                src = A["weights"][t] if not per else \
                    A["weights"][bass.ds(i * per + t, 1)].rearrange("a p n -> p (a n)")
                sp.dma_start(w_raw[:, t % RAW, :], src).then_inc(raw_loaded[t % RAW], 16)

            for t in range(RAW):
                load(t)
            loops = (N_CHUNKS - RAW) // RAW
            with sp.Fori(0, loops) as i:
                for u in range(RAW):
                    load(RAW + u, RAW, i)
            for t in range(RAW + loops * RAW, N_CHUNKS):
                load(t)

        @block.gpsimd
        def _(pool):
            def rest(t, per=0, i=0):
                pool.wait_ge(hi_ready, t + 1 + per * i)
                nc.gpsimd.tensor_tensor(w_lo[:, t % RING, :], w_raw[:, t % RAW, :],
                                        w_hi[:, t % RING, :].bitcast(F32), ALU.subtract).then_inc(lo_ready, 1)

            def rests(t, end):
                while t < end and t % RING:
                    rest(t)
                    t += 1
                loops = (end - t) // RING
                if loops:
                    with pool.Fori(0, loops) as i:
                        for u in range(RING):
                            rest(t + u, RING, i)
                for t in range(t + loops * RING, end):
                    rest(t)

            def stage(hh, kind, pair, u, i):
                rows = slice(HD * hh, HD * hh + HD)
                before = STAGED[kind] + 2 * pair + hh + 2 * i
                if not isinstance(before, int) or before:
                    pool.wait_ge(q_staged, before)
                if kind.startswith("mem"):
                    src = (qmem0 if kind == "mem0" else qmem1)[rows, pair, :]
                    nc.gpsimd.tensor_copy(q_plain[rows, :], src).then_inc(q_staged, 1)
                    return
                if kind.startswith("nsa"):
                    src = q1[rows, bass.ds(i + 3 * int(kind[3]), 1), :].rearrange("p a n -> p (a n)")
                    nc.gpsimd.tensor_copy(q_pos0[rows, :], src).then_inc(pos0_staged, 1)
                    pool.wait_ge(pos0_staged, 6 * int(kind[3]) + hh + 1 + 2 * i)
                q, head, _ = split_queries(kind)
                src = q[:, bass.ds(head + hh + 2 * i, 1), :].rearrange("p a n -> p (a n)")
                nc.gpsimd.tensor_copy(staged(kind)[:, hh, :], src).then_inc(q_staged, 1)

            def attention_begin(at):
                for hh in range(2):
                    stage(hh, *at(0))

            def pair_of_heads(per, at):
                for hh in range(2):
                    if at(per):
                        kind, pair, u, i = at((hh + 1) * per // 2 - 1)
                        pool.wait_ge(scores_ready, UNIT0[kind] + pair * per + u + 1 + per * i)
                        stage(hh, *at(per))

            def add_squares(name):
                b = SUMS.index(name)
                pool.wait_ge(small_done, SMALL[f"sum.{SUMS[b - 1]}"] + 1)
                nc.gpsimd.memset(sqacc[:, :], 0.0).then_inc(sq_added, 1)
                for k in range(KT):
                    pool.wait_ge(sq_done, KT * b + k + 1)
                    pool.wait_ge(sq_added, 9 * b + k + 1)
                    nc.gpsimd.tensor_tensor(sqacc[:, :], sqacc[:, :], sq[:, k % 2, :], ALU.add).then_inc(sq_added, 1)

            def rest_of_norm(name, hi, lo, n=SEQ):
                for k in range(1, KT, 2):
                    pool.wait_ge(h_rounded, KT * NORMS.index(name) + k + 1)
                    nc.gpsimd.tensor_tensor(lo[:, k, :], norm_tile(k)[:, 0:n], hi[:, k, :].bitcast(F32), ALU.subtract).then_inc(h_ready[1], 1)

            def norms(start, names):
                for name in names:
                    end = CHUNK[FIRST[name]] + AHEAD
                    if name == "mem1":
                        end = start
                    rests(start, end)
                    start = end
                    if name in BURSTS:
                        add_squares(name)
                    if name.startswith("mem"):
                        rest_of_norm(name, mem_hi[int(name[3])], mem_lo[int(name[3])], N_MEM)
                    else:
                        rest_of_norm(name, h_hi, h_lo)
                return start

            start = norms(0, ["mem0", "mem1", "attn0"])
            for passes, after, heads, last, names in ((STREAMS[0], "wo0.0", 12, "qmem0.1", ["ffn0", "attn1"]),
                                                      (STREAMS[1], "wo1.0", 24, "qmem1.1", ["ffn1", "mixpre0", "mlppre0", "mixpre1"]),
                                                      (STREAMS[2], "mix1.0", 40, None, ["mlppre1"])):
                rests(start, CHUNK[after] + AHEAD)
                start = CHUNK[after] + AHEAD
                pool.wait_ge(q_split, heads)
                if last:
                    for name in (last[:-1] + "0", last):
                        wait_evacuated(pool, name)
                attention_stream(pool, passes, attention_begin, pair_of_heads)
                start = norms(start, names)
            rests(start, N_CHUNKS)

        @block.tensor
        def _(pe):
            def bank_free(n, per=0, i=0):
                if per or n >= 2:
                    pe.wait_ge(evacuated[n % 2], n // 2 + per // 2 * i)

            def chunk_ready(t, per=0, i=0):
                pe.wait_ge(lo_ready, t + 1 + per * i)

            def three(out, w, xs, first, last, swap=False):
                (wh, wl), (xh, xl) = w, xs
                for n, (a, b) in enumerate(((wh, xh), (wh, xl), (wl, xh))):
                    if swap:
                        a, b = b, a
                    r = nc.tensor.matmul(out, a, b, start=first and n == 0, stop=last and n == 2)
                return r

            def slot(t, k, width=P):
                return (w_hi[:, t % RING, k * P:k * P + width], w_lo[:, t % RING, k * P:k * P + width])

            def column_tile(name, hs=(h_hi, h_lo), n=SEQ, last=True, norm=None):
                t = CHUNK[name]
                bank_free(JOB[name])
                chunk_ready(t)
                for k in range(KT):
                    if norm:
                        normed(norm, k)
                    r = three(of(name)[:, 0:n], slot(t, k), (hs[0][:, k, :], hs[1][:, k, :]), k == 0, last and k == KT - 1)
                if last:
                    r.then_inc(chunks_used, 1)

            def token_tiles(name, chunks, tiles, hs=(h_hi, h_lo)):
                t = CHUNK[name]
                assert t % RING < RING - 1
                bank_free(JOB[name])
                chunk_ready(t + 1)
                for n, a in enumerate(tiles):
                    for k in range(KT):
                        w = [part[:, t % RING:t % RING + 2, k * P:(k + 1) * P] for part in (w_hi, w_lo)]
                        xs = (hs[0][:, k, a * P:(a + 1) * P], hs[1][:, k, a * P:(a + 1) * P])
                        out = of(name)[:, n * 2 * P:(n + 1) * 2 * P].rearrange("p (c n) -> p c n", c=2)
                        r = three(out, w, xs, k == 0, k == KT - 1, swap=True)
                r.then_inc(*((chunks_used, 2) if chunks else (small_done, 1)))

            def token_tile(name, hs=(h_hi, h_lo), tiles=TT, width=P, bias=None):
                t = CHUNK[name]
                bank_free(JOB[name])
                chunk_ready(t)
                for a in range(tiles):
                    out = of(name)[:, a * width:(a + 1) * width]
                    for k in range(KT):
                        xs = (hs[0][:, k, a * P:(a + 1) * P], hs[1][:, k, a * P:(a + 1) * P])
                        r = three(out, slot(t, k, width), xs, k == 0, bias is None and k == KT - 1, swap=True)
                    if bias is not None:
                        r = nc.tensor.matmul(out, one_row[0:1, :], bias, start=False, stop=True)
                r.then_inc(chunks_used, 1)

            def normed(name, k):
                pe.wait_ge(h_ready[k % 2], KT // 2 * NORMS.index(name) + k // 2 + 1)

            def sum_of(job, sources, n=SEQ):
                bank_free(JOB[job])
                for a in range(n // P):
                    for c, src in enumerate(sources):
                        r = nc.tensor.matmul(of(job)[:, a:a + 1], src[:, a * P:(a + 1) * P], ones[:, 0:1],
                                             start=c == 0, stop=c == len(sources) - 1)
                r.then_inc(small_done, 1)
                job = inverse_of(job)
                bank_free(JOB[job])
                pe.wait_ge(diag_ready, ROOTS.index(job.replace("inv", "sum")) + 1)
                nc.tensor.matmul(of(job)[:, 0:n], ones[:, :], diag[:, 0:n], start=True, stop=True).then_inc(small_done, 1)

            def sum_squares(name, n=SEQ):
                pe.wait_ge(sq_added, 9 * (SUMS.index(name) + 1))
                sum_of("memsum" if name == "mem" else f"sum.{name}", [sqacc], n)

            def rope(name):
                job = f"rope.{name}"
                bank_free(JOB[job])
                wait_evacuated(pe, name)
                nc.tensor.matmul(of(job)[:, :], perm[:, :], rope_tile(name)[0], start=True, stop=True).then_inc(small_done, 1)

            def index_scores(qt):
                for h in range(IDX_HEADS):
                    n = (qt - 1) * IDX_HEADS + h
                    if n >= 2:
                        pe.wait_ge(idx_relu, n - 1)
                    o = HD * (h % 2)
                    nc.tensor.matmul(score_bank[n % 2][:, 0:(qt + 1) * P], qidx[o:o + HD, h // 2, qt * P:(qt + 1) * P],
                                     kidx[o:o + HD, 0:(qt + 1) * P], start=True, stop=True).then_inc(idx_ready, 1)

            def scores(kind, pair, u, i):
                hh, qt, br = attention_unit(kind, u)
                per, o, l = PER_PAIR[kind], HD * hh, int(kind[3]) if kind[3:] else 0
                g = UNIT0[kind] + pair * per + u
                out = score_bank[bank_of(kind, u)]
                if u % (per // 2) == 0:
                    pe.wait_ge(q_staged, STAGED[kind] + 2 * pair + hh + 1 + 2 * i)
                pe.wait_ge(probs_ready, g + per * i)
                if compressed(kind, u):
                    nc.tensor.matmul(out[:, 0:P], ident_b[:, :], masks_b[:, 2 * P:3 * P], start=True, stop=False)
                    for a in range(TT):
                        r = nc.tensor.matmul(out[:, 32 * a:32 * a + N_CMP], q_pos0[o:o + HD, a * P:(a + 1) * P],
                                             k_cmp[o:o + HD, l * N_CMP:(l + 1) * N_CMP], start=False, stop=a == TT - 1)
                    r.then_inc(scores_ready, 1)
                    return
                kts = key_tiles(kind, qt, br)
                n = len(kts) * P
                if kind.startswith("mem"):
                    nc.tensor.matmul(out[:, 0:n], q_plain[o:o + HD, qt * P:(qt + 1) * P], k_mem[o:o + HD, l, pair, :],
                                     start=True, stop=True).then_inc(scores_ready, 1)
                    return
                q = staged(kind)[:, hh, qt * P:(qt + 1) * P]
                if kind == "dsa":
                    ks, mask = [k[:, 0:n] for k in k_dsa], dsa_mask[:, qt, 0:n]
                elif kind.startswith("swa"):
                    ks, mask = [k[:, l, kts[0] * P:(qt + 1) * P] for k in k_swa], masks_b[:, 2 * P - n:2 * P]
                else:
                    ks, mask = [k[:, 2 * (br - 1) + l, 0:n] for k in k_nsa], masks_b[:, P:2 * P]
                for part, k in enumerate(ks):
                    nc.tensor.matmul(out[:, 0:n], q, k, start=part == 0, stop=False)
                m0 = n - P if kind.startswith("nsa") else 0
                nc.tensor.matmul(out[:, m0:n], ident_b[:, :], mask, start=False, stop=True).then_inc(scores_ready, 1)

            def transposes(kind, pair, u, i):
                _, qt, br = attention_unit(kind, u)
                per = PER_PAIR[kind]
                g = UNIT0[kind] + pair * per + u
                pe.wait_ge(probs_ready, g + 3 + per * i)
                pe.wait_ge(probT_ready[g % 2], g // 2 + 1 + per // 2 * i)
                for n in range(1 if compressed(kind, u) else len(key_tiles(kind, qt, br))):
                    r = nc.tensor.transpose(probT_bank[g % 2][:, n * P:(n + 1) * P], prob[:, g % 2, n * P:(n + 1) * P], ident[:, :])
                r.then_inc(transposed, 1)

            def values(kind, pair, u, i):
                hh, qt, br = attention_unit(kind, u)
                per, l = PER_PAIR[kind], int(kind[3]) if kind[3:] else 0
                g = UNIT0[kind] + pair * per + u
                pe.wait_ge(probT_ready[g % 2], g // 2 + 2 + per // 2 * i)
                pe.wait_ge(o_done, g + 1 + per * i)
                if compressed(kind, u):
                    r = nc.tensor.matmul(o_bank[g % 2][:, 0:TT * HD + TT], probT[:, g % 2, 0:P], v_cmp[:, l, :], start=True, stop=True)
                    r.then_inc(pv_done, 1)
                    return
                kts = key_tiles(kind, qt, br)
                for n, kt in enumerate(kts):
                    if kind == "dsa":
                        v = dsa_v[:, kt, :]
                    elif kind.startswith("mem"):
                        v = v_mem[:, l, kt, (2 * pair + hh) * HD:(2 * pair + hh + 1) * HD]
                    elif kind.startswith("swa"):
                        v = sv[:, kt, l * HD:(l + 1) * HD]
                    else:
                        v = v_nsa[:, kt, (br - 1) * P + l * HD:(br - 1) * P + (l + 1) * HD]
                    r = nc.tensor.matmul(o_bank[g % 2][:, 0:HD], probT[:, g % 2, n * P:(n + 1) * P], v, start=n == 0, stop=n == len(kts) - 1)
                r.then_inc(pv_done, 1)

            def attention_begin(at):
                for u in range(4):
                    scores(*at(u))
                for u in range(2):
                    transposes(*at(u))

            def pair_of_heads(per, at):
                for u in range(per):
                    if at(u + 4):
                        scores(*at(u + 4))
                    if at(u + 2):
                        transposes(*at(u + 2))
                    values(*at(u))

            def concat(prefix, kind, units):
                o_tok = output_of(kind)
                pe.wait_ge(o_done, 2 + units)
                for j in range(KT):
                    name = f"{prefix}.{j}"
                    bank_free(JOB[name])
                    for a in range(TT):
                        r = nc.tensor.transpose(of(name)[:, a * P:(a + 1) * P], o_tok[:, a, j * P:(j + 1) * P], ident[:, :])
                    r.then_inc(small_done, 1)

            def up(prefix, tiles, norm):
                n0, t0 = JOB[f"{prefix}.0"], CHUNK[f"{prefix}.0"]
                with pe.Fori(0, tiles // 4) as i:
                    for u in range(4):
                        bank_free(n0 + u, 4, i)
                        chunk_ready(t0 + u, 4, i)
                        for k in range(KT):
                            if u == 0:
                                normed(norm, k)
                            r = three(bank[(n0 + u) % 2][:, :], slot(t0 + u, k), (h_hi[:, k, :], h_lo[:, k, :]), k == 0, k == KT - 1)
                        r.then_inc(chunks_used, 1)

            def down(prefix, hi, lo, tiles, per_tile, step):
                n0, t0 = JOB[f"{prefix}.0"], CHUNK[f"{prefix}.0"]
                with pe.Fori(0, KT // step) as i:
                    for j in range(step):
                        bank_free(n0 + j, step, i)
                        for c in range(per_tile):
                            t = t0 + j * per_tile + c
                            chunk_ready(t, step * per_tile, i)
                            ks_ = min(KT, tiles - c * KT)
                            for k in range(ks_):
                                f = c * KT + k
                                r = three(bank[(n0 + j) % 2][:, :], slot(t, k), (hi[:, f, :], lo[:, f, :]), f == 0, f == tiles - 1)
                            r.then_inc(chunks_used, 1)

            pe.sem_inc(transposed, 2)
            pe.sem_inc(pv_done, 2)
            pe.wait_ge(consts_made, 1)
            sum_squares("mem", N_MEM)
            for l in range(DEPTH):
                for j in range(2):
                    column_tile(f"mk{l}.{j}", (mem_hi[l], mem_lo[l]), N_MEM, norm=None if j else f"mem{l}")
                token_tiles(f"mv{l}", 2, range(2), (mem_hi[l], mem_lo[l]))
            sum_squares("attn0")
            column_tile("ckv", norm="attn0")
            wait_evacuated(pe, "ckv")
            sum_of("ckvsum", [sq[:, 0, :]])
            column_tile("kidx")
            for j in range(4):
                column_tile(f"qidx{j}")
            rope("kidx")
            for j in range(4):
                rope(f"qidx{j}")
            token_tile("widx", width=IDX_HEADS)
            column_tile("dsa_k", last=False)
            pe.wait_ge(ckv_normed, 1)
            nc.tensor.matmul(of("dsa_k")[:, :], w_uk[:, :], ckv_n[:, :], start=False, stop=True).then_inc(chunks_used, 1)
            bank_free(JOB["dsa_v"])
            for a in range(TT):
                r = nc.tensor.matmul(of("dsa_v")[:, a * HD:(a + 1) * HD], ckv_n[:, a * P:(a + 1) * P], w_uv[:, :], start=True, stop=True)
            r.then_inc(small_done, 1)
            rope("dsa_k")
            pe.wait_ge(roped, 5)
            index_scores(1)
            for j in range(3):
                column_tile(f"q0.{j}")
            index_scores(2)
            for j in range(3, 6):
                column_tile(f"q0.{j}")
            index_scores(3)
            for j in range(6):
                rope(f"q0.{j}")
            for j in range(2):
                column_tile(f"qmem0.{j}")
            pe.wait_ge(roped, 12)
            pe.wait_ge(dsa_masked, TT)
            wait_evacuated(pe, "dsa_v")
            for j in range(2):
                wait_evacuated(pe, f"qmem0.{j}")
            pe.wait_ge(q_split, 12)
            pe.wait_ge(k_split, 1)
            attention_stream(pe, STREAMS[0], attention_begin, pair_of_heads)
            for l in range(DEPTH):
                if l == 1:
                    for s_ in ("kc", "vc", "ks", "kw"):
                        for g in range(2):
                            column_tile(f"{s_}{g}", norm="attn1" if f"{s_}{g}" == "kc0" else None)
                    for c, name in enumerate(("cmp_hk", "cmp_hv")):
                        bank_free(JOB[name])
                        pe.wait_ge(cmp_built, 4 * (c + 1))
                        for p_ in range(CMP_PAIRS):
                            r = nc.tensor.matmul(of(name)[:, 0:2 * N_CMP], cmp_w1[c][:, p_, :],
                                                 cmp_x[c][:, p_, :, :].rearrange("p g c -> p (g c)"),
                                                 start=p_ == 0, stop=p_ == CMP_PAIRS - 1)
                        r.then_inc(small_done, 1)
                    for s_ in ("ks", "kw"):
                        for g in range(2):
                            rope(f"{s_}{g}")
                    bank_free(JOB["cmp_k"])
                    wait_evacuated(pe, "cmp_hk")
                    nc.tensor.matmul(of("cmp_k")[:, 0:2 * N_CMP], cmp_w2k[:, :], cmp_hk[:, :], start=True, stop=True).then_inc(small_done, 1)
                    bank_free(JOB["cmp_v"])
                    wait_evacuated(pe, "cmp_hv")
                    for g in range(2):
                        r = nc.tensor.matmul(of("cmp_v")[:, g * HD:(g + 1) * HD], cmp_hv[:, g, :, :].rearrange("p a c -> p (a c)"),
                                             cmp_w2v[:, :], start=True, stop=True)
                    r.then_inc(small_done, 1)
                    column_tile("q1.0")
                    for j in range(1, 6):
                        column_tile(f"q1.{j}")
                        rope(f"q1.{j - 1}")
                    token_tiles("vsw.a", 0, (0, 1))
                    token_tiles("vsw.b", 2, (2, 3))
                    rope("q1.5")
                    token_tile("gates", width=3 * TOK_HEADS)
                    for j in range(2):
                        column_tile(f"qmem1.{j}")
                    pe.wait_ge(roped, len(ROPES))
                    for name in ("cmp_k", "cmp_v", "vsw.a", "vsw.b"):
                        wait_evacuated(pe, name)
                    for j in range(2):
                        wait_evacuated(pe, f"qmem1.{j}")
                    pe.wait_ge(q_split, 24)
                    pe.wait_ge(k_split, 5)
                    attention_stream(pe, STREAMS[1], attention_begin, pair_of_heads)
                concat(f"cat{l}", f"mem{l}", UNIT0[f"mem{l}"] + 16)
                wait_evacuated(pe, f"cat{l}.{KT - 2}")
                wait_evacuated(pe, f"cat{l}.{KT - 1}")
                for j in range(KT):
                    column_tile(f"wo{l}.{j}")
                sum_squares(f"ffn{l}")
                up(f"up{l}", 2 * FT, f"ffn{l}")
                pe.wait_ge(act_ready, FT * (l + 1))
                down(f"down{l}", act_hi, act_lo, FT, 3, 4)
                sum_squares("attn1" if l == 0 else "final")
            sum_squares("mixpre0")
            column_tile("glr", norm="mixpre0")
            for h in range(4):
                column_tile(f"gk{h}")
            for h in range(4):
                column_tile(f"gq{h}")
            pe.wait_ge(gla_in, 32)
            for h in range(4):
                bank_free(JOB[f"gz{h}"])
                wait_evacuated(pe, "glr")
                nc.tensor.matmul(of(f"gz{h}")[:, :], w_gate[:, h * P:(h + 1) * P], glr[0:16, :], start=True, stop=True).then_inc(small_done, 1)
                token_tiles(f"gv{h}.a", 0, (0, 1))
                token_tiles(f"gv{h}.b", 2, (2, 3))
            for j in range(KT):
                column_tile(f"gg{j}")
            for h in range(4):
                name = f"gket{h}"
                bank_free(JOB[name])
                pe.wait_ge(g_gated, 3 * (h + 1))
                for a in range(TT):
                    r = nc.tensor.transpose(of(name)[:, a * P:(a + 1) * P], gk[:, h, a * P:(a + 1) * P], ident[:, :])
                r.then_inc(small_done, 1)
                name = f"gatt{h}"
                bank_free(JOB[name])
                for a in range(TT):
                    r = nc.tensor.matmul(of(name)[:, a * P:(a + 1) * P], k_inv[:, h, a * P:(a + 1) * P], gq[:, h, a * P:(a + 1) * P],
                                         start=True, stop=True)
                r.then_inc(small_done, 1)
                wait_evacuated(pe, f"gket{h}")
                for n in range(N_CHUNK - 1):
                    name = f"gds{h}.{n}"
                    bank_free(JOB[name])
                    o = GLA_CHUNK * (n % 2)
                    nc.tensor.matmul(of(name)[:, 0:2 * P], k_endT[o:o + GLA_CHUNK, n // 2, :],
                                     gv[o:o + GLA_CHUNK, n // 2, h * 2 * P:(h + 1) * 2 * P], start=True, stop=True).then_inc(small_done, 1)
                wait_evacuated(pe, f"gatt{h}")
                wait_evacuated(pe, f"gds{h}.{N_CHUNK - 2}")
                for j in range(2):
                    name = f"go{h}.{j}"
                    bank_free(JOB[name])
                    for a in range(TT):
                        c0 = h * 2 * P + j * P
                        r = nc.tensor.matmul(of(name)[:, a * P:(a + 1) * P], gv[:, a, c0:c0 + P], attT[:, a, :], start=True, stop=False)
                        for n in (2 * a, 2 * a + 1):
                            if n:
                                r = nc.tensor.matmul(of(name)[:, n * GLA_CHUNK:(n + 1) * GLA_CHUNK], state[:, n, j * P:(j + 1) * P],
                                                     gq[:, h, n * GLA_CHUNK:(n + 1) * GLA_CHUNK], start=False, stop=n % 2 == 1)
                    r.then_inc(small_done, 1)
                for j in range(2):
                    wait_evacuated(pe, f"go{h}.{j}")
                sum_of(f"gosum{h}", [sq[:, j, :] for j in range(2)])
            pe.wait_ge(go_split, KT)
            for l in range(DEPTH):
                if l == 1:
                    sum_squares("mixpre1")
                    for g in range(2):
                        column_tile(f"sk{g}", norm=None if g else "mixpre1")
                    pe.wait_ge(swa_in, 16)
                    token_tile("sv", bias=sv_b[0:1, :])
                    for j in range(KT):
                        column_tile(f"sq{j}")
                    for name in ("sk0", "sk1", "sv"):
                        wait_evacuated(pe, name)
                    pe.wait_ge(q_split, 40)
                    pe.wait_ge(k_split, 7)
                    attention_stream(pe, STREAMS[2], attention_begin, pair_of_heads)
                    concat("scat", "swa1", UNIT0["swa1"] + 32)
                    wait_evacuated(pe, f"scat.{KT - 2}")
                    wait_evacuated(pe, f"scat.{KT - 1}")
                for j in range(KT):
                    column_tile(f"mix{l}.{j}")
                sum_squares(f"mixpost{l}")
                sum_squares(f"mlppre{l}")
                for half in range(2):
                    up(f"mup{l}{half}", HALF_FT, f"mlppre{l}")
                    pe.wait_ge(act_ready, 2 * FT + HALF_FT * (2 * l + half + 1))
                    down(f"mdown{l}{half}", mact_hi, mact_lo, HALF_FT, 2, 2)
                sum_squares(f"mlppost{l}")

        @block.scalar
        def _(act):
            following = [0]

            def split(t, per=0, i=0):
                act.wait_ge(raw_loaded[t % RAW], 16 * (t // RAW + 1) + 16 * per // RAW * i)
                if per or t >= RING:
                    act.wait_ge(chunks_used, t - RING + 1 + per * i)
                nc.scalar.activation(w_hi[:, t % RING, :], w_raw[:, t % RAW, :], ACT.Copy).then_inc(hi_ready, 1)

            def split_ahead(t):
                while following[0] <= min(t + AHEAD, N_CHUNKS - 1):
                    split(following[0])
                    following[0] += 1

            def product(name, c=None):
                n = dict(JOBS)[name]
                if n:
                    split_ahead(CHUNK[name] + n - 1)
                wait_product(act, name)

            def move(name, out, src=None, func=ACT.Copy, **how):
                product(name)
                nc.scalar.activation(out, of(name)[:, 0:SEQ] if src is None else src, func, **how).then_inc(evacuated[JOB[name] % 2], 1)

            def square(k, name, src, n=SEQ, ready=None, later=0):
                b = 9 * SUMS.index(name)
                if b or k >= 2:
                    act.wait_ge(sq_added, b + k if k >= 2 else b)
                if name == "attn0" and k < 2:
                    act.wait_ge(h_ready[k], KT)
                nc.scalar.activation(sq[:, k % 2, 0:n], src, ACT.Square).then_inc(sq_done, 1)

            def deviation(job, n=SEQ, scale=1.0):
                product(job)
                nc.scalar.activation(root[:, 0:n // P], of(job)[:, 0:n // P], ACT.Sqrt, scale=scale, bias=eps[:, 0:1]).then_inc(evacuated[JOB[job] % 2], 1)

            def round_norm(name, hi, n=SEQ):
                for k in range(KT):
                    act.wait_ge(h_made, KT * NORMS.index(name) + k + 1)
                    nc.scalar.activation(hi[:, k, :], norm_tile(k)[:, 0:n], ACT.Copy).then_inc(h_rounded, 1)

            def index_relu(qt):
                n_ = (qt + 1) * P
                for h in range(IDX_HEADS):
                    n = (qt - 1) * IDX_HEADS + h
                    act.wait_ge(idx_ready, n + 1)
                    if n >= 2:
                        act.wait_ge(idx_added, n - 1)
                    nc.scalar.activation(relu_l[:, n % 2, 0:n_], score_bank[n % 2][:, 0:n_], ACT.Relu).then_inc(idx_relu, 1)

            def round_queries(kind, j, tile):
                for part, hi, _ in both_heads(kind, j, tile):
                    nc.scalar.activation(hi, part, ACT.Copy).then_inc(q_rounded, 1)

            def exponentials(kind, pair, u, i):
                _, qt, br = attention_unit(kind, u)
                per = PER_PAIR[kind]
                g, s4 = UNIT0[kind] + pair * per + u, slot_of(kind, u)
                act.wait_ge(max_ready, g + 1 + per * i)
                act.wait_ge(transposed, g + 1 + per * i)
                if compressed(kind, u):
                    nc.scalar.activation(prob[:, g % 2, 0:P], c_shift[:, :, :].rearrange("p a c -> p (a c)"), ACT.Exp).then_inc(probs_ready, 1)
                    return
                n = P * len(key_tiles(kind, qt, br))
                nc.scalar.activation(prob[:, g % 2, 0:n], score_bank[bank_of(kind, u)][:, 0:n], ACT.Exp, bias=nmax[:, s4:s4 + 1],
                                     accum_out=psum_p[:, s4:s4 + 1]).then_inc(probs_ready, 1)
                if kind.startswith("swa"):
                    head = (8 * int(kind[3]) + u // 4) + 2 * i
                    nc.scalar.activation(sinkexp[:, s4:s4 + 1], sinks[:, bass.ds(head, 1)], ACT.Exp,
                                         bias=nmax[:, s4:s4 + 1]).then_inc(sink_ready, 1)

            def move_transposed(kind, pair, u, i):
                _, qt, br = attention_unit(kind, u)
                per = PER_PAIR[kind]
                g, n = UNIT0[kind] + pair * per + u, P if compressed(kind, u) else P * len(key_tiles(kind, qt, br))
                act.wait_ge(transposed, g + 3 + per * i)
                act.wait_ge(pv_done, g + 1 + per * i)
                nc.scalar.activation(probT[:, g % 2, 0:n], probT_bank[g % 2][:, 0:n], ACT.Copy).then_inc(probT_ready[g % 2], 1)

            def attention_begin(at):
                for u in range(3):
                    exponentials(*at(u))
                move_transposed(*at(0))

            def pair_of_heads(per, at):
                for u in range(per):
                    if at(u + 3):
                        exponentials(*at(u + 3))
                    if u % 2 == 0 and at(u + 2):
                        move_transposed(*at(u + 2))

            def concat(prefix, n):
                for j in range(KT):
                    name = f"{prefix}.{j}"
                    product(name)
                    nc.scalar.activation(h_hi[:, j, :], of(name)[:, :], ACT.Copy).then_inc(cat_rounded, 1)

            def loop(t0, steps, per, body):
                split_ahead(t0 - 1)
                over = t0 + per * steps + AHEAD > N_CHUNKS
                with act.Fori(0, steps - over) as i:
                    body(i, lambda u: split(t0 + u + AHEAD, per, i))
                following[0] = t0 + per * (steps - over) + AHEAD
                if over:
                    last = steps - 1
                    body(last, lambda u: split_ahead(t0 + per * last + u))

            def up_gated(l):
                n0, t0 = JOB[f"up{l}.0"], CHUNK[f"up{l}.0"]

                def body(i, ahead):
                    for f in range(2):
                        b = n0 + 2 * f
                        ahead(2 * f)
                        act.wait_ge(chunks_used, t0 + 2 * f + 1 + 4 * i)
                        if FT * l or f == 0:
                            pass
                        act.wait_ge(act_made, FT * l + f + 2 * i)
                        nc.scalar.activation(sq[:, f, :], bank[b % 2][:, :], ACT.Silu).then_inc(evacuated[b % 2], 1)
                        ahead(2 * f + 1)
                        act.wait_ge(act_made, FT * l + f + 1 + 2 * i)
                        nc.scalar.activation(act_hi[:, bass.ds(2 * i + f, 1), :].rearrange("p a n -> p (a n)"), tmp[:, f, :], ACT.Copy).then_inc(act_rounded, 1)

                loop(t0, FT // 2, 4, body)

            def up_relu(l, half):
                t0, n0 = CHUNK[f"mup{l}{half}.0"], JOB[f"mup{l}{half}.0"]
                c0 = 2 * FT + HALF_FT * (2 * l + half)

                def body(i, ahead):
                    for f in range(4):
                        ahead(f)
                        act.wait_ge(chunks_used, t0 + f + 1 + 4 * i)
                        act.wait_ge(act_made, c0 + f - 1 + 4 * i)
                        nc.scalar.activation(sq[:, f % 2, :], bank[(n0 + f) % 2][:, :], ACT.Relu).then_inc(relu_done, 1)
                        act.wait_ge(act_made, c0 + f + 1 + 4 * i)
                        nc.scalar.activation(mact_hi[:, bass.ds(4 * i + f, 1), :].rearrange("p a n -> p (a n)"), tmp[:, f % 2, :], ACT.Copy).then_inc(act_rounded, 1)

                loop(t0, HALF_FT // 4, 4, body)

            def down(prefix, per_tile, step, name, dst):
                t0, n0 = CHUNK[f"{prefix}.0"], JOB[f"{prefix}.0"]

                def body(i, ahead):
                    for j in range(step):
                        for c in range(per_tile):
                            ahead(j * per_tile + c)
                        if name:
                            act.wait_ge(evacuated[(n0 + j) % 2], (n0 + j) // 2 + 1 + step // 2 * i)
                            act.wait_ge(sq_added, 9 * SUMS.index(name) + j + step * i)
                            nc.scalar.activation(sq[:, j % 2, :], dst[:, bass.ds(step * i + j, 1), :].rearrange("p a n -> p (a n)"),
                                                 ACT.Square).then_inc(sq_done, 1)

                loop(t0, KT // step, step * per_tile, body)

            act.sem_inc(probs_ready, 2)
            act.sem_inc(probT_ready[0], 1)
            act.dma_start(memx[:, :, :], A["memT"]).then_inc(mem_in, 16)
            for dst, src in ((cols[:, :], A["cols"]), (ident[:, :], A["ident"]), (perm[:, :], A["perm"]), (rope_c[:, :], A["rope_c"]),
                             (rope_s[:, :], A["rope_s"]), (masks[:, :], A["masks"]),
                             (w_uk[:, :], A["w_uk"]), (w_uv[:, :], A["w_uv"]), (sinks[:, :], A["sinks"])):
                act.dma_start(dst, src).then_inc(consts_in, 16)
            act.dma_start(x[:, :, :], A["xT"]).then_inc(x_in, 16)
            act.wait_ge(consts_made, 1)
            act.wait_ge(mem_in, 16)
            for k in range(KT):
                square(k, "mem", memx[:, k, :], N_MEM)
            deviation("memsum", N_MEM)
            split_ahead(-1)
            round_norm("mem0", mem_hi[0], N_MEM)
            round_norm("mem1", mem_hi[1], N_MEM)
            act.wait_ge(x_in, 16)
            for k in range(KT):
                square(k, "attn0", x[:, k, :])
            for l in range(DEPTH):
                for j in range(2):
                    move(f"mk{l}.{j}", k_mem[:, l, j, :], of(f"mk{l}.{j}")[:, 0:N_MEM])
                move(f"mv{l}", v_mem[:, l, :, :], of(f"mv{l}")[:, :].rearrange("p (a n) -> p a n", a=2))
            deviation("sum.attn0")
            round_norm("attn0", h_hi)
            product("ckv")
            nc.scalar.activation(ckv[:, :], of("ckv")[:, :], ACT.Copy).then_inc(act_step, 1)
            act.wait_ge(sq_added, 9 * (SUMS.index("attn0") + 1))
            nc.scalar.activation(sq[:, 0, :], of("ckv")[:, :], ACT.Square, scale=math.sqrt(D // RANK) if math.sqrt(D // RANK).is_integer() else 1.0).then_inc(evacuated[JOB["ckv"] % 2], 1)
            deviation("ckvsum", scale=float(D // RANK))
            move("kidx", kidx[:, :])
            for j in range(4):
                move(f"qidx{j}", qidx[:, j, :])
            move("widx", widx[:, :, :], of("widx")[:, 0:TT * IDX_HEADS].rearrange("p (a n) -> p a n", a=TT),
                 scale=IDX_HEADS ** -0.5 * IDX_DIM ** -0.5)
            move("dsa_k", dsa_k[:, :])
            move("dsa_v", dsa_v[:, :, :], of("dsa_v")[:, 0:TT * HD].rearrange("p (a n) -> p a n", a=TT))
            index_relu(1)
            act.wait_ge(roped, 6)
            nc.scalar.activation(k_dsa[0][:, :], dsa_k[:, :], ACT.Copy).then_inc(k_rounded, 1)
            for j in range(3):
                move(f"q0.{j}", q0[:, j, :], scale=SCALE)
            index_relu(2)
            for j in range(3, 6):
                move(f"q0.{j}", q0[:, j, :], scale=SCALE)
            index_relu(3)
            for j in range(6):
                act.wait_ge(roped, 7 + j)
                round_queries("dsa", j, q0[:, j, :])
            for j in range(2):
                move(f"qmem0.{j}", qmem0[:, j, :], scale=SCALE)
            attention_stream(act, STREAMS[0], attention_begin, pair_of_heads)
            for l in range(DEPTH):
                if l == 1:
                    wait_product(act, f"down0.{KT - 1}")
                    for c in range(2):
                        act.dma_start(cmp_w1[c][:, :, :], A["cmp_w1"][c]).then_inc(cmp_in, 16)
                        act.dma_start(cmp_pos[c][:, :], A["cmp_pos"][c]).then_inc(cmp_in, 16)
                    act.dma_start(cmp_w2k[:, :], A["cmp_w2k"]).then_inc(cmp_in, 16)
                    act.dma_start(cmp_w2v[:, :], A["cmp_w2v"]).then_inc(cmp_in, 16)
                    deviation("sum.attn1")
                    round_norm("attn1", h_hi)
                    for name in ("kc0", "kc1", "vc0", "vc1"):
                        split_ahead(CHUNK[name])
                    for g in range(2):
                        move(f"ks{g}", k_raw[:, g, :])
                    for g in range(2):
                        move(f"kw{g}", k_raw[:, 2 + g, :])
                    move("cmp_hk", cmp_hk[:, :], of("cmp_hk")[:, 0:2 * N_CMP], ACT.Gelu_apprx_tanh)
                    hidden = of("cmp_hv")[:, 0:2 * N_CMP].rearrange("p (g c) -> p g c", g=2)
                    move("cmp_hv", cmp_hv[:, :, :, 0:N_CMP], hidden.unsqueeze(2).to_broadcast([P, 2, TT, N_CMP]), ACT.Gelu_apprx_tanh)
                    move("cmp_k", k_cmp[:, :], of("cmp_k")[:, 0:2 * N_CMP])
                    product("cmp_v")
                    for a in range(TT):
                        rows = slice(32 * a, 32 * a + 32)
                        r = nc.scalar.activation(v_cmp[rows, :, a * HD:(a + 1) * HD],
                                                 of("cmp_v")[rows, 0:2 * HD].rearrange("p (g n) -> p g n", g=2), ACT.Copy)
                    r.then_inc(evacuated[JOB["cmp_v"] % 2], 1)
                    for n in range(4):
                        act.wait_ge(roped, 13 + n)
                        nc.scalar.activation(k_nsa[0][:, n, :], k_raw[:, n, :], ACT.Copy).then_inc(k_rounded, 1)

                    def round_rotated(j):
                        act.wait_ge(roped, 17 + j)
                        round_queries("nsa0", j, q1r[:, j % 2, :])

                    for j in range(6):
                        move(f"q1.{j}", q1[:, j, :], scale=SCALE)
                        if j >= 2:
                            round_rotated(j - 2)
                    move("vsw.a", v_nsa[:, 0:2, :], of("vsw.a")[:, :].rearrange("p (a n) -> p a n", a=2))
                    round_rotated(4)
                    move("vsw.b", v_nsa[:, 2:4, :], of("vsw.b")[:, :].rearrange("p (a n) -> p a n", a=2))
                    round_rotated(5)
                    move("gates", gates[:, :, :], of("gates")[:, 0:TT * 3 * TOK_HEADS].rearrange("p (a n) -> p a n", a=TT), ACT.Sigmoid)
                    for j in range(2):
                        move(f"qmem1.{j}", qmem1[:, j, :], scale=SCALE)
                    attention_stream(act, STREAMS[1], attention_begin, pair_of_heads)
                concat(f"cat{l}", l)
                for j in range(KT):
                    split_ahead(CHUNK[f"wo{l}.{j}"])
                    wait_evacuated(act, f"wo{l}.{j}")
                    square(j, f"ffn{l}", x[:, j, :])
                deviation(f"sum.ffn{l}")
                round_norm(f"ffn{l}", h_hi)
                up_gated(l)
                down(f"down{l}", 3, 4, "attn1" if l == 0 else "final", x)
            deviation("sum.final")
            for k in range(KT):
                act.wait_ge(x_normed, k + 1)
                square(k, "mixpre0", x[:, k, :])
            act.dma_start(w_gate[:, :], A["w_gate"]).then_inc(gla_in, 16)
            act.dma_start(gla_mask[:, :], A["gla_mask"]).then_inc(gla_in, 16)
            deviation("sum.mixpre0")
            round_norm("mixpre0", h_hi)
            move("glr", glr[:, :])
            for h in range(4):
                move(f"gk{h}", gk[:, h, :])
            for h in range(4):
                move(f"gq{h}", gq[:, h, :])
            for h in range(4):
                product(f"gz{h}")
                if h:
                    act.wait_ge(g_cummed, 2 * h)
                nc.scalar.activation(g_ab[:, :], of(f"gz{h}")[:, :], ACT.Abs, bias=col(f"gla_b{h}")).then_inc(g_absed, 1)
                act.wait_ge(g_absed, h + 1)
                nc.scalar.activation(g_ab[:, :], g_ab[:, :], ACT.Exp, scale=-1.0).then_inc(act_step, 1)
                act.wait_ge(act_step, 2 + h)
                nc.scalar.activation(g_ab[:, :], g_ab[:, :], ACT.Ln, bias=1.0).then_inc(g_logged, 1)
                name = f"gv{h}.a"
                move(name, gv[:, 0:2, 2 * h * P:(2 * h + 2) * P], of(name)[:, :].rearrange("p (a n) -> p a n", a=2))
                act.wait_ge(g_cummed, 2 * h + 2)
                act.wait_ge(g_gated, 3 * h)
                nc.scalar.activation(g_exp[:, :], g_cum[:, :], ACT.Exp, scale=1.0 / GATE_NORM).then_inc(g_exped, 1)
                nc.scalar.activation(g_inv, g_cum[:, :], ACT.Exp, scale=-1.0 / GATE_NORM).then_inc(g_exped, 1)
                act.wait_ge(g_diffed, h + 1)
                nc.scalar.activation(g_end, g_end, ACT.Exp, scale=1.0 / GATE_NORM).then_inc(g_exped, 1)
                name = f"gv{h}.b"
                move(name, gv[:, 2:4, 2 * h * P:(2 * h + 2) * P], of(name)[:, :].rearrange("p (a n) -> p a n", a=2))
            for j in range(KT):
                move(f"gg{j}", gsilu[:, j, :], func=ACT.Silu)
            for h in range(4):
                name = f"gket{h}"
                move(name, k_endT[:, :, :], of(name)[:, :].rearrange("p (a n) -> p a n", a=TT))
                for j in range(2):
                    name = f"go{h}.{j}"
                    product(name)
                    if h:
                        act.wait_ge(go_made, 2 * (h - 1) + j + 1)
                        wait_product(act, f"gosum{h - 1}")
                    nc.scalar.activation(g_o[:, j, :], of(name)[:, :], ACT.Copy).then_inc(act_step, 1)
                    nc.scalar.activation(sq[:, j, :], of(name)[:, :], ACT.Square).then_inc(evacuated[JOB[name] % 2], 1)
                deviation(f"gosum{h}", scale=float(KT // 2))
                for j in range(2):
                    act.wait_ge(go_made, 2 * h + j + 1)
                    nc.scalar.activation(h_hi[:, 2 * h + j, :], tmp[:, j, :], ACT.Copy).then_inc(go_rounded, 1)
            for l in range(DEPTH):
                if l == 1:
                    act.dma_start(sv_b[0:1, :], A["sv_b"]).then_inc(swa_in, 16)
                    deviation("sum.mixpre1")
                    round_norm("mixpre1", h_hi)
                    for g in range(2):
                        move(f"sk{g}", sk[:, g, :], func=ACT.Identity, bias=col(f"swa_bk{g}"))
                        wait_evacuated(act, f"sk{g}")
                        nc.scalar.activation(k_swa[0][:, g, :], sk[:, g, :], ACT.Copy).then_inc(k_rounded, 1)
                    move("sv", sv[:, :, :], of("sv")[:, :].rearrange("p (a n) -> p a n", a=TT))
                    for j in range(KT):
                        split_ahead(CHUNK[f"sq{j}"])
                        wait_evacuated(act, f"sq{j}")
                        round_queries("swa0", j, sq_q[:, j, :])
                    attention_stream(act, STREAMS[2], attention_begin, pair_of_heads)
                    concat("scat", 2)
                for j in range(KT):
                    split_ahead(CHUNK[f"mix{l}.{j}"])
                    wait_evacuated(act, f"mix{l}.{j}")
                    square(j, f"mixpost{l}", m[:, j, :])
                deviation(f"sum.mixpost{l}")
                for k in range(KT):
                    act.wait_ge(x_added, KT * 2 * l + k + 1)
                    square(k, f"mlppre{l}", x[:, k, :])
                deviation(f"sum.mlppre{l}")
                round_norm(f"mlppre{l}", h_hi)
                for half in range(2):
                    up_relu(l, half)
                    down(f"mdown{l}{half}", 2, 2, f"mlppost{l}" if half else None, m)
                deviation(f"sum.mlppost{l}")
                for k in range(KT):
                    act.wait_ge(x_added, KT * (2 * l + 1) + k + 1)
                    if l == 0:
                        square(k, "mixpre1", x[:, k, :])
                    else:
                        act.dma_start(A["out"][k], x[:, k, :]).then_inc(stored, 16)
            act.wait_ge(stored, 16 * KT)

        @block.vector
        def _(dve):
            steps = [0]

            def step(ins):
                steps[0] += 1
                ins.then_inc(dve_step, 1)
                dve.wait_ge(dve_step, steps[0])

            def zero_sum(name):
                nc.vector.memset(sqacc[:, :], 0.0).then_inc(sq_added, 1)

            def add_square(k, name, n=SEQ, per=0, i=0):
                b = SUMS.index(name)
                dve.wait_ge(sq_done, KT * b + k + 1 + per * i)
                dve.wait_ge(sq_added, 9 * b + k + 1 + per * i)
                nc.vector.tensor_tensor(sqacc[:, 0:n], sqacc[:, 0:n], sq[:, k % 2, 0:n], ALU.add).then_inc(sq_added, 1)

            def inverse(job, n=SEQ):
                a = n // P
                wait_evacuated(dve, job)
                step(nc.vector.reciprocal(inv_root[:, 0:a], root[:, 0:a]))
                nc.vector.scalar_tensor_tensor(diag[:, 0:n].rearrange("p (a n) -> p a n", a=a), ident[:, :].unsqueeze(1).to_broadcast([P, a, P]),
                                               float(D), inv_root[:, 0:a].unsqueeze(2).to_broadcast([P, a, P]), ALU.mult, ALU.mult).then_inc(diag_ready, 1)
                wait_product(dve, inverse_of(job))
                return of(inverse_of(job))[:, 0:n]

            def release(job):
                dve.sem_inc(evacuated[JOB[inverse_of(job)] % 2], 1)

            def norm(name, src, hi, lo, rstd, n=SEQ):
                b = NORMS.index(name)

                def whole(k):
                    if k >= 4:
                        dve.wait_ge(h_ready[k % 2], KT // 2 * b + k // 2 - 1)
                    nc.vector.scalar_tensor_tensor(norm_tile(k)[:, 0:n], src[:, k, :], col(name, k), rstd, ALU.mult, ALU.mult).then_inc(h_made, 1)

                if b:
                    for part in range(2):
                        dve.wait_ge(h_ready[part], KT // 2 * b)
                whole(0)
                whole(1)
                for k in range(0, KT, 2):
                    if k + 2 < KT:
                        whole(k + 2)
                    dve.wait_ge(h_rounded, KT * b + k + 1)
                    nc.vector.tensor_tensor(lo[:, k, :], norm_tile(k)[:, 0:n], hi[:, k, :].bitcast(F32), ALU.subtract).then_inc(h_ready[0], 1)
                    if k + 2 < KT:
                        whole(k + 3)
                dve.wait_ge(h_made, KT * (b + 1))

            def rope(name):
                raw, out, t = rope_tile(name)
                wait_evacuated(dve, name)
                if ROPES.index(name):
                    dve.wait_ge(roped, ROPES.index(name))
                nc.vector.tensor_tensor(t[:, 0, :], raw, rope_c[:, :], ALU.mult).then_inc(dve_step, 1)
                steps[0] += 1
                job = f"rope.{name}"
                wait_product(dve, job)
                nc.vector.tensor_tensor(t[:, 1, :], of(job)[:, :], rope_s[:, :], ALU.mult).then_inc(evacuated[JOB[job] % 2], 1)
                dve.wait_ge(dve_step, steps[0])
                wait_evacuated(dve, job)
                nc.vector.tensor_tensor(out, t[:, 0, :], t[:, 1, :], ALU.add).then_inc(roped, 1)

            def index_mask(qt):
                n = (qt + 1) * P
                if qt:
                    dve.wait_ge(dsa_masked, qt)
                    step(nc.vector.memset(score[:, 0:qt * P], 0.0))
                    nc.vector.tensor_copy(score[:, qt * P:n], masks[:, P:2 * P]).then_inc(idx_chain, 1)
                    dve.wait_ge(idx_chain, qt)
                    for h in range(IDX_HEADS):
                        c = (qt - 1) * IDX_HEADS + h
                        dve.wait_ge(idx_relu, c + 1)
                        if h:
                            dve.wait_ge(idx_added, c)
                        nc.vector.scalar_tensor_tensor(score[:, 0:n], relu_l[:, c % 2, 0:n], widx[:, qt, h:h + 1], score[:, 0:n],
                                                       ALU.mult, ALU.add).then_inc(idx_added, 1)
                    dve.wait_ge(idx_added, qt * IDX_HEADS)

            def index_top(qt):
                n = (qt + 1) * P
                if qt:
                    for _ in range(TOPK // 8):
                        step(nc.vector.max(top8[:, :], score[:, 0:n]))
                        step(nc.vector.match_replace(score[:, 0:n], top8[:, :], score[:, 0:n], -3e38))
                    nc.vector.tensor_scalar(dsa_mask[:, qt, 0:n], score[:, 0:n], -2e38, NEG, ALU.is_gt, ALU.mult).then_inc(dsa_masked, 1)
                else:
                    nc.vector.tensor_copy(dsa_mask[:, 0, 0:P], masks[:, P:2 * P]).then_inc(dsa_masked, 1)

            def rest_of_queries(kind, j, tile):
                dve.wait_ge(q_rounded, 2 * (split_queries(kind)[2] + j) + 2)
                for part, hi, lo in both_heads(kind, j, tile):
                    nc.vector.tensor_tensor(lo, part, hi.bitcast(F32), ALU.subtract).then_inc(q_split, 1)

            def rest_of_keys(n, raw, hi, lo):
                dve.wait_ge(k_rounded, n + 1)
                nc.vector.tensor_tensor(lo, raw, hi.bitcast(F32), ALU.subtract).then_inc(k_split, 1)

            def maximum(kind, pair, u, i):
                _, qt, br = attention_unit(kind, u)
                per, group = PER_PAIR[kind], int(kind[3]) if kind[3:] else 0
                g, s4 = UNIT0[kind] + pair * per + u, slot_of(kind, u)
                dve.wait_ge(scores_ready, g + 1 + per * i)
                if compressed(kind, u):
                    src = score_bank[bank_of(kind, u)][:, 0:P].rearrange("p (a c) -> p a c", a=TT)
                    r0 = 2 * (6 * group + u // 9)
                    nc.vector.tensor_reduce(c_max[:, :, 0], src, AX.X, ALU.max).then_inc(rawmax_ready, 1)
                    dve.wait_ge(rawmax_ready, r0 + 1 + 4 * i)
                    nc.vector.tensor_scalar(c_max[:, :, 0], c_max[:, :, 0], NEG / 10, None, ALU.max).then_inc(rawmax_ready, 1)
                    dve.wait_ge(rawmax_ready, r0 + 2 + 4 * i)
                    nc.vector.tensor_tensor(c_shift[:, :, :], src, c_max[:, :, :].to_broadcast([P, TT, 32]), ALU.subtract).then_inc(max_ready, 1)
                    return
                src = score_bank[bank_of(kind, u)][:, 0:P * len(key_tiles(kind, qt, br))]
                if kind.startswith("swa"):
                    r0 = 24 + g - UNIT0["swa0"]
                    nc.vector.tensor_reduce(rawmax[:, s4:s4 + 1], src, AX.X, ALU.max, negate=True).then_inc(rawmax_ready, 1)
                    dve.wait_ge(rawmax_ready, r0 + 1 + per * i)
                    head = 8 * group + u // 4 + 2 * i
                    nc.vector.tensor_tensor(nmax[:, s4:s4 + 1], rawmax[:, s4:s4 + 1], nsinks[:, bass.ds(head, 1)], ALU.min).then_inc(max_ready, 1)
                else:
                    nc.vector.tensor_reduce(nmax[:, s4:s4 + 1], src, AX.X, ALU.max, negate=True).then_inc(max_ready, 1)

            def move_transposed(kind, pair, u, i):
                _, qt, br = attention_unit(kind, u)
                per = PER_PAIR[kind]
                g, n = UNIT0[kind] + pair * per + u, P if compressed(kind, u) else P * len(key_tiles(kind, qt, br))
                dve.wait_ge(transposed, g + 3 + per * i)
                dve.wait_ge(pv_done, g + 1 + per * i)
                nc.vector.tensor_copy(probT[:, g % 2, 0:n], probT_bank[g % 2][:, 0:n]).then_inc(probT_ready[g % 2], 1)

            def output(kind, pair, u, i):
                hh, qt, br = attention_unit(kind, u)
                per, o_tok, group = PER_PAIR[kind], output_of(kind), int(kind[3]) if kind[3:] else 0
                g, s4 = UNIT0[kind] + pair * per + u, slot_of(kind, u)
                nsa, swa = kind.startswith("nsa"), kind.startswith("swa")
                out = o_bank[g % 2]
                if kind.startswith("mem"):
                    c = (TOK_HEADS + 2 * pair + hh) * HD
                    of_head = slice(c, c + HD)
                else:
                    of_head = bass.ds(((6 if nsa else 8) * group + hh) * HD + P * i, HD)
                gate = bass.ds((6 * group + hh) * 3 + br + 6 * i, 1)
                if compressed(kind, u):
                    r0 = 6 * group + u // 9
                    dve.wait_ge(pv_done, g + 3 + per * i)
                    nc.vector.tensor_scalar(c_scale[:, :, 0], out[:, TT * HD:TT * HD + TT], 1e-30, None, ALU.max).then_inc(sum_ready, 1)
                    dve.wait_ge(sum_ready, r0 + 1 + 2 * i)
                    nc.vector.reciprocal(c_scale[:, :, 0], c_scale[:, :, 0]).then_inc(rinv_ready, 1)
                    dve.wait_ge(rinv_ready, g + 1 + per * i)
                    nc.vector.tensor_tensor(c_scale[:, :, :], c_scale[:, :, :], gates[:, :, gate], ALU.mult).then_inc(oscale_ready, 1)
                    dve.wait_ge(oscale_ready, g - UNIT0["nsa0"] + 1 + per * i)
                    nc.vector.tensor_tensor(o_tok[:, :, of_head], out[:, 0:TT * HD].rearrange("p (a n) -> p a n", a=TT),
                                            c_scale[:, :, :].to_broadcast([P, TT, HD]), ALU.mult).then_inc(o_done, 1)
                    return
                den = psum_p[:, s4:s4 + 1]
                dve.wait_ge(probs_ready, g + 3 + per * i)
                if swa:
                    r0 = g - UNIT0["swa0"]
                    dve.wait_ge(sink_ready, r0 + 1 + per * i)
                    nc.vector.tensor_tensor(oscale[:, s4:s4 + 1], den, sinkexp[:, s4:s4 + 1], ALU.add).then_inc(sum_ready, 1)
                    den = oscale[:, s4:s4 + 1]
                    dve.wait_ge(sum_ready, 12 + r0 + 1 + per * i)
                nc.vector.reciprocal(rinv[:, s4:s4 + 1], den).then_inc(rinv_ready, 1)
                dve.wait_ge(rinv_ready, g + 1 + per * i)
                factor = rinv[:, s4:s4 + 1]
                if nsa:
                    nc.vector.tensor_tensor(oscale[:, s4:s4 + 1], factor, gates[:, qt, gate], ALU.mult).then_inc(oscale_ready, 1)
                    dve.wait_ge(oscale_ready, g - UNIT0["nsa0"] + 1 + per * i)
                    factor = oscale[:, s4:s4 + 1]
                dve.wait_ge(pv_done, g + 3 + per * i)
                if nsa:
                    dve.wait_ge(o_done, g + 2 + per * i)
                    nc.vector.scalar_tensor_tensor(o_tok[:, qt, of_head], out[:, 0:HD], factor, o_tok[:, qt, of_head], ALU.mult, ALU.add).then_inc(o_done, 1)
                else:
                    nc.vector.tensor_scalar(o_tok[:, qt, of_head], out[:, 0:HD], factor, None, ALU.mult).then_inc(o_done, 1)

            def attention_begin(at):
                for u in range(4):
                    maximum(*at(u))
                move_transposed(*at(1))

            def pair_of_heads(per, at):
                for u in range(per):
                    if at(u + 4):
                        maximum(*at(u + 4))
                    if u % 2 and at(u + 2):
                        move_transposed(*at(u + 2))
                    output(*at(u))

            def concat(prefix, n):
                for j in range(KT):
                    name = f"{prefix}.{j}"
                    dve.wait_ge(cat_rounded, KT * n + j + 1)
                    nc.vector.tensor_tensor(h_lo[:, j, :], of(name)[:, :], h_hi[:, j, :].bitcast(F32), ALU.subtract).then_inc(evacuated[JOB[name] % 2], 1)

            def up_gated(l):
                n0, t0 = JOB[f"up{l}.0"], CHUNK[f"up{l}.0"]
                with dve.Fori(0, FT // 2) as i:
                    for f in range(2):
                        c = FT * l + f
                        b = n0 + 2 * f + 1
                        dve.wait_ge(chunks_used, t0 + 2 * f + 2 + 4 * i)
                        dve.wait_ge(evacuated[(b - 1) % 2], (b - 1) // 2 + 1 + 2 * i)
                        nc.vector.tensor_tensor(tmp[:, f, :], sq[:, f, :], bank[b % 2][:, :], ALU.mult).then_inc(act_made, 1)
                        dve.wait_ge(act_made, c + 1 + 2 * i)
                        dve.sem_inc(evacuated[b % 2], 1)
                        dve.wait_ge(act_rounded, c + 1 + 2 * i)
                        j = bass.ds(2 * i + f, 1)
                        nc.vector.tensor_tensor(act_lo[:, j, :].rearrange("p a n -> p (a n)"), tmp[:, f, :],
                                                act_hi[:, j, :].rearrange("p a n -> p (a n)").bitcast(F32), ALU.subtract).then_inc(act_ready, 1)

            def up_relu(l, half):
                n0, t0 = JOB[f"mup{l}{half}.0"], CHUNK[f"mup{l}{half}.0"]
                c0, r0 = 2 * FT + HALF_FT * (2 * l + half), HALF_FT * (2 * l + half)
                with dve.Fori(0, HALF_FT // 4) as i:
                    for f in range(4):
                        b = n0 + f
                        dve.wait_ge(relu_done, r0 + f + 1 + 4 * i)
                        nc.vector.tensor_tensor(tmp[:, f % 2, :], sq[:, f % 2, :], bank[b % 2][:, :], ALU.mult).then_inc(act_made, 1)
                        dve.wait_ge(act_made, c0 + f + 1 + 4 * i)
                        dve.sem_inc(evacuated[b % 2], 1)
                        dve.wait_ge(act_rounded, c0 + f + 1 + 4 * i)
                        j = bass.ds(4 * i + f, 1)
                        nc.vector.tensor_tensor(mact_lo[:, j, :].rearrange("p a n -> p (a n)"), tmp[:, f % 2, :],
                                                mact_hi[:, j, :].rearrange("p a n -> p (a n)").bitcast(F32), ALU.subtract).then_inc(act_ready, 1)

            def down(prefix, per_tile, step_, name, dst, add):
                n0, t0 = JOB[f"{prefix}.0"], CHUNK[f"{prefix}.0"]
                if name:
                    zero_sum(name)
                with dve.Fori(0, KT // step_) as i:
                    for j in range(step_):
                        b = bank[(n0 + j) % 2][:, :]
                        d = dst[:, bass.ds(step_ * i + j, 1), :].rearrange("p a n -> p (a n)")
                        dve.wait_ge(chunks_used, t0 + (j + 1) * per_tile + step_ * per_tile * i)
                        ins = nc.vector.tensor_tensor(d, d, b, ALU.add) if add else nc.vector.tensor_copy(d, b)
                        ins.then_inc(evacuated[(n0 + j) % 2], 1)
                        if name:
                            add_square(j, name, per=step_, i=i)

            dve.sem_inc(o_done, 2)
            dve.sem_inc(probT_ready[1], 1)
            nc.vector.memset(ones[:, :], 1.0 / D)
            nc.vector.memset(eps[:, :], EPS)
            dve.wait_ge(consts_in, 144)
            nc.vector.tensor_copy(ident_b[:, :], ident[:, :])
            nc.vector.tensor_copy(masks_b[:, :], masks[:, :])
            nc.vector.tensor_scalar(nsinks[:, :], sinks[:, :], -1.0, None, ALU.mult).then_inc(consts_made, 1)
            zero_sum("mem")
            for k in range(KT):
                add_square(k, "mem", N_MEM)
            rstd = inverse("memsum", N_MEM)
            for l in range(DEPTH):
                norm(f"mem{l}", memx, mem_hi[l], mem_lo[l], rstd, N_MEM)
            release("memsum")
            zero_sum("attn0")
            for k in range(KT):
                add_square(k, "attn0")
            norm("attn0", x, h_hi, h_lo, inverse("sum.attn0"))
            release("sum.attn0")
            rstd = inverse("ckvsum")
            nc.vector.scalar_tensor_tensor(ckv_n[:, :], ckv[:, :], col("ckv"), rstd, ALU.mult, ALU.mult).then_inc(ckv_normed, 1)
            dve.wait_ge(ckv_normed, 1)
            release("ckvsum")
            index_top(0)
            for name in ROPES[0:6]:
                rope(name)
            wait_evacuated(dve, "widx")
            index_mask(1)
            index_top(1)
            rest_of_keys(0, dsa_k[:, :], k_dsa[0][:, :], k_dsa[1][:, :])
            index_mask(2)
            index_top(2)
            index_mask(3)
            for j in range(6):
                rope(f"q0.{j}")
                if j:
                    rest_of_queries("dsa", j - 1, q0[:, j - 1, :])
            rest_of_queries("dsa", 5, q0[:, 5, :])
            index_top(3)
            dve.wait_ge(roped, 12)
            attention_stream(dve, STREAMS[0], attention_begin, pair_of_heads)
            for l in range(DEPTH):
                if l == 1:
                    norm("attn1", x, h_hi, h_lo, inverse("sum.attn1"))
                    release("sum.attn1")
                    nc.vector.memset(cmp_hv[:, :, :, N_CMP:32], 0.0)
                    step(nc.vector.memset(v_cmp[:, :, :], 0.0))
                    for a in range(TT):
                        nc.vector.memset(v_cmp[32 * a:32 * a + 32, :, TT * HD + a:TT * HD + a + 1], 1.0)
                    dve.wait_ge(cmp_in, 96)
                    for c, s_ in enumerate("kv"):
                        for g in range(2):
                            name = f"{s_}c{g}"
                            wait_product(dve, name)
                            src = of(name)
                            for half in range(2):
                                rows = slice(HD * half, HD * half + HD)
                                tok = src[rows, half:half + 16 * (N_CMP - 1) + 2 * (CMP_PAIRS - 1) + 1]
                                out = cmp_x[c][rows, :, g, :]
                                pos = cmp_pos[c][rows, :].unsqueeze(2).to_broadcast([HD, CMP_PAIRS, N_CMP])
                                win = bass.AP(tok.tensor, tok.offset, [tok.ap[0], [2, CMP_PAIRS], [16, N_CMP]])
                                ins = nc.vector.tensor_tensor(out, win, pos, ALU.add)
                                ins.then_inc(cmp_built, 1)
                            dve.wait_ge(cmp_built, 4 * c + 2 * g + 2)
                            dve.sem_inc(evacuated[JOB[name] % 2], 1)
                    for name in ROPES[12:16]:
                        rope(name)
                    for n in range(4):
                        rest_of_keys(1 + n, k_raw[:, n, :], k_nsa[0][:, n, :], k_nsa[1][:, n, :])
                    for j in range(6):
                        rope(f"q1.{j}")
                        if j:
                            rest_of_queries("nsa0", j - 1, q1r[:, (j - 1) % 2, :])
                    rest_of_queries("nsa0", 5, q1r[:, 5 % 2, :])
                    wait_evacuated(dve, "gates")
                    dve.wait_ge(roped, len(ROPES))
                    attention_stream(dve, STREAMS[1], attention_begin, pair_of_heads)
                concat(f"cat{l}", l)
                zero_sum(f"ffn{l}")
                for j in range(KT):
                    name = f"wo{l}.{j}"
                    wait_product(dve, name)
                    nc.vector.tensor_tensor(x[:, j, :], x[:, j, :], of(name)[:, :], ALU.add).then_inc(evacuated[JOB[name] % 2], 1)
                    add_square(j, f"ffn{l}")
                norm(f"ffn{l}", x, h_hi, h_lo, inverse(f"sum.ffn{l}"))
                release(f"sum.ffn{l}")
                up_gated(l)
                down(f"down{l}", 3, 4, "attn1" if l == 0 else "final", x, True)
            rstd = inverse("sum.final")
            for k in range(KT):
                nc.vector.scalar_tensor_tensor(x[:, k, :], x[:, k, :], col("final", k), rstd, ALU.mult, ALU.mult).then_inc(x_normed, 1)
            dve.wait_ge(x_normed, KT)
            release("sum.final")
            norm("mixpre0", x, h_hi, h_lo, inverse("sum.mixpre0"))
            release("sum.mixpre0")
            nc.vector.memset(attT[:, :, :], 0.0)
            step(nc.vector.memset(g_reset[:, :], 1.0))
            step(nc.vector.memset(g_reset[:, :].rearrange("p (n c) -> p n c", c=GLA_CHUNK)[:, :, 0:1], 0.0))
            for h in range(4):
                name = f"gz{h}"
                dve.wait_ge(g_absed, h + 1)
                nc.vector.tensor_scalar(g_la[:, :], of(name)[:, :], col(f"gla_b{h}"), 0.0, ALU.add, ALU.min).then_inc(evacuated[JOB[name] % 2], 1)
                wait_evacuated(dve, name)
                dve.wait_ge(g_logged, h + 1)
                nc.vector.tensor_tensor(g_la[:, :], g_la[:, :], g_ab[:, :], ALU.subtract).then_inc(g_cummed, 1)
                dve.wait_ge(g_cummed, 2 * h + 1)
                nc.vector.tensor_tensor_scan(g_cum[:, :], g_reset[:, :], g_la[:, :], 0.0, ALU.mult, ALU.add).then_inc(g_cummed, 1)
                dve.wait_ge(g_cummed, 2 * h + 2)
                cum = g_cum[:, :].rearrange("p (n c) -> p n c", c=GLA_CHUNK)
                last = cum[:, :, GLA_CHUNK - 1:GLA_CHUNK].to_broadcast([P, N_CHUNK, GLA_CHUNK])
                nc.vector.tensor_tensor(g_end.rearrange("p (n c) -> p n c", c=GLA_CHUNK), last, cum, ALU.subtract).then_inc(g_diffed, 1)
                dve.wait_ge(g_exped, 3 * h + 2)
                wait_evacuated(dve, f"gq{h}")
                nc.vector.tensor_copy(decay[:, h, :], g_exp[:, :].rearrange("p (n c) -> p n c", c=GLA_CHUNK)[:, :, GLA_CHUNK - 1])
                nc.vector.scalar_tensor_tensor(gq[:, h, :], gq[:, h, :], float(P) ** -0.5, g_exp[:, :], ALU.mult, ALU.mult).then_inc(g_gated, 1)
                nc.vector.tensor_tensor(k_inv[:, h, :], gk[:, h, :], g_inv, ALU.mult).then_inc(g_gated, 1)
                dve.wait_ge(g_exped, 3 * h + 3)
                nc.vector.tensor_tensor(gk[:, h, :], gk[:, h, :], g_end, ALU.mult).then_inc(g_gated, 1)
            dve.wait_ge(g_gated, 12)
            dve.wait_ge(gla_in, 32)
            for h in range(4):
                name = f"gatt{h}"
                wait_product(dve, name)
                nc.vector.copy_predicated(attT[:, :, :], gla_mask[:, :].unsqueeze(1).to_broadcast([P, TT, P]),
                                          of(name)[:, :].rearrange("p (a n) -> p a n", a=TT)).then_inc(evacuated[JOB[name] % 2], 1)
                for n in range(N_CHUNK - 1):
                    name = f"gds{h}.{n}"
                    wait_product(dve, name)
                    src = of(name)[:, 0:2 * P]
                    if n:
                        wait_evacuated(dve, f"gds{h}.{n - 1}")
                        ins = nc.vector.scalar_tensor_tensor(state[:, n + 1, :], state[:, n, :], decay[:, h, n:n + 1], src, ALU.mult, ALU.add)
                    else:
                        ins = nc.vector.tensor_copy(state[:, 1, :], src)
                    ins.then_inc(evacuated[JOB[name] % 2], 1)
                rstd = inverse(f"gosum{h}")
                for j in range(2):
                    step(nc.vector.scalar_tensor_tensor(tmp[:, j, :], g_o[:, j, :], col(f"gla_n{j}"), rstd, ALU.mult, ALU.mult))
                    if j:
                        release(f"gosum{h}")
                    wait_evacuated(dve, f"gg{2 * h + j}")
                    nc.vector.tensor_tensor(tmp[:, j, :], tmp[:, j, :], gsilu[:, 2 * h + j, :], ALU.mult).then_inc(go_made, 1)
                for j in range(2):
                    k = 2 * h + j
                    dve.wait_ge(go_rounded, k + 1)
                    nc.vector.tensor_tensor(h_lo[:, k, :], tmp[:, j, :], h_hi[:, k, :].bitcast(F32), ALU.subtract).then_inc(go_split, 1)
            for l in range(DEPTH):
                if l == 1:
                    rstd = inverse("sum.mixpre1")
                    nc.vector.memset(one_row[:, :], 1.0)
                    norm("mixpre1", x, h_hi, h_lo, rstd)
                    release("sum.mixpre1")
                    for j in range(KT):
                        name = f"sq{j}"
                        wait_product(dve, name)
                        nc.vector.tensor_scalar(sq_q[:, j, :], of(name)[:, :], col("swa_b_q", j), SCALE, ALU.add, ALU.mult).then_inc(evacuated[JOB[name] % 2], 1)
                        if j < 2:
                            rest_of_keys(5 + j, sk[:, j, :], k_swa[0][:, j, :], k_swa[1][:, j, :])
                        else:
                            rest_of_queries("swa0", j - 2, sq_q[:, j - 2, :])
                    for j in (KT - 2, KT - 1):
                        rest_of_queries("swa0", j, sq_q[:, j, :])
                    attention_stream(dve, STREAMS[2], attention_begin, pair_of_heads)
                    concat("scat", 2)
                zero_sum(f"mixpost{l}")
                for j in range(KT):
                    name = f"mix{l}.{j}"
                    wait_product(dve, name)
                    if l == 0:
                        ins = nc.vector.tensor_copy(m[:, j, :], of(name)[:, :])
                    else:
                        ins = nc.vector.tensor_scalar(m[:, j, :], of(name)[:, :], col("swa_b_out", j), None, ALU.add)
                    ins.then_inc(evacuated[JOB[name] % 2], 1)
                    add_square(j, f"mixpost{l}")

                def add_normed(name):
                    rstd = inverse(f"sum.{name}")
                    first = steps[0]

                    def scaled(k):
                        steps[0] += 1
                        nc.vector.scalar_tensor_tensor(tmp[:, k % 2, :], m[:, k, :], col(name, k), rstd, ALU.mult, ALU.mult).then_inc(dve_step, 1)

                    scaled(0)
                    for k in range(KT):
                        if k + 1 < KT:
                            if k:
                                dve.wait_ge(x_added, KT * SUMMED.index(name) + k)
                            scaled(k + 1)
                        dve.wait_ge(dve_step, first + k + 1)
                        nc.vector.tensor_tensor(x[:, k, :], x[:, k, :], tmp[:, k % 2, :], ALU.add).then_inc(x_added, 1)
                    release(f"sum.{name}")

                add_normed(f"mixpost{l}")
                norm(f"mlppre{l}", x, h_hi, h_lo, inverse(f"sum.mlppre{l}"))
                release(f"sum.mlppre{l}")
                for half in range(2):
                    up_relu(l, half)
                    down(f"mdown{l}{half}", 2, 2, f"mlppost{l}" if half else None, m, half == 1)
                add_normed(f"mlppost{l}")


def by_columns(w):
    k, n = w.shape
    pad = -n % P
    if pad:
        w = np.concatenate([w, np.zeros((k, pad), w.dtype)], 1)
    n = (n + pad) // P
    return w.reshape(k // P, P, n, P).transpose(2, 1, 0, 3).reshape(n, P, k)


def by_rows_of(w, per_tile):
    f, n = w.shape
    pad = per_tile * D - f
    if pad:
        w = np.concatenate([w, np.zeros((pad, n), w.dtype)], 0)
    return w.reshape(per_tile, KT, P, n // P, P).transpose(3, 0, 2, 1, 4).reshape(-1, P, D)


def interleave(a, b):
    return np.stack([a, b], 1).reshape(-1, *a.shape[1:])


def twice(w):
    return np.concatenate([w, w], 1)


def weight_stream(v):
    out = []
    for l in range(DEPTH):
        out.append(by_columns(v["mem_w_kv"][l]))
    w = v["dsa_w_in"][0]
    q, ckv, k_rope, q_idx, k_idx, w_idx, q_mem = np.split(w, np.cumsum([768, 128, 16, 512, 64, 8]).tolist(), 1)
    gap = np.zeros((D, HD - ROPE), w.dtype)
    out += [by_columns(a) for a in (ckv, twice(k_idx), q_idx, w_idx, twice(np.concatenate([k_rope, gap], 1)), q, q_mem)]
    for l in range(DEPTH):
        if l == 1:
            w = v["nsa_w_in"][0]
            q, kc, vc, ks, vs, kw, vw, gates, q_mem = np.split(w, np.cumsum([768] + [128] * 6 + [36]).tolist(), 1)
            for a in (kc, vc, ks, kw):
                out += [by_columns(twice(a[:, 0:HD])), by_columns(twice(a[:, HD:]))]
            out += [by_columns(a) for a in (q, vs, vw, gates, q_mem)]
        out.append(by_columns(v["w_o"][l]))
        gate, upw = np.split(v["ffn_w_in"][l], 2, 1)
        out.append(interleave(by_columns(gate), by_columns(upw)))
        out.append(by_rows_of(v["ffn_w_down"][l], 3))
    w = v["gla_w_in_2"][0]
    q, k, vv, g, glr = np.split(w, np.cumsum([512, 512, 1024, 1024]).tolist(), 1)
    out += [by_columns(a) for a in (glr, k, q, vv, g)]
    for l in range(DEPTH):
        if l == 1:
            w = v["swa_w_in_2"][0]
            q, k, vv = np.split(w, [1024, 1152], 1)
            out += [by_columns(twice(k[:, 0:HD])), by_columns(twice(k[:, HD:])), by_columns(vv), by_columns(q)]
        out.append(by_columns(v["gla_w_out_2"][0] if l == 0 else v["swa_w_out_2"][0]))
        upw, downw = v["mlp_w_up_2"][l], v["mlp_w_down_2"][l]
        for half in range(2):
            f = slice(half * D_FF2 // 2, (half + 1) * D_FF2 // 2)
            out += [by_columns(upw[:, f]), by_rows_of(downw[f], 2)]
    return np.concatenate(out, 0)


def shape_constants():
    inv = 500000.0 ** (-np.arange(0, ROPE, 2, dtype=np.float64) / ROPE)
    ang = np.arange(SEQ, dtype=np.float64)[:, None] * inv[None, :]
    cos, sin = np.cos(ang).astype(np.float32).T, np.sin(ang).astype(np.float32).T
    c, s, perm = np.ones((P, SEQ), np.float32), np.zeros((P, SEQ), np.float32), np.zeros((P, P), np.float32)
    half = ROPE // 2
    for o in (0, HD):
        for d in range(half):
            c[o + d] = c[o + half + d] = cos[d]
            s[o + d] = s[o + half + d] = sin[d]
            perm[o + half + d, o + d] = -1.0
            perm[o + d, o + half + d] = 1.0
    a = np.arange(P)
    prev = np.where(a[None, :] > a[:, None], 0.0, NEG)
    own = np.where(a[None, :] <= a[:, None], 0.0, NEG)
    blocks = np.arange(32)
    cmp_ = [np.where((blocks * 16 + 31)[None, :] <= (t * P + a)[:, None], 0.0, NEG) for t in range(TT)]
    masks = np.concatenate([prev, own] + cmp_, 1).astype(np.float32)
    same = (a[:, None] // GLA_CHUNK == a[None, :] // GLA_CHUNK) & (a[:, None] <= a[None, :])
    return {"ident": np.eye(P, dtype=np.float32), "perm": perm, "rope_c": c, "rope_s": s, "masks": masks, "gla_mask": same.astype(np.int32)}


def lay_out(v):
    f = {n: np.asarray(a) for n, a in v.items()}
    vec = {"final": f["final_norm"], "swa_b_out": f["swa_b_out_2"][0], "swa_b_q": f["swa_b_in_2"][0][0:D]}
    for l in range(DEPTH):
        for name, src in (("attn", "attn_norm"), ("ffn", "ffn_norm"), ("mem", "mem_norm"), ("mixpre", "ln_mix_pre_2"),
                          ("mixpost", "ln_mix_post_2"), ("mlppre", "ln_mlp_pre_2"), ("mlppost", "ln_mlp_post_2")):
            vec[f"{name}{l}"] = f[src][l]
    bk = f["swa_b_in_2"][0][D:D + 2 * HD].reshape(2, HD)
    columns = [vec[n].reshape(KT, P).T for n in GAINS] + [f["dsa_ckv_norm"][0][:, None], f["gla_b_gate_up_2"][0].reshape(4, P).T,
               f["gla_g_norm_2"][0].reshape(2, P).T] + [np.concatenate([b, b])[:, None] for b in bk]
    gap = np.zeros((P, ROPE), np.float32)
    uk = f["dsa_w_uk"][0]
    pairs = lambda a: a.reshape(CMP_PAIRS, P, -1).transpose(1, 0, 2)
    out = {
        "weights": weight_stream(f),
        "memT": f["mem"][0].T.reshape(KT, P, N_MEM).transpose(1, 0, 2),
        "xT": f["x"][0].T.reshape(KT, P, SEQ).transpose(1, 0, 2),
        "cols": np.concatenate(columns, 1),
        "w_uk": np.concatenate([gap, uk, gap, uk], 1),
        "w_uv": f["dsa_w_uv"][0],
        "sinks": np.broadcast_to(f["swa_sinks_2"][0][None, :], (P, 16)),
        "cmp_w1": np.stack([pairs(f["nsa_cmp_k_w1"][0]), pairs(f["nsa_cmp_v_w1"][0])]),
        "cmp_pos": np.stack([f[f"nsa_cmp_pos_{c}"][0].reshape(CMP_PAIRS, P).T for c in "kv"]),
        "cmp_w2k": twice(f["nsa_cmp_k_w2"][0]),
        "cmp_w2v": f["nsa_cmp_v_w2"][0],
        "w_gate": f["gla_w_gate_up_2"][0],
        "sv_b": f["swa_b_in_2"][0][None, D + 2 * HD:],
    }
    out.update(shape_constants())
    return {"in_" + n: np.ascontiguousarray(a) for n, a in out.items()}


def build(nc, arrays):
    A = {n[3:]: nc.dram_tensor(n, a.shape, mybir.dt.from_np(a.dtype), kind="ExternalInput").ap() for n, a in arrays.items()}
    A["out"] = nc.dram_tensor("out", (KT, P, SEQ), F32, kind="ExternalOutput").ap()
    program(nc, A)


def kernel(**inputs):
    import concourse.bacc as bacc
    from concourse.bass_utils import run_bass_kernel_spmd

    arrays = lay_out(inputs)
    nc = bacc.Bacc("TRN2", target_bir_lowering=False, num_devices=1)
    build(nc, arrays)
    r = run_bass_kernel_spmd(nc, [arrays], core_ids=[0])
    return np.ascontiguousarray(r.results[0]["out"].reshape(D, SEQ).T)[None]
```

```python
from contextlib import ExitStack

import numpy as np

import concourse.bass as bass
from concourse import mybir

F32 = mybir.dt.float32
F32R = mybir.dt.float32r
BF16 = mybir.dt.bfloat16
I32 = mybir.dt.int32
ALU = mybir.AluOpType
ACT = mybir.ActivationFunctionType
AX = mybir.AxisListType

P = 128
SEQ, D, N_MEM, DEPTH = 512, 1024, 256, 2
KT = D // P
TT = SEQ // P
HD, ROPE = 64, 16
TOK_HEADS, MEM_HEADS = 12, 4
RANK, IDX_HEADS, IDX_DIM, TOPK = 128, 8, 64, 128
D_FF, D_FF2 = 2816, 4096
FT = D_FF // P
HALF_FT = D_FF2 // P // 2
N_CMP = (SEQ - 32) // 16 + 1
CMP_PAIRS = 16
GLA_HEADS, GLA_CHUNK = 4, 64
N_CHUNK = SEQ // GLA_CHUNK
GATE_NORM = 16.0
SWA_PAIRS = 8
EPS = 1e-6
NEG = -1e30
SCALE = HD ** -0.5
RING = 4
RAW = 2
AHEAD = RING - 1

GAINS = ["attn0", "attn1", "ffn0", "ffn1", "final", "mem0", "mem1", "mixpre0", "mixpre1", "mixpost0",
         "mixpost1", "mlppre0", "mlppre1", "mlppost0", "mlppost1", "swa_b_out", "swa_b_q"]
EXTRA = ["ckv", "gla_b0", "gla_b1", "gla_b2", "gla_b3", "gla_n0", "gla_n1", "swa_bk0", "swa_bk1", "swa_bv"]
N_COLS = len(GAINS) * KT + len(EXTRA)


GLA_STAGES = [("gate", 0), ("gate", 1), ("scores", 0), ("gate", 2), ("scores", 1), ("gate", 3), ("outputs", 0), ("gate", 4), ("scores", 2), ("sum", 0),
              ("outputs", 1), ("gate", 5), ("norm", 0), ("scores", 3), ("sum", 1), ("outputs", 2), ("gate", 6), ("norm", 1), ("sum", 2),
              ("outputs", 3), ("gate", 7), ("norm", 2), ("split", 0), ("sum", 3), ("split", 1), ("norm", 3), ("split", 2), ("split", 3)]


def inverse_of(job):
    return job.replace("sum", "inv")


def plan():
    jobs = [("sum.attn0", 0), ("ckv", 1), ("kidx", 1), ("ckvsum", 0), ("qidx0", 1), ("ckvinv", 0), ("rope.kidx", 0),
            ("qidx1", 1), ("memsum", 0), ("rope.qidx0", 0), ("qidx2", 1), ("meminv", 0), ("rope.qidx1", 0), ("qidx3", 1), ("rope.qidx2", 0)]
    jobs += [("widx", 1), ("rope.qidx3", 0), ("dsa_k", 1), ("widxT", 0), ("dsa_v", 0), ("rope.dsa_k", 0)]
    jobs += [(f"q0.{j}", 1) for j in range(6)]
    jobs += [(f"mk0.{j}", 1) for j in range(2)] + [("mv0", 2)]
    jobs += [(f"rope.q0.{j}", 0) for j in range(6)]
    jobs += [(f"qmem0.{j}", 1) for j in range(2)]
    jobs += [(f"mk1.{j}", 1) for j in range(2)] + [("mv1", 2)]
    for l in range(DEPTH):
        if l == 1:
            for s in ("kc", "vc"):
                jobs += [(f"{s}{g}", 1) for g in range(2)]
            jobs += [(f"ks{g}", 1) for g in range(2)] + [(f"kw{g}", 1) for g in range(2)]
            jobs += [("cmp_hk", 0), ("cmp_hv", 0)]
            jobs += [(f"rope.ks{g}", 0) for g in range(2)] + [(f"rope.kw{g}", 0) for g in range(2)]
            jobs += [("cmp_k", 0), ("cmp_v", 0)]
            jobs += [("q1.0", 1)]
            for j in range(1, 6):
                jobs += [(f"q1.{j}", 1), (f"rope.q1.{j - 1}", 0)]
            jobs += [("vsw.a", 0), ("vsw.b", 2), ("rope.q1.5", 0), ("gates", 1)]
            jobs += [("qmem1.0", 1), ("gatesT", 0), ("qmem1.1", 1)]
        jobs += [(f"cat{l}.{j}", 0) for j in range(KT)]
        jobs += [(f"wo{l}.{j}", 1) for j in range(KT)]
        jobs += [(f"sum.ffn{l}", 0)]
        jobs += [(f"up{l}.{j}", 1) for j in range(2 * FT)]
        jobs += [(f"down{l}.{j}", 3) for j in range(KT)]
        jobs += [("sum.attn1" if l == 0 else "sum.final", 0)]
    jobs += [("glr", 1), ("gk0", 1), ("inv.x", 0)]
    jobs += [(f"gk{h}", 1) for h in range(1, 4)] + [(f"gq{h}", 1) for h in range(4)]
    for h in range(4):
        jobs += [(f"gz{h}", 0), (f"gv{h}.a", 0), (f"gv{h}.b", 2)]
    for stage, h in GLA_STAGES:
        jobs += {"gate": [(f"gg{h}", 1)], "scores": [(f"gket{h}", 0), (f"gatt{h}", 0), (f"gds{h}", 0)],
                 "outputs": [(f"go{h}.{j}", 0) for j in range(2)], "sum": [(f"gosum{h}", 0)], "norm": [(f"goinv{h}", 0)], "split": []}[stage]
    for l in range(DEPTH):
        if l == 1:
            jobs += [(f"sq{j}", 1) for j in range(KT)] + [("sv", 1)] + [(f"sk{g}", 1) for g in range(2)] + [("svT", 0)]
            jobs += [(f"scat.{j}", 0) for j in range(KT)]
        jobs += [(f"mix{l}.{j}", 1) for j in range(KT)]
        jobs += [(f"sum.mixpost{l}", 0)]
        for half in range(2):
            jobs += [(f"mup{l}{half}.{j}", 1) for j in range(HALF_FT)]
            if half:
                jobs += [(f"sum.mlppre{l}", 0)]
            jobs += [(f"mdown{l}{half}.{j}", 2) for j in range(KT)]
        jobs += [(f"sum.mlppost{l}", 0)]
    return [j for job in jobs for j in ([job, (inverse_of(job[0]), 0)] if job[0].startswith("sum.") and
                                        "mlppre" not in job[0] else [job])]


JOBS = plan()
JOB, CHUNK, SMALL = {}, {}, {}
_chunks = _small = 0
for _n, (_name, _c) in enumerate(JOBS):
    JOB[_name], CHUNK[_name], SMALL[_name] = _n, _chunks, _small
    _chunks += _c
    _small += _c == 0
N_CHUNKS = _chunks

INVERSES = [name for name, _ in JOBS if "inv" in name]
INVERSES.insert(INVERSES.index("inv.mixpost1"), "inv.mixpre1")
GAINED = ["mlppre0", "mixpre1", "mlppre1"]
FOLLOWED = {"mixpost0": "mlppre0", "mlppost0": "mixpre1", "mixpost1": "mlppre1"}
ROOTED = ["final", "mlppost0", "mixpre1", "mlppost1"]
FIRST = {"attn0": "ckv", "mem0": "qidx3", "mem1": "widx", "ffn0": "up0.0", "attn1": "kc0", "ffn1": "up1.0", "mixpre0": "glr",
         "mlppre0": "mup00.0", "mixpre1": "sq0", "mlppre1": "mup10.0"}
SUMS = ["attn0", "mem", "ffn0", "attn1", "ffn1", "final", "mixpost0", "mlppre0", "mlppost0",
        "mixpre1", "mixpost1", "mlppre1", "mlppost1"]
SUMMED = ["mixpost0", "mlppost0", "mixpost1", "mlppost1"]
NORMS = ["attn0", "mem0", "mem1", "ffn0", "attn1", "ffn1", "mixpre0"]
UNITS = [("dsa", 48), ("mem0", 16), ("nsa0", 54), ("nsa1", 54), ("mem1", 16), ("swa0", 32), ("swa1", 32)]
UNIT0 = {n: sum(c for _, c in UNITS[:k]) for k, (n, _) in enumerate(UNITS)}
STAGED = {"dsa": 0, "mem0": 12, "nsa0": 16, "nsa1": 22, "mem1": 28, "swa0": 32, "swa1": 40}


PER_PAIR = {n: 18 if n.startswith("nsa") else 8 for n, _ in UNITS}
STREAMS = [[("dsa", 6, 0), ("mem0", 1, 0), ("mem0", 1, 1)],
           [("nsa0", 3, 0), ("nsa1", 3, 0), ("mem1", 1, 0), ("mem1", 1, 1)],
           [("swa0", 4, 0), ("swa1", 4, 0)]]


def attention_unit(kind, u):
    if kind.startswith("nsa"):
        hh, r = divmod(u, 9)
        return (hh, (r - 1) // 2, 1 + (r - 1) % 2) if r else (hh, 0, 0)
    return u // 4, u % 4, 1


def compressed(kind, u):
    return kind.startswith("nsa") and u % 9 == 0


def slot_of(kind, u):
    return u % (9 if kind.startswith("nsa") else 8)


def moved_by_vector(kind, u):
    return not kind.startswith(("nsa", "swa")) and u % 4 == 1


def bank_of(kind, u):
    return u % (3 if kind.startswith("nsa") else 4)


def attention_stream(eng, passes, begin, pair_of_heads):
    for n, (kind, pairs, pair) in enumerate(passes):
        per = PER_PAIR[kind]
        follow = passes[n + 1] if n + 1 < len(passes) else None
        if n == 0:
            begin(lambda u: (kind, pair, u, 0))
        if pairs > 1:
            with eng.Fori(0, pairs - 1) as i:
                pair_of_heads(per, lambda u: (kind, pair, u, i) if u < per else (kind, pair, u - per, i + 1))

        def at(u):
            if u < per:
                return kind, pair, u, pairs - 1
            return (follow[0], follow[2], u - per, 0) if follow else None

        pair_of_heads(per, at)


def heads_before(kind, u):
    return 8 * int(kind[3]) + u // TT


def key_tiles(kind, qt, branch):
    if kind.startswith("mem"):
        return list(range(N_MEM // P))
    if kind.startswith("swa"):
        return [qt - 1, qt] if qt else [0]
    return list(range(qt + 1))


def program(nc, A):
    with ExitStack() as ctx:
        def sb(name, shape, dt=F32, where=ctx):
            return where.enter_context(nc.sbuf_tensor(name, shape, dt))

        def sem(name):
            return ctx.enter_context(nc.semaphore(name))

        x = sb("x", [P, KT, SEQ])
        h_hi = sb("h_hi", [P, KT, SEQ], F32R)
        h_lo = sb("h_lo", [P, KT, SEQ], F32R)
        tmp = sb("tmp", [P, 2, SEQ])
        sq = sb("sq", [P, 2, SEQ])
        sqacc = sb("sqacc", [P, SEQ])
        diag = sb("diag", [P, SEQ])
        spare = sb("spare", [P, SEQ])
        w_raw = sb("w_raw", [P, RAW, KT * P])
        w_hi = sb("w_hi", [P, RING, KT * P], F32R)
        w_lo = sb("w_lo", [P, RING, KT * P], F32R)
        ident = sb("ident", [P, P])
        perm = sb("perm", [P, P])
        rope_c = sb("rope_c", [P, SEQ])
        rope_s = sb("rope_s", [P, SEQ])
        masks = sb("masks", [P, 2 * P + TT * 32])
        masks_b = sb("masks_b", [P, 2 * P + TT * 32], BF16)
        ident_b = sb("ident_b", [P, P], BF16)
        ones = sb("ones", [P, P])
        eps = sb("eps", [P, 1])
        cols = sb("cols", [P, N_COLS])
        w_uk = sb("w_uk", [P, P])
        w_uv = sb("w_uv", [P, HD])
        sinks = sb("sinks", [P, 16])
        nsinks = sb("nsinks", [P, 16])
        k_mem = sb("k_mem", [P, DEPTH, 2, N_MEM])
        v_mem = sb("v_mem", [P, DEPTH, 2, 2 * P])
        nmax = sb("nmax", [P, 9])
        psum_p = sb("psum_p", [P, 9])
        rinv = sb("rinv", [P, 9])
        oscale = sb("oscale", [P, 9])

        mean_sq = sb("mean_sq", [P, TT])
        both_gains = sb("both_gains", [P, KT])
        eps_out = sb("eps_out", [P, TT])
        root, inv_root = rinv[:, 0:TT], oscale[:, 0:TT]

        def norm_tile(k):
            return (tmp, sq)[k // 2 % 2][:, k % 2, :]

        relu_l, weighed, rope_t0 = sq, [diag, spare], tmp
        prob, probT = tmp, sq
        q_plain, q_pos0 = diag, spare

        layer0 = ExitStack()
        mem_hi1 = sb("mem_hi1", [P, KT, N_MEM], F32R, layer0)
        mem_lo1 = sb("mem_lo1", [P, KT, N_MEM], F32R, layer0)
        with ExitStack() as s:
            memx = sb("memx", [P, KT, N_MEM], where=s)
            mem_hi = [sb("mem_hi0", [P, KT, N_MEM], F32R, s), mem_hi1]
            mem_lo = [sb("mem_lo0", [P, KT, N_MEM], F32R, s), mem_lo1]
        with layer0, ExitStack() as s:
            q_dsa = sb("q_dsa", [P, TOK_HEADS, SEQ], F32R, s)
            k_dsa = [sb(f"k_dsa_{part}", [P, SEQ], F32R, s) for part in ("hi", "lo")]
            dsa_v = sb("dsa_v", [P, TT, HD], where=s)
            dsa_mask = sb("dsa_mask", [P, TT, SEQ], BF16, s)
            qmem0 = sb("qmem0", [P, 2, SEQ], where=s)
            with ExitStack() as s2:
                q0 = sb("q0", [P, 6, SEQ], where=s2)
                ckv = sb("ckv", [P, SEQ], where=s2)
                ckv_n = sb("ckv_n", [P, SEQ], where=s2)
                dsa_k = sb("dsa_k", [P, SEQ], where=s2)
                qidx = sb("qidx", [P, 4, SEQ], where=s2)
                kidx = sb("kidx", [P, SEQ], where=s2)
                widx = sb("widx", [P, TT, IDX_HEADS], where=s2)
                score = sb("score", [P, 2, SEQ], where=s2)
                widx_f = score[:, 0, :]
                top8 = sb("top8", [P, 8], where=s2)
            q_stage0 = sb("q_stage0", [P, 2, SEQ], F32R, s)
            o_tok0 = sb("o_tok0", [P, TT, D], where=s)
        with ExitStack() as s:
            act_hi = sb("act_hi", [P, FT, SEQ], F32R, s)
            act_lo = sb("act_lo", [P, FT, SEQ], F32R, s)
        with ExitStack() as s:
            q1 = sb("q1", [P, 6, SEQ], where=s)
            qmem1 = sb("qmem1", [P, 2, SEQ], where=s)
            k_nsa = [sb(f"k_nsa_{part}", [P, 4, SEQ], F32R, s) for part in ("hi", "lo")]
            v_nsa = sb("v_nsa", [P, TT, 2 * P], where=s)
            gates = sb("gates", [P, TT, 3 * TOK_HEADS], where=s)
            k_cmp = sb("k_cmp", [P, 2 * N_CMP], where=s)
            v_cmp = sb("v_cmp", [P, 2, TT * HD + TT], where=s)
            c_max = sb("c_max", [P, TT, 1], where=s)
            c_shift = sb("c_shift", [P, TT, 32], where=s)
            c_scale = sb("c_scale", [P, TT, 1], where=s)
            cmp_hk = sb("cmp_hk", [P, 2 * N_CMP], where=s)
            cmp_hv = sb("cmp_hv", [P, 2, TT, 32], where=s)
            cmp_w2k = sb("cmp_w2k", [P, P], where=s)
            cmp_w2v = sb("cmp_w2v", [P, HD], where=s)
            cmp_pos = [sb(f"cmp_pos{c}", [P, CMP_PAIRS], where=s) for c in "kv"]
            with ExitStack() as s2:
                q1r = sb("q1r", [P, 2, SEQ], where=s2)
                k_raw = sb("k_raw", [P, 4, SEQ], where=s2)
                rope_t1 = sb("rope_t1", [P, 2, SEQ], where=s2)
            q_stage1 = sb("q_stage1", [P, 2, SEQ], F32R, s)
            o_tok1 = sb("o_tok1", [P, TT, D], where=s)
            with ExitStack() as s2:
                cmp_w1 = [sb(f"cmp_w1{c}", [P, CMP_PAIRS, P], where=s2) for c in "kv"]
                cmp_x = [sb(f"cmp_x{c}", [P, CMP_PAIRS, 2, N_CMP], where=s2) for c in "kv"]
            q_nsa = sb("q_nsa", [P, TOK_HEADS, SEQ], F32R, s)
        with ExitStack() as s:
            gq = sb("gq", [P, 4, SEQ], where=s)
            gk = sb("gk", [P, 4, SEQ], where=s)
            gv = sb("gv", [P, TT, D], where=s)
            gsilu = sb("gsilu", [P, KT, SEQ], where=s)
            gla_mask = sb("gla_mask", [P, P], I32, s)
            k_inv = sb("k_inv", [P, 4, SEQ], where=s)
            decay = sb("decay", [P, 4, N_CHUNK], where=s)
            with ExitStack() as s2:
                glr = sb("glr", [P, SEQ], where=s2)
                w_gate = sb("w_gate", [16, 4 * P], where=s2)
                g_ab = sb("g_ab", [P, SEQ], where=s2)
                g_la = sb("g_la", [P, SEQ], where=s2)
                g_cum = sb("g_cum", [P, SEQ], where=s2)
                g_exp = sb("g_exp", [P, SEQ], where=s2)
                g_inv = sb("g_inv", [P, SEQ], where=s2)
                g_end = sb("g_end", [P, SEQ], where=s2)
                g_reset = sb("g_reset", [P, SEQ], where=s2)
            k_endT = sb("k_endT", [P, 2, TT, P], where=s)
            state = sb("state", [P, 2, N_CHUNK, 2 * P], where=s)
            attT = sb("attT", [P, 2, TT, P], where=s)
            g_o = [gk, k_inv]
        with ExitStack() as s:
            sq_q = sb("sq_q", [P, KT, SEQ], where=s)
            sk = sb("sk", [P, 2, SEQ], where=s)
            sv = sb("sv", [P, TT, P], where=s)
            k_swa = [sb(f"k_swa_{part}", [P, 2, SEQ], F32R, s) for part in ("hi", "lo")]
            q_swa = sb("q_swa", [P, 2 * SWA_PAIRS, SEQ], F32R, s)
            q_stage2 = sb("q_stage2", [P, 2, SEQ], F32R, s)
            rawmax = sb("rawmax", [P, 9], where=s)
            sinkexp = sb("sinkexp", [P, 9], where=s)
            sink_shift = sb("sink_shift", [P, 9], where=s)
            o_tok2 = sb("o_tok2", [P, TT, D], where=s)
        with ExitStack() as s:
            m = sb("m", [P, KT, SEQ], where=s)
            with ExitStack() as s2:
                gained = sb("gained", [P, KT // 2, SEQ], where=s2)
            mact_hi = sb("mact_hi", [P, HALF_FT, SEQ], F32R, s)
            mact_lo = sb("mact_lo", [P, HALF_FT, SEQ], F32R, s)

        bank = [ctx.enter_context(nc.psum_tensor(f"bank{b}", [P, SEQ], F32)) for b in range(8)]
        score_bank, probT_bank, o_bank = bank[2:4] + bank[0:2], bank[4:6], bank[6:8]

        def output_place(kind, u, g):
            if kind.startswith("swa"):
                return o_bank[g // TT % 2][:, HD * (u % TT):HD * (u % TT + 1)]
            return o_bank[g % 2][:, 0:HD]

        def index_bank(n):
            return bank[2 + n % 6]

        late_sum_bank, late_inverse_bank = bank[6], bank[7]

        def state_bank(n):
            return bank[2 + n % 6][:, 0:2 * P]

        consts_in, mem_in, x_in = sem("consts_in"), sem("mem_in"), [sem("x_in0"), sem("x_in1")]
        cmp_in, gla_in = sem("cmp_in"), sem("gla_in")
        raw_loaded = [sem(f"raw_loaded{b}") for b in range(RAW)]
        hi_ready, lo_ready = sem("hi_ready"), sem("lo_ready")
        chunks_used = sem("chunks_used")
        small_done = sem("small_done")
        evacuated = [sem(f"evacuated{b}") for b in range(2)]
        consts_made = sem("consts_made")
        sq_done, sq_added = sem("sq_done"), sem("sq_added")
        h_made, h_rounded = sem("h_made"), sem("h_rounded")
        h_ready = [sem("h_ready_even"), sem("h_ready_odd")]
        diag_ready, root_ready = sem("diag_ready"), sem("root_ready")
        late_sum, late_inverse, swa_biased = sem("late_sum"), sem("late_inverse"), sem("swa_biased")
        act_made, act_rounded, act_ready = sem("act_made"), sem("act_rounded"), sem("act_ready")
        gain_made = sem("gain_made")
        gain_rounded, gain_split = sem("gain_rounded"), [sem("gain_split_even"), sem("gain_split_odd")]
        gained_sq_done, gained_sq_added = sem("gained_sq_done"), sem("gained_sq_added")
        x_normed, m_scaled = sem("x_normed"), sem("m_scaled")
        x_added = [sem("x_added_even"), sem("x_added_odd")]
        ckv_normed, roped = sem("ckv_normed"), sem("roped")
        idx_ready, idx_relu, idx_weighed = sem("idx_ready"), sem("idx_relu"), sem("idx_weighed")
        idx_added, idx_chain = sem("idx_added"), sem("idx_chain")
        dsa_masked = sem("dsa_masked")
        q_staged, pos0_staged = sem("q_staged"), sem("pos0_staged")
        q_rounded, q_split, k_rounded, k_split = sem("q_rounded"), sem("q_split"), sem("k_rounded"), sem("k_split")
        scores_ready, max_ready, probs_ready = sem("scores_ready"), sem("max_ready"), sem("probs_ready")
        transposed, pv_done, o_done = sem("transposed"), sem("pv_done"), sem("o_done")
        probT_ready = [sem("probT_ready0"), sem("probT_ready1")]
        rawmax_ready, sum_ready, rinv_ready = sem("rawmax_ready"), sem("sum_ready"), sem("rinv_ready")
        sink_shifted, sink_ready = sem("sink_shifted"), sem("sink_ready")
        oscale_ready = sem("oscale_ready")
        cat_rounded = sem("cat_rounded")
        cmp_built = sem("cmp_built")
        g_absed, g_logged, g_cummed, g_exped, g_gated = (sem("g_absed"), sem("g_logged"), sem("g_cummed"),
                                                                  sem("g_exped"), sem("g_gated"))
        g_diffed, gds_ready, state_made = sem("g_diffed"), sem("gds_ready"), sem("state_made")
        go_made, go_rounded, go_split = sem("go_made"), sem("go_rounded"), sem("go_split")
        dve_step, act_step = sem("dve_step"), sem("act_step")
        relu_done, stored = sem("relu_done"), sem("stored")

        def col(name, k=0):
            n = GAINS.index(name) * KT + k if name in GAINS else len(GAINS) * KT + EXTRA.index(name)
            return cols[:, n:n + 1]

        def wait_evacuated(eng, name, later=0):
            n = JOB[name]
            eng.wait_ge(evacuated[n % 2], n // 2 + 1 + later)

        def wait_product(eng, name, later=0):
            chunks = dict(JOBS)[name]
            if chunks:
                eng.wait_ge(chunks_used, CHUNK[name] + chunks + later)
            else:
                eng.wait_ge(small_done, SMALL[name] + 1)

        def of(name):
            return bank[JOB[name] % 2]

        ROPES = ["kidx"] + [f"qidx{j}" for j in range(4)] + ["dsa_k"] + [f"q0.{j}" for j in range(6)] + \
                [f"{s}{g}" for s in ("ks", "kw") for g in range(2)] + [f"q1.{j}" for j in range(6)]

        def rope_tile(name):
            if name == "kidx":
                return kidx[:, :], kidx[:, :], rope_t0
            if name.startswith("qidx"):
                t = qidx[:, int(name[4]), :]
                return t, t, rope_t0
            if name == "dsa_k":
                return dsa_k[:, :], dsa_k[:, :], rope_t0
            if name.startswith("q0."):
                t = q0[:, int(name[3]), :]
                return t, t, rope_t0
            if name.startswith("q1."):
                return q1[:, int(name[3]), :], q1r[:, int(name[3]) % 2, :], rope_t1
            t = k_raw[:, 2 * (name[1] == "w") + int(name[2]), :]
            return t, t, rope_t1

        def output_of(kind):
            return {"dsa": o_tok0, "mem0": o_tok0, "nsa0": o_tok1, "nsa1": o_tok1, "mem1": o_tok1}.get(kind, o_tok2)

        def split_queries(kind):
            return {"dsa": (q_dsa, 0, 0), "nsa0": (q_nsa, 0, 6), "nsa1": (q_nsa, 6, 6), "swa0": (q_swa, 0, 12), "swa1": (q_swa, 8, 12)}[kind]

        def staged(kind):
            return {"d": q_stage0, "n": q_stage1, "s": q_stage2}[kind[0]]

        def both_heads(kind, j, tile):
            q = split_queries(kind)[0]
            for hh in range(2):
                rows, others = slice(HD * hh, HD * hh + HD), slice(HD - HD * hh, P - HD * hh)
                yield tile[rows, :], q[rows, 2 * j + hh, :], q[others, 2 * j + hh, :]

        block = ctx.enter_context(nc.Block())

        @block.sync
        def _(sp):
            def load(t, per=0, i=0):
                if per or t >= RAW:
                    sp.wait_ge(lo_ready, t - RAW + 1 + per * i)
                src = A["weights"][t] if not per else \
                    A["weights"][bass.ds(i * per + t, 1)].rearrange("a p n -> p (a n)")
                sp.dma_start(w_raw[:, t % RAW, :], src).then_inc(raw_loaded[t % RAW], 16)

            for t in range(RAW):
                load(t)
            for dst, src in ((cols[:, :], A["cols"]), (ident[:, :], A["ident"]), (perm[:, :], A["perm"]), (rope_c[:, :], A["rope_c"]),
                             (rope_s[:, :], A["rope_s"]), (masks[:, :], A["masks"]),
                             (w_uk[:, :], A["w_uk"]), (w_uv[:, :], A["w_uv"]), (sinks[:, :], A["sinks"])):
                sp.dma_start(dst, src).then_inc(consts_in, 16)
            sp.dma_start(memx[:, :, :], A["memT"]).then_inc(mem_in, 16)
            loops = (N_CHUNKS - RAW) // RAW
            with sp.Fori(0, loops) as i:
                for u in range(RAW):
                    load(RAW + u, RAW, i)
            for t in range(RAW + loops * RAW, N_CHUNKS):
                load(t)

        @block.gpsimd
        def _(pool):
            def rest(t, per=0, i=0):
                pool.wait_ge(hi_ready, t + 1 + per * i)
                nc.gpsimd.tensor_tensor(w_lo[:, t % RING, :], w_raw[:, t % RAW, :],
                                        w_hi[:, t % RING, :].bitcast(F32), ALU.subtract).then_inc(lo_ready, 1)

            def rests(t, end):
                while t < end and t % RING:
                    rest(t)
                    t += 1
                loops = (end - t) // RING
                if loops:
                    with pool.Fori(0, loops) as i:
                        for u in range(RING):
                            rest(t + u, RING, i)
                for t in range(t + loops * RING, end):
                    rest(t)

            def stage(hh, kind, pair, u, i):
                rows = slice(HD * hh, HD * hh + HD)
                before = STAGED[kind] + 2 * pair + hh + 2 * i
                if not isinstance(before, int) or before:
                    pool.wait_ge(q_staged, before)
                if kind.startswith("mem"):
                    wait_evacuated(pool, f"q{kind}.{pair}")
                    src = (qmem0 if kind == "mem0" else qmem1)[rows, pair, :]
                    nc.gpsimd.tensor_copy(q_plain[rows, :], src).then_inc(q_staged, 1)
                    return
                if kind.startswith("nsa"):
                    src = q1[rows, bass.ds(i + 3 * int(kind[3]), 1), :].rearrange("p a n -> p (a n)")
                    nc.gpsimd.tensor_copy(q_pos0[rows, :], src).then_inc(pos0_staged, 1)
                    pool.wait_ge(pos0_staged, 6 * int(kind[3]) + hh + 1 + 2 * i)
                q, head, _ = split_queries(kind)
                src = q[:, bass.ds(head + hh + 2 * i, 1), :].rearrange("p a n -> p (a n)")
                nc.gpsimd.tensor_copy(staged(kind)[:, hh, :], src).then_inc(q_staged, 1)

            def attention_begin(at):
                for hh in range(2):
                    stage(hh, *at(0))

            def add_sink(kind, pair, u, i):
                head, four = heads_before(kind, u), slice(slot_of(kind, u), slot_of(kind, u) + TT)
                pool.wait_ge(sink_ready, head + 1 + 2 * i)
                nc.gpsimd.tensor_tensor(oscale[:, four], psum_p[:, four], sinkexp[:, four], ALU.add).then_inc(sum_ready, 1)

            def pair_of_heads(per, at):
                for hh in range(2):
                    half = range(hh * per // 2, (hh + 1) * per // 2)
                    if at(0)[0].startswith("swa"):
                        add_sink(*at(half[0]))
                    if at(per):
                        kind, pair, u, i = at(half[-1])
                        pool.wait_ge(scores_ready, UNIT0[kind] + pair * per + u + 1 + per * i)
                        stage(hh, *at(per))

            def add_normed(name):
                b = SUMMED.index(name)

                def rest_of_gained(k):
                    pool.wait_ge(gain_made, KT // 2 * GAINED.index(FOLLOWED[name]) + k // 2 + 1)
                    nc.gpsimd.tensor_tensor(h_lo[:, k, :], gained[:, k // 2, :], h_hi[:, k, :].bitcast(F32), ALU.subtract).then_inc(gain_split[1], 1)

                for k in range(1, KT, 2):
                    pool.wait_ge(m_scaled, KT * b + k + 1)
                    nc.gpsimd.tensor_tensor(x[:, k, :], x[:, k, :], tmp[:, k % 2, :], ALU.add).then_inc(x_added[1], 1)
                    if name in FOLLOWED and k >= 3:
                        rest_of_gained(k - 2)
                if name in FOLLOWED:
                    rest_of_gained(KT - 1)

            def rest_of_norm(name, hi, lo, n=SEQ):
                for k in range(1, KT, 2):
                    pool.wait_ge(h_rounded, KT * NORMS.index(name) + k + 1)
                    nc.gpsimd.tensor_tensor(lo[:, k, :], norm_tile(k)[:, 0:n], hi[:, k, :].bitcast(F32), ALU.subtract).then_inc(h_ready[1], 1)

            def norms(start, names):
                for name in names:
                    end = CHUNK[FIRST[name]] + AHEAD
                    rests(start, end)
                    start = end
                    if name in SUMS[1:] and SUMS[SUMS.index(name) - 1] in SUMMED:
                        add_normed(SUMS[SUMS.index(name) - 1])
                    if name in GAINED:
                        continue
                    if name.startswith("mem"):
                        rest_of_norm(name, mem_hi[int(name[3])], mem_lo[int(name[3])], N_MEM)
                    else:
                        rest_of_norm(name, h_hi, h_lo)
                return start

            def index_scores(qt):
                n = (qt + 1) * P
                tile = score[:, qt % 2, 0:n]
                if qt > 2:
                    pool.wait_ge(dsa_masked, qt - 1)
                nc.gpsimd.memset(tile[:, 0:qt * P], 0.0).then_inc(idx_chain, 1)
                nc.gpsimd.tensor_copy(tile[:, qt * P:n], masks[:, P:2 * P]).then_inc(idx_chain, 1)
                pool.wait_ge(idx_chain, 2 * qt)
                for h in range(IDX_HEADS):
                    c = (qt - 1) * IDX_HEADS + h
                    pool.wait_ge(idx_weighed, c + 1)
                    if h:
                        pool.wait_ge(idx_added, c)
                    nc.gpsimd.tensor_tensor(tile, tile, weighed[c % 2][:, 0:n], ALU.add).then_inc(idx_added, 1)

            start = norms(0, ["attn0", "mem0", "mem1"])
            for qt, after in ((1, "q0.0"), (2, "q0.3"), (3, "qmem0.0")):
                rests(start, CHUNK[after] + AHEAD)
                start = CHUNK[after] + AHEAD
                if qt == 1:
                    pool.wait_ge(consts_made, 2)
                index_scores(qt)
            for j in range(6):
                pool.wait_ge(q_rounded, 2 * j + 2)
                for hh, (part, hi, lo) in enumerate(both_heads("dsa", j, q0[:, j, :])):
                    if j or hh:
                        pool.wait_ge(q_split, 2 * j + hh)
                    else:
                        pool.wait_ge(idx_added, 3 * IDX_HEADS)
                    nc.gpsimd.tensor_tensor(lo, part, hi.bitcast(F32), ALU.subtract).then_inc(q_split, 1)
            pool.wait_ge(q_split, 12)
            for passes, after, heads, names in ((STREAMS[0], "wo0.0", 12, ["ffn0", "attn1"]),
                                                (STREAMS[1], "wo1.0", 24, ["ffn1", "mixpre0", "mlppre0", "mixpre1"]),
                                                (STREAMS[2], "mix1.0", 40, ["mlppre1"])):
                rests(start, CHUNK[after] + AHEAD)
                start = CHUNK[after] + AHEAD
                pool.wait_ge(q_split, heads)
                attention_stream(pool, passes, attention_begin, pair_of_heads)
                start = norms(start, names)
            rests(start, N_CHUNKS)
            add_normed("mlppost1")

        @block.tensor
        def _(pe):
            def bank_free(n, per=0, i=0):
                if per or n >= 2:
                    pe.wait_ge(evacuated[n % 2], n // 2 + per // 2 * i)

            def chunk_ready(t, per=0, i=0):
                pe.wait_ge(lo_ready, t + 1 + per * i)

            def three(out, w, xs, first, last, swap=False):
                (wh, wl), (xh, xl) = w, xs
                for n, (a, b) in enumerate(((wh, xh), (wh, xl), (wl, xh))):
                    if swap:
                        a, b = b, a
                    r = nc.tensor.matmul(out, a, b, start=first and n == 0, stop=last and n == 2)
                return r

            def after_norm(out, t, xs, norm):
                for k in range(KT):
                    wh, wl = slot(t, k)
                    rounded(norm, k)
                    nc.tensor.matmul(out, wh, xs[0][:, k, :], start=k == 0, stop=False)
                    nc.tensor.matmul(out, wl, xs[0][:, k, :], start=False, stop=False)
                for k in range(KT):
                    normed(norm, k)
                    r = nc.tensor.matmul(out, slot(t, k)[0], xs[1][:, k, :], start=False, stop=k == KT - 1)
                return r

            def slot(t, k, width=P):
                return (w_hi[:, t % RING, k * P:k * P + width], w_lo[:, t % RING, k * P:k * P + width])

            def column_tile(name, hs=(h_hi, h_lo), n=SEQ, last=True, norm=None, cat=None):
                t = CHUNK[name]
                bank_free(JOB[name])
                chunk_ready(t)
                for k in range(0 if norm else KT):
                    if cat == "gla":
                        pe.wait_ge(go_split, k + 1)
                    elif cat:
                        wait_evacuated(pe, f"{cat}.{k}")
                    r = three(of(name)[:, 0:n], slot(t, k), (hs[0][:, k, :], hs[1][:, k, :]), k == 0, last and k == KT - 1)
                if norm:
                    r = after_norm(of(name)[:, 0:n], t, hs, norm)
                if last:
                    r.then_inc(chunks_used, 1)

            def token_tiles(name, chunks, tiles, hs=(h_hi, h_lo)):
                t = CHUNK[name]
                assert t % RING < RING - 1
                bank_free(JOB[name])
                chunk_ready(t + 1)
                for n, a in enumerate(tiles):
                    for k in range(KT):
                        w = [part[:, t % RING:t % RING + 2, k * P:(k + 1) * P] for part in (w_hi, w_lo)]
                        xs = (hs[0][:, k, a * P:(a + 1) * P], hs[1][:, k, a * P:(a + 1) * P])
                        out = of(name)[:, n * 2 * P:(n + 1) * 2 * P].rearrange("p (c n) -> p c n", c=2)
                        r = three(out, w, xs, k == 0, k == KT - 1, swap=True)
                r.then_inc(*((chunks_used, 2) if chunks else (small_done, 1)))

            def to_tokens(name, tile):
                job = f"{name}T"
                bank_free(JOB[job])
                wait_evacuated(pe, name)
                if name == "sv":
                    pe.wait_ge(swa_biased, KT + 1)
                for a in range(TT):
                    r = nc.tensor.transpose(of(job)[:, a * P:(a + 1) * P], tile[:, a * P:(a + 1) * P], ident[:, :])
                r.then_inc(small_done, 1)

            def rounded(name, k):
                if name in GAINED:
                    pe.wait_ge(gain_rounded, KT * GAINED.index(name) + k + 1)
                    return
                pe.wait_ge(h_rounded, KT * NORMS.index(name) + k + 1)

            def normed(name, k):
                if name in GAINED:
                    pe.wait_ge(gain_split[k % 2], KT // 2 * GAINED.index(name) + k // 2 + 1)
                    return
                pe.wait_ge(h_ready[k % 2], KT // 2 * NORMS.index(name) + k // 2 + 1)

            def sum_of(job, sources, n=SEQ, inverse=True):
                bank_free(JOB[job])
                for a in range(n // P):
                    for c, src in enumerate(sources):
                        r = nc.tensor.matmul(of(job)[:, a:a + 1], src[:, a * P:(a + 1) * P], ones[:, 0:1],
                                             start=c == 0, stop=c == len(sources) - 1)
                r.then_inc(small_done, 1)
                if inverse:
                    inverse_roots(job, n)

            def inverse_roots(job, n=SEQ):
                job = inverse_of(job)
                bank_free(JOB[job])
                pe.wait_ge(diag_ready, INVERSES.index(job) + 1)
                nc.tensor.matmul(of(job)[:, 0:n], ones[:, :], diag[:, 0:n], start=True, stop=True).then_inc(small_done, 1)

            def sum_squares(name, n=SEQ):
                b = 9 * SUMS.index(name)
                pe.wait_ge(sq_added, b + 9)
                if name == "final":
                    pe.wait_ge(gained_sq_added, KT + 2)
                    bank_free(JOB["sum.final"])
                    for n, src in enumerate((sqacc, spare)):
                        for a in range(TT):
                            r = nc.tensor.matmul(of("sum.final")[:, n * TT + a:n * TT + a + 1], src[:, a * P:(a + 1) * P], ones[:, 0:1],
                                                 start=True, stop=True)
                    r.then_inc(small_done, 1)
                    inverse_roots("sum.final")
                    return
                sum_of("memsum" if name == "mem" else f"sum.{name}", [sqacc], n, name not in GAINED and name != "mem")

            def rope(name):
                job = f"rope.{name}"
                bank_free(JOB[job])
                wait_evacuated(pe, name)
                nc.tensor.matmul(of(job)[:, :], perm[:, :], rope_tile(name)[0], start=True, stop=True).then_inc(small_done, 1)

            def index_scores(qt):
                for h in range(IDX_HEADS):
                    n = (qt - 1) * IDX_HEADS + h
                    if n >= 6:
                        pe.wait_ge(idx_relu, n - 5)
                    o = HD * (h % 2)
                    nc.tensor.matmul(index_bank(n)[:, 0:(qt + 1) * P], qidx[o:o + HD, h // 2, qt * P:(qt + 1) * P],
                                     kidx[o:o + HD, 0:(qt + 1) * P], start=True, stop=True).then_inc(idx_ready, 1)

            def scores(kind, pair, u, i):
                hh, qt, br = attention_unit(kind, u)
                per, o, l = PER_PAIR[kind], HD * hh, int(kind[3]) if kind[3:] else 0
                g = UNIT0[kind] + pair * per + u
                out = score_bank[bank_of(kind, u)]
                if u % (per // 2) == 0:
                    pe.wait_ge(q_staged, STAGED[kind] + 2 * pair + hh + 1 + 2 * i)
                pe.wait_ge(probs_ready, g - kind.startswith("swa") + per * i)
                if compressed(kind, u):
                    nc.tensor.matmul(out[:, 0:P], ident_b[:, :], masks_b[:, 2 * P:3 * P], start=True, stop=False)
                    for a in range(TT):
                        r = nc.tensor.matmul(out[:, 32 * a:32 * a + N_CMP], q_pos0[o:o + HD, a * P:(a + 1) * P],
                                             k_cmp[o:o + HD, l * N_CMP:(l + 1) * N_CMP], start=False, stop=a == TT - 1)
                    r.then_inc(scores_ready, 1)
                    return
                kts = key_tiles(kind, qt, br)
                n = len(kts) * P
                if kind.startswith("mem"):
                    nc.tensor.matmul(out[:, 0:n], q_plain[o:o + HD, qt * P:(qt + 1) * P], k_mem[o:o + HD, l, pair, :],
                                     start=True, stop=True).then_inc(scores_ready, 1)
                    return
                q = staged(kind)[:, hh, qt * P:(qt + 1) * P]
                if kind == "dsa":
                    ks, mask = [k[:, 0:n] for k in k_dsa], dsa_mask[:, qt, 0:n]
                elif kind.startswith("swa"):
                    ks, mask = [k[:, l, kts[0] * P:(qt + 1) * P] for k in k_swa], masks_b[:, 2 * P - n:2 * P]
                else:
                    ks, mask = [k[:, 2 * (br - 1) + l, 0:n] for k in k_nsa], masks_b[:, P:2 * P]
                for part, k in enumerate(ks):
                    nc.tensor.matmul(out[:, 0:n], q, k, start=part == 0, stop=False)
                m0 = n - P if kind.startswith("nsa") else 0
                nc.tensor.matmul(out[:, m0:n], ident_b[:, :], mask, start=False, stop=True).then_inc(scores_ready, 1)

            def transposes(kind, pair, u, i):
                _, qt, br = attention_unit(kind, u)
                per = PER_PAIR[kind]
                g = UNIT0[kind] + pair * per + u
                pe.wait_ge(probs_ready, g + 3 + per * i)
                pe.wait_ge(probT_ready[g % 2], g // 2 + 1 + per // 2 * i)
                for n in range(1 if compressed(kind, u) else len(key_tiles(kind, qt, br))):
                    r = nc.tensor.transpose(probT_bank[g % 2][:, n * P:(n + 1) * P], prob[:, g % 2, n * P:(n + 1) * P], ident[:, :])
                r.then_inc(transposed, 1)

            def values(kind, pair, u, i):
                hh, qt, br = attention_unit(kind, u)
                per, l = PER_PAIR[kind], int(kind[3]) if kind[3:] else 0
                g = UNIT0[kind] + pair * per + u
                pe.wait_ge(probT_ready[g % 2], g // 2 + 2 + per // 2 * i)
                if not kind.startswith("swa"):
                    pe.wait_ge(o_done, g + 1 + per * i)
                elif u % TT == 0:
                    pe.wait_ge(o_done, g - 2 + per * i)
                if compressed(kind, u):
                    r = nc.tensor.matmul(o_bank[g % 2][:, 0:TT * HD + TT], probT[:, g % 2, 0:P], v_cmp[:, l, :], start=True, stop=True)
                    r.then_inc(pv_done, 1)
                    return
                kts = key_tiles(kind, qt, br)
                for n, kt in enumerate(kts):
                    if kind == "dsa":
                        v = dsa_v[:, kt, :]
                    elif kind.startswith("mem"):
                        v = v_mem[:, l, kt, (2 * pair + hh) * HD:(2 * pair + hh + 1) * HD]
                    elif kind.startswith("swa"):
                        v = sv[:, kt, l * HD:(l + 1) * HD]
                    else:
                        v = v_nsa[:, kt, (br - 1) * P + l * HD:(br - 1) * P + (l + 1) * HD]
                    r = nc.tensor.matmul(output_place(kind, u, g), probT[:, g % 2, n * P:(n + 1) * P], v, start=n == 0, stop=n == len(kts) - 1)
                r.then_inc(pv_done, 1)

            def attention_begin(at):
                for u in range(4):
                    scores(*at(u))
                for u in range(2):
                    transposes(*at(u))

            def pair_of_heads(per, at):
                for u in range(per):
                    if at(u + 4):
                        scores(*at(u + 4))
                    if at(u + 2):
                        transposes(*at(u + 2))
                    values(*at(u))

            def concat(prefix, kind, units):
                o_tok = output_of(kind)
                pe.wait_ge(o_done, 2 + units)
                for j in range(KT):
                    name = f"{prefix}.{j}"
                    bank_free(JOB[name])
                    for a in range(TT):
                        r = nc.tensor.transpose(of(name)[:, a * P:(a + 1) * P], o_tok[:, a, j * P:(j + 1) * P], ident[:, :])
                    r.then_inc(small_done, 1)

            def up(prefix, tiles, norm):
                n0, t0 = JOB[f"{prefix}.0"], CHUNK[f"{prefix}.0"]
                with pe.Fori(0, tiles // 4) as i:
                    for u in range(4):
                        bank_free(n0 + u, 4, i)
                        chunk_ready(t0 + u, 4, i)
                        out = bank[(n0 + u) % 2][:, :]
                        if u == 0:
                            r = after_norm(out, t0 + u, (h_hi, h_lo), norm)
                        else:
                            for k in range(KT):
                                r = three(out, slot(t0 + u, k), (h_hi[:, k, :], h_lo[:, k, :]), k == 0, k == KT - 1)
                        r.then_inc(chunks_used, 1)

            def down(prefix, hi, lo, tiles, per_tile, step, before):
                n0, t0 = JOB[f"{prefix}.0"], CHUNK[f"{prefix}.0"]
                with pe.Fori(0, KT // step) as i:
                    for j in range(step):
                        bank_free(n0 + j, step, i)
                        for c in range(per_tile):
                            t = t0 + j * per_tile + c
                            chunk_ready(t, step * per_tile, i)
                            ks_ = min(KT, tiles - c * KT)
                            for k in range(ks_):
                                f = c * KT + k
                                if j == 0:
                                    pe.wait_ge(act_ready, before + f + 1)
                                r = three(bank[(n0 + j) % 2][:, :], slot(t, k), (hi[:, f, :], lo[:, f, :]), f == 0, f == tiles - 1)
                            r.then_inc(chunks_used, 1)

            pe.sem_inc(transposed, 2)
            pe.sem_inc(pv_done, 2)
            pe.wait_ge(consts_made, 1)
            def memory(l):
                for j in range(2):
                    column_tile(f"mk{l}.{j}", (mem_hi[l], mem_lo[l]), N_MEM, norm=None if j else f"mem{l}")
                token_tiles(f"mv{l}", 2, range(2), (mem_hi[l], mem_lo[l]))

            sum_squares("attn0")
            column_tile("ckv", norm="attn0")
            column_tile("kidx")
            wait_evacuated(pe, "ckv")
            sum_of("ckvsum", [sq[:, 0, :]], inverse=False)
            column_tile("qidx0")
            inverse_roots("ckvsum")
            pe.wait_ge(consts_made, 2)
            rope("kidx")
            column_tile("qidx1")
            sum_squares("mem", N_MEM)
            rope("qidx0")
            column_tile("qidx2")
            inverse_roots("memsum", N_MEM)
            rope("qidx1")
            column_tile("qidx3")
            rope("qidx2")
            column_tile("widx")
            rope("qidx3")
            column_tile("dsa_k", last=False)
            pe.wait_ge(ckv_normed, 1)
            nc.tensor.matmul(of("dsa_k")[:, :], w_uk[:, :], ckv_n[:, :], start=False, stop=True).then_inc(chunks_used, 1)
            to_tokens("widx", widx_f)
            bank_free(JOB["dsa_v"])
            for a in range(TT):
                r = nc.tensor.matmul(of("dsa_v")[:, a * HD:(a + 1) * HD], ckv_n[:, a * P:(a + 1) * P], w_uv[:, :], start=True, stop=True)
            r.then_inc(small_done, 1)
            rope("dsa_k")
            pe.wait_ge(roped, 5)
            index_scores(1)
            for j in range(3):
                column_tile(f"q0.{j}")
            index_scores(2)
            for j in range(3, 6):
                column_tile(f"q0.{j}")
            memory(0)
            index_scores(3)
            for j in range(6):
                rope(f"q0.{j}")
            for j in range(2):
                column_tile(f"qmem0.{j}")
            memory(1)
            pe.wait_ge(roped, 12)
            pe.wait_ge(dsa_masked, TT)
            wait_evacuated(pe, "dsa_v")
            for j in range(2):
                wait_evacuated(pe, f"qmem0.{j}")
            for name in ("mk1.1", "mv1"):
                wait_evacuated(pe, name)
            pe.wait_ge(q_split, 12)
            pe.wait_ge(k_split, 1)
            attention_stream(pe, STREAMS[0], attention_begin, pair_of_heads)
            for l in range(DEPTH):
                if l == 1:
                    for s_ in ("kc", "vc", "ks", "kw"):
                        for g in range(2):
                            column_tile(f"{s_}{g}", norm="attn1" if f"{s_}{g}" == "kc0" else None)
                    for c, name in enumerate(("cmp_hk", "cmp_hv")):
                        bank_free(JOB[name])
                        pe.wait_ge(cmp_built, 4 * (c + 1))
                        for p_ in range(CMP_PAIRS):
                            r = nc.tensor.matmul(of(name)[:, 0:2 * N_CMP], cmp_w1[c][:, p_, :],
                                                 cmp_x[c][:, p_, :, :].rearrange("p g c -> p (g c)"),
                                                 start=p_ == 0, stop=p_ == CMP_PAIRS - 1)
                        r.then_inc(small_done, 1)
                    for s_ in ("ks", "kw"):
                        for g in range(2):
                            rope(f"{s_}{g}")
                    bank_free(JOB["cmp_k"])
                    wait_evacuated(pe, "cmp_hk")
                    nc.tensor.matmul(of("cmp_k")[:, 0:2 * N_CMP], cmp_w2k[:, :], cmp_hk[:, :], start=True, stop=True).then_inc(small_done, 1)
                    bank_free(JOB["cmp_v"])
                    wait_evacuated(pe, "cmp_hv")
                    for g in range(2):
                        r = nc.tensor.matmul(of("cmp_v")[:, g * HD:(g + 1) * HD], cmp_hv[:, g, :, :].rearrange("p a c -> p (a c)"),
                                             cmp_w2v[:, :], start=True, stop=True)
                    r.then_inc(small_done, 1)
                    column_tile("q1.0")
                    for j in range(1, 6):
                        column_tile(f"q1.{j}")
                        rope(f"q1.{j - 1}")
                    token_tiles("vsw.a", 0, (0, 1))
                    token_tiles("vsw.b", 2, (2, 3))
                    rope("q1.5")
                    column_tile("gates")
                    column_tile("qmem1.0")
                    to_tokens("gates", diag)
                    column_tile("qmem1.1")
                    pe.wait_ge(roped, len(ROPES))
                    for name in ("cmp_k", "cmp_v", "vsw.a", "vsw.b"):
                        wait_evacuated(pe, name)
                    for j in range(2):
                        wait_evacuated(pe, f"qmem1.{j}")
                    pe.wait_ge(q_split, 24)
                    pe.wait_ge(k_split, 5)
                    attention_stream(pe, STREAMS[1], attention_begin, pair_of_heads)
                concat(f"cat{l}", f"mem{l}", UNIT0[f"mem{l}"] + 16)
                for j in range(KT):
                    column_tile(f"wo{l}.{j}", cat=None if j else f"cat{l}")
                sum_squares(f"ffn{l}")
                up(f"up{l}", 2 * FT, f"ffn{l}")
                down(f"down{l}", act_hi, act_lo, FT, 3, 4, FT * l)
                sum_squares("attn1" if l == 0 else "final")
            column_tile("glr", norm="mixpre0")
            column_tile("gk0")
            inverse_roots("inv.x")
            for h in range(1, 4):
                column_tile(f"gk{h}")
            for h in range(4):
                column_tile(f"gq{h}")
            pe.wait_ge(gla_in, 32)
            for h in range(4):
                bank_free(JOB[f"gz{h}"])
                wait_evacuated(pe, "glr")
                nc.tensor.matmul(of(f"gz{h}")[:, :], w_gate[:, h * P:(h + 1) * P], glr[0:16, :], start=True, stop=True).then_inc(small_done, 1)
                token_tiles(f"gv{h}.a", 0, (0, 1))
                token_tiles(f"gv{h}.b", 2, (2, 3))

            def gla_scores(h):
                name = f"gket{h}"
                bank_free(JOB[name])
                for a in range(TT):
                    r = nc.tensor.transpose(of(name)[:, a * P:(a + 1) * P], gk[:, h, a * P:(a + 1) * P], ident[:, :])
                r.then_inc(small_done, 1)
                name = f"gatt{h}"
                bank_free(JOB[name])
                for a in range(TT):
                    r = nc.tensor.matmul(of(name)[:, a * P:(a + 1) * P], k_inv[:, h, a * P:(a + 1) * P], gq[:, h, a * P:(a + 1) * P],
                                         start=True, stop=True)
                r.then_inc(small_done, 1)
                wait_evacuated(pe, f"gket{h}")
                bank_free(JOB[f"gds{h}"])
                if h:
                    wait_evacuated(pe, f"gds{h - 1}")
                for n in range(N_CHUNK - 1):
                    o = GLA_CHUNK * (n % 2)
                    if n >= 6:
                        pe.wait_ge(state_made, (N_CHUNK - 2) * h + n - 5)
                    nc.tensor.matmul(state_bank(n), k_endT[o:o + GLA_CHUNK, h % 2, n // 2, :],
                                     gv[o:o + GLA_CHUNK, n // 2, h * 2 * P:(h + 1) * 2 * P], start=True, stop=True).then_inc(
                                         gds_ready if n < N_CHUNK - 2 else small_done, 1)

            def gla_outputs(h):
                wait_evacuated(pe, f"gatt{h}")
                wait_evacuated(pe, f"gds{h}")
                for j in range(2):
                    name = f"go{h}.{j}"
                    bank_free(JOB[name])
                    for a in range(TT):
                        c0 = h * 2 * P + j * P
                        r = nc.tensor.matmul(of(name)[:, a * P:(a + 1) * P], gv[:, a, c0:c0 + P], attT[:, h % 2, a, :], start=True, stop=False)
                        for n in (2 * a, 2 * a + 1):
                            if n:
                                r = nc.tensor.matmul(of(name)[:, n * GLA_CHUNK:(n + 1) * GLA_CHUNK], state[:, h % 2, n, j * P:(j + 1) * P],
                                                     gq[:, h, n * GLA_CHUNK:(n + 1) * GLA_CHUNK], start=False, stop=n % 2 == 1)
                    r.then_inc(small_done, 1)

            def gla_sum(h):
                for j in range(2):
                    wait_evacuated(pe, f"go{h}.{j}")
                sum_of(f"gosum{h}", [sq[:, j, :] for j in range(2)], inverse=False)

            for stage, h in GLA_STAGES:
                if stage == "gate":
                    column_tile(f"gg{h}")
                elif stage == "scores":
                    pe.wait_ge(g_gated, 12)
                    gla_scores(h)
                elif stage == "outputs":
                    gla_outputs(h)
                elif stage == "sum":
                    gla_sum(h)
                elif stage == "norm":
                    inverse_roots(f"gosum{h}")
            for l in range(DEPTH):
                if l == 1:
                    for j in range(KT):
                        column_tile(f"sq{j}", norm=None if j else "mixpre1")
                        if j == 1:
                            pe.wait_ge(sq_added, 9 * (SUMS.index("mixpre1") + 1))
                            for a in range(TT):
                                r = nc.tensor.matmul(late_sum_bank[:, a:a + 1], sqacc[:, a * P:(a + 1) * P], ones[:, 0:1], start=True, stop=True)
                            r.then_inc(late_sum, 1)
                            pe.wait_ge(diag_ready, INVERSES.index("inv.mixpre1") + 1)
                            nc.tensor.matmul(late_inverse_bank[:, :], ones[:, :], diag[:, :], start=True, stop=True).then_inc(late_inverse, 1)
                    column_tile("sv")
                    for g in range(2):
                        column_tile(f"sk{g}")
                    to_tokens("sv", diag)
                    for name in ("sk0", "sk1", "svT"):
                        wait_evacuated(pe, name)
                    pe.wait_ge(q_split, 40)
                    pe.wait_ge(k_split, 7)
                    attention_stream(pe, STREAMS[2], attention_begin, pair_of_heads)
                    concat("scat", "swa1", UNIT0["swa1"] + 32)
                for j in range(KT):
                    column_tile(f"mix{l}.{j}", cat=None if j else "scat" if l else "gla")
                sum_squares(f"mixpost{l}")
                for half in range(2):
                    up(f"mup{l}{half}", HALF_FT, f"mlppre{l}")
                    if half:
                        sum_squares(f"mlppre{l}")
                    down(f"mdown{l}{half}", mact_hi, mact_lo, HALF_FT, 2, 2, 2 * FT + HALF_FT * (2 * l + half))
                sum_squares(f"mlppost{l}")

        @block.scalar
        def _(act):
            following = [0]

            def split(t, per=0, i=0):
                act.wait_ge(raw_loaded[t % RAW], 16 * (t // RAW + 1) + 16 * per // RAW * i)
                if per or t >= RING:
                    act.wait_ge(chunks_used, t - RING + 1 + per * i)
                nc.scalar.activation(w_hi[:, t % RING, :], w_raw[:, t % RAW, :], ACT.Copy).then_inc(hi_ready, 1)

            def split_ahead(t):
                while following[0] <= min(t + AHEAD, N_CHUNKS - 1):
                    split(following[0])
                    following[0] += 1

            def product(name, c=None):
                n = dict(JOBS)[name]
                if n:
                    split_ahead(CHUNK[name] + n - 1)
                wait_product(act, name)

            def move(name, out, src=None, func=ACT.Copy, **how):
                product(name)
                nc.scalar.activation(out, of(name)[:, 0:SEQ] if src is None else src, func, **how).then_inc(evacuated[JOB[name] % 2], 1)

            def square(k, name, src, n=SEQ, ready=None, later=0):
                b = 9 * SUMS.index(name)
                if b or k >= 2:
                    act.wait_ge(sq_added, b + k if k >= 2 else b)
                nc.scalar.activation(sq[:, k % 2, 0:n], src, ACT.Square).then_inc(sq_done, 1)

            def deviation(job, n=SEQ, scale=1.0):
                if job == "sum.final":
                    wait_evacuated(act, job)
                    nc.scalar.activation(rinv[:, 0:2 * TT], oscale[:, 0:2 * TT], ACT.Sqrt, bias=eps[:, 0:1]).then_inc(root_ready, 1)
                    return
                if job[4:] in ROOTED:
                    wait_evacuated(act, job)
                    nc.scalar.activation(root[:, :], inv_root[:, :], ACT.Sqrt).then_inc(root_ready, 1)
                    return
                product(job)
                nc.scalar.activation(root[:, 0:n // P], of(job)[:, 0:n // P], ACT.Sqrt, scale=scale, bias=eps[:, 0:1]).then_inc(evacuated[JOB[job] % 2], 1)

            def round_norm(name, hi, n=SEQ):
                for k in range(KT):
                    act.wait_ge(h_made, KT * NORMS.index(name) + k + 1)
                    nc.scalar.activation(hi[:, k, :], norm_tile(k)[:, 0:n], ACT.Copy).then_inc(h_rounded, 1)

            def round_gained(name, added):
                for k in range(KT):
                    act.wait_ge(x_added[k % 2], added + k // 2 + 1)
                    nc.scalar.activation(h_hi[:, k, :], x[:, k, :], ACT.Identity, scale=col(name, k)).then_inc(gain_rounded, 1)
                    if k % 2:
                        nc.scalar.activation(gained[:, k // 2, :], x[:, k, :], ACT.Identity, scale=col(name, k)).then_inc(gain_made, 1)

            def index_logits(qt):
                n_ = (qt + 1) * P

                def relu(h):
                    n = (qt - 1) * IDX_HEADS + h
                    act.wait_ge(idx_ready, n + 1)
                    if n >= 2:
                        act.wait_ge(idx_weighed, n - 1)
                    nc.scalar.activation(relu_l[:, n % 2, 0:n_], index_bank(n)[:, 0:n_], ACT.Relu).then_inc(idx_relu, 1)

                relu(0)
                for h in range(IDX_HEADS):
                    if h + 1 < IDX_HEADS:
                        relu(h + 1)
                    n = (qt - 1) * IDX_HEADS + h
                    act.wait_ge(idx_relu, n + 1)
                    if n >= 2:
                        act.wait_ge(idx_added, n - 1)
                    nc.scalar.activation(weighed[n % 2][:, 0:n_], relu_l[:, n % 2, 0:n_], ACT.Identity,
                                         scale=widx[:, qt, h:h + 1]).then_inc(idx_weighed, 1)

            def round_queries(kind, j, tile):
                for part, hi, _ in both_heads(kind, j, tile):
                    nc.scalar.activation(hi, part, ACT.Copy).then_inc(q_rounded, 1)

            def exponentials(kind, pair, u, i):
                _, qt, br = attention_unit(kind, u)
                per = PER_PAIR[kind]
                g, s4 = UNIT0[kind] + pair * per + u, slot_of(kind, u)
                act.wait_ge(max_ready, g + 1 + per * i)
                act.wait_ge(transposed, g + 1 + per * i)
                if compressed(kind, u):
                    nc.scalar.activation(prob[:, g % 2, 0:P], c_shift[:, :, :].rearrange("p a c -> p (a c)"), ACT.Exp).then_inc(probs_ready, 1)
                    return
                n = P * len(key_tiles(kind, qt, br))
                nc.scalar.activation(prob[:, g % 2, 0:n], score_bank[bank_of(kind, u)][:, 0:n], ACT.Exp, bias=nmax[:, s4:s4 + 1],
                                     accum_out=psum_p[:, s4:s4 + 1]).then_inc(probs_ready, 1)
                if kind.startswith("swa") and u % TT == TT - 1:
                    four = slice(s4 - TT + 1, s4 + 1)
                    act.wait_ge(sink_shifted, heads_before(kind, u) + 1 + 2 * i)
                    nc.scalar.activation(sinkexp[:, four], sink_shift[:, four], ACT.Exp).then_inc(sink_ready, 1)

            def move_transposed(kind, pair, u, i):
                _, qt, br = attention_unit(kind, u)
                per = PER_PAIR[kind]
                g, n = UNIT0[kind] + pair * per + u, P if compressed(kind, u) else P * len(key_tiles(kind, qt, br))
                act.wait_ge(transposed, g + 3 + per * i)
                act.wait_ge(pv_done, g + 1 + per * i)
                nc.scalar.activation(probT[:, g % 2, 0:n], probT_bank[g % 2][:, 0:n], ACT.Copy).then_inc(probT_ready[g % 2], 1)

            def attention_begin(at):
                for u in range(3):
                    exponentials(*at(u))
                for u in range(2):
                    if not moved_by_vector(at(u)[0], u):
                        move_transposed(*at(u))

            def pair_of_heads(per, at):
                for u in range(per):
                    if at(u + 3):
                        exponentials(*at(u + 3))
                    if at(u + 2) and not moved_by_vector(at(u + 2)[0], at(u + 2)[2]):
                        move_transposed(*at(u + 2))

            def concat(prefix, n):
                for j in range(KT):
                    name = f"{prefix}.{j}"
                    product(name)
                    nc.scalar.activation(h_hi[:, j, :], of(name)[:, :], ACT.Copy).then_inc(cat_rounded, 1)

            def loop(t0, steps, per, body):
                split_ahead(t0 - 1)
                over = t0 + per * steps + AHEAD > N_CHUNKS
                with act.Fori(0, steps - over) as i:
                    body(i, lambda u: split(t0 + u + AHEAD, per, i))
                following[0] = t0 + per * (steps - over) + AHEAD
                if over:
                    last = steps - 1
                    body(last, lambda u: split_ahead(t0 + per * last + u))

            def up_gated(l):
                n0, t0 = JOB[f"up{l}.0"], CHUNK[f"up{l}.0"]

                def body(i, ahead):
                    for f in range(2):
                        b = n0 + 2 * f
                        ahead(2 * f)
                        act.wait_ge(chunks_used, t0 + 2 * f + 1 + 4 * i)
                        act.wait_ge(act_made, FT * l + f + 2 * i)
                        nc.scalar.activation(sq[:, f, :], bank[b % 2][:, :], ACT.Silu).then_inc(evacuated[b % 2], 1)
                        ahead(2 * f + 1)
                        act.wait_ge(act_made, FT * l + f + 1 + 2 * i)
                        nc.scalar.activation(act_hi[:, bass.ds(2 * i + f, 1), :].rearrange("p a n -> p (a n)"), tmp[:, f, :], ACT.Copy).then_inc(act_rounded, 1)

                loop(t0, FT // 2, 4, body)

            def up_relu(l, half):
                t0, n0 = CHUNK[f"mup{l}{half}.0"], JOB[f"mup{l}{half}.0"]
                c0 = 2 * FT + HALF_FT * (2 * l + half)

                def body(i, ahead):
                    for f in range(4):
                        ahead(f)
                        act.wait_ge(chunks_used, t0 + f + 1 + 4 * i)
                        act.wait_ge(act_made, c0 + f - 1 + 4 * i)
                        nc.scalar.activation(sq[:, f % 2, :], bank[(n0 + f) % 2][:, :], ACT.Relu).then_inc(relu_done, 1)
                        act.wait_ge(act_made, c0 + f + 1 + 4 * i)
                        nc.scalar.activation(mact_hi[:, bass.ds(4 * i + f, 1), :].rearrange("p a n -> p (a n)"), tmp[:, f % 2, :], ACT.Copy).then_inc(act_rounded, 1)

                loop(t0, HALF_FT // 4, 4, body)

            def down(prefix, per_tile, step, name, src):
                t0, n0 = CHUNK[f"{prefix}.0"], JOB[f"{prefix}.0"]

                def body(i, ahead):
                    for j in range(step):
                        for c in range(per_tile):
                            ahead(j * per_tile + c)
                        act.wait_ge(evacuated[(n0 + j) % 2], (n0 + j) // 2 + 1 + step // 2 * i)
                        act.wait_ge(sq_added, 9 * SUMS.index(name) + j + step * i)
                        tile = src[:, bass.ds(step * i + j, 1), :].rearrange("p a n -> p (a n)")
                        nc.scalar.activation(sq[:, j % 2, :], tile, ACT.Square).then_inc(sq_done, 1)
                        if name == "final":
                            act.wait_ge(gained_sq_added, j + 1 + step * i)
                            nc.scalar.activation(tmp[:, j % 2, :], tile, ACT.Square,
                                                 scale=cols[:, bass.ds(GAINS.index("final") * KT + j + step * i, 1)]).then_inc(gained_sq_done, 1)

                loop(t0, KT // step, step * per_tile, body)

            act.sem_inc(probs_ready, 2)
            act.sem_inc(probT_ready[0], 1)
            for part in range(2):
                half = slice(part * KT // 2, (part + 1) * KT // 2)
                act.dma_start(x[:, half, :], A["xT"][:, half, :]).then_inc(x_in[part], 16)
            act.wait_ge(consts_made, 1)
            for k in range(KT):
                act.wait_ge(x_in[k // (KT // 2)], 16)
                square(k, "attn0", x[:, k, :])

            def memory(l):
                for j in range(2):
                    move(f"mk{l}.{j}", k_mem[:, l, j, :], of(f"mk{l}.{j}")[:, 0:N_MEM])
                move(f"mv{l}", v_mem[:, l, :, :], of(f"mv{l}")[:, :].rearrange("p (a n) -> p a n", a=2))

            deviation("sum.attn0")
            split_ahead(-1)
            round_norm("attn0", h_hi)
            product("ckv")
            nc.scalar.activation(ckv[:, :], of("ckv")[:, :], ACT.Copy).then_inc(act_step, 1)
            nc.scalar.activation(sq[:, 0, :], of("ckv")[:, :], ACT.Square).then_inc(evacuated[JOB["ckv"] % 2], 1)
            move("kidx", kidx[:, :])
            deviation("ckvsum", scale=float(D // RANK))
            move("qidx0", qidx[:, 0, :])
            act.wait_ge(mem_in, 16)
            for k in range(KT):
                square(k, "mem", memx[:, k, :], N_MEM)
            move("qidx1", qidx[:, 1, :])
            deviation("memsum", N_MEM)
            for l in range(DEPTH):
                move(f"qidx{l + 2}", qidx[:, l + 2, :])
                round_norm(f"mem{l}", mem_hi[l], N_MEM)
            move("widx", widx_f, scale=IDX_HEADS ** -0.5 * IDX_DIM ** -0.5)
            move("dsa_k", dsa_k[:, :])
            move("widxT", widx[:, :, :], of("widxT")[:, :].rearrange("p (a n) -> p a n", a=TT)[:, :, 0:IDX_HEADS])
            move("dsa_v", dsa_v[:, :, :], of("dsa_v")[:, 0:TT * HD].rearrange("p (a n) -> p a n", a=TT))
            wait_evacuated(act, "widxT")
            index_logits(1)
            act.wait_ge(roped, 6)
            nc.scalar.activation(k_dsa[0][:, :], dsa_k[:, :], ACT.Copy).then_inc(k_rounded, 1)
            for j in range(3):
                move(f"q0.{j}", q0[:, j, :], scale=SCALE)
            index_logits(2)
            for j in range(3, 6):
                move(f"q0.{j}", q0[:, j, :], scale=SCALE)
            memory(0)
            index_logits(3)
            for j in range(6):
                act.wait_ge(roped, 7 + j)
                round_queries("dsa", j, q0[:, j, :])
            for j in range(2):
                move(f"qmem0.{j}", qmem0[:, j, :], scale=SCALE)
            memory(1)
            attention_stream(act, STREAMS[0], attention_begin, pair_of_heads)
            for l in range(DEPTH):
                if l == 1:
                    wait_product(act, f"down0.{KT - 1}")
                    for c in range(2):
                        act.dma_start(cmp_w1[c][:, :, :], A["cmp_w1"][c]).then_inc(cmp_in, 16)
                        act.dma_start(cmp_pos[c][:, :], A["cmp_pos"][c]).then_inc(cmp_in, 16)
                    act.dma_start(cmp_w2k[:, :], A["cmp_w2k"]).then_inc(cmp_in, 16)
                    act.dma_start(cmp_w2v[:, :], A["cmp_w2v"]).then_inc(cmp_in, 16)
                    deviation("sum.attn1")
                    round_norm("attn1", h_hi)
                    for name in ("kc0", "kc1", "vc0", "vc1"):
                        split_ahead(CHUNK[name])
                    for g in range(2):
                        move(f"ks{g}", k_raw[:, g, :])
                    for g in range(2):
                        move(f"kw{g}", k_raw[:, 2 + g, :])
                    move("cmp_hk", cmp_hk[:, :], of("cmp_hk")[:, 0:2 * N_CMP], ACT.Gelu_apprx_tanh)
                    hidden = of("cmp_hv")[:, 0:2 * N_CMP].rearrange("p (g c) -> p g c", g=2)
                    move("cmp_hv", cmp_hv[:, :, :, 0:N_CMP], hidden.unsqueeze(2).to_broadcast([P, 2, TT, N_CMP]), ACT.Gelu_apprx_tanh)
                    move("cmp_k", k_cmp[:, :], of("cmp_k")[:, 0:2 * N_CMP])
                    product("cmp_v")
                    for a in range(TT):
                        rows = slice(32 * a, 32 * a + 32)
                        r = nc.scalar.activation(v_cmp[rows, :, a * HD:(a + 1) * HD],
                                                 of("cmp_v")[rows, 0:2 * HD].rearrange("p (g n) -> p g n", g=2), ACT.Copy)
                    r.then_inc(evacuated[JOB["cmp_v"] % 2], 1)
                    for n in range(4):
                        act.wait_ge(roped, 13 + n)
                        nc.scalar.activation(k_nsa[0][:, n, :], k_raw[:, n, :], ACT.Copy).then_inc(k_rounded, 1)

                    def round_rotated(j):
                        act.wait_ge(roped, 17 + j)
                        round_queries("nsa0", j, q1r[:, j % 2, :])

                    for j in range(6):
                        move(f"q1.{j}", q1[:, j, :], scale=SCALE)
                        if j >= 2:
                            round_rotated(j - 2)
                    move("vsw.a", v_nsa[:, 0:2, :], of("vsw.a")[:, :].rearrange("p (a n) -> p a n", a=2))
                    round_rotated(4)
                    move("vsw.b", v_nsa[:, 2:4, :], of("vsw.b")[:, :].rearrange("p (a n) -> p a n", a=2))
                    round_rotated(5)
                    move("gates", diag[:, :], func=ACT.Sigmoid)
                    move("qmem1.0", qmem1[:, 0, :], scale=SCALE)
                    move("gatesT", gates[:, :, :], of("gatesT")[:, :].rearrange("p (a n) -> p a n", a=TT)[:, :, 0:3 * TOK_HEADS])
                    move("qmem1.1", qmem1[:, 1, :], scale=SCALE)
                    attention_stream(act, STREAMS[1], attention_begin, pair_of_heads)
                concat(f"cat{l}", l)
                for j in range(KT):
                    split_ahead(CHUNK[f"wo{l}.{j}"])
                    wait_evacuated(act, f"wo{l}.{j}")
                    square(j, f"ffn{l}", x[:, j, :])
                deviation(f"sum.ffn{l}")
                round_norm(f"ffn{l}", h_hi)
                up_gated(l)
                down(f"down{l}", 3, 4, "attn1" if l == 0 else "final", x)
            deviation("sum.final")
            act.dma_start(w_gate[:, :], A["w_gate"]).then_inc(gla_in, 16)
            act.dma_start(gla_mask[:, :], A["gla_mask"]).then_inc(gla_in, 16)
            round_norm("mixpre0", h_hi)
            move("glr", glr[:, :])
            for h in range(4):
                move(f"gk{h}", gk[:, h, :])
            for h in range(4):
                move(f"gq{h}", gq[:, h, :])
            for h in range(4):
                product(f"gz{h}")
                if h:
                    act.wait_ge(g_cummed, 2 * h)
                nc.scalar.activation(g_ab[:, :], of(f"gz{h}")[:, :], ACT.Abs, bias=col(f"gla_b{h}")).then_inc(g_absed, 1)
                act.wait_ge(g_absed, h + 1)
                nc.scalar.activation(g_ab[:, :], g_ab[:, :], ACT.Exp, scale=-1.0).then_inc(act_step, 1)
                act.wait_ge(act_step, 2 + h)
                nc.scalar.activation(g_ab[:, :], g_ab[:, :], ACT.Ln, bias=1.0).then_inc(g_logged, 1)
                name = f"gv{h}.a"
                move(name, gv[:, 0:2, 2 * h * P:(2 * h + 2) * P], of(name)[:, :].rearrange("p (a n) -> p a n", a=2))
                act.wait_ge(g_cummed, 2 * h + 2)
                act.wait_ge(g_gated, 3 * h)
                nc.scalar.activation(g_exp[:, :], g_cum[:, :], ACT.Exp, scale=1.0 / GATE_NORM).then_inc(g_exped, 1)
                nc.scalar.activation(g_inv[:, :], g_cum[:, :], ACT.Exp, scale=-1.0 / GATE_NORM).then_inc(g_exped, 1)
                act.wait_ge(g_diffed, h + 1)
                nc.scalar.activation(g_end[:, :], g_end[:, :], ACT.Exp, scale=1.0 / GATE_NORM).then_inc(g_exped, 1)
                name = f"gv{h}.b"
                move(name, gv[:, 2:4, 2 * h * P:(2 * h + 2) * P], of(name)[:, :].rearrange("p (a n) -> p a n", a=2))
            for stage, h in GLA_STAGES:
                if stage == "gate":
                    move(f"gg{h}", gsilu[:, h, :], func=ACT.Silu)
                elif stage == "scores":
                    name = f"gket{h}"
                    move(name, k_endT[:, h % 2, :, :], of(name)[:, :].rearrange("p (a n) -> p a n", a=TT))
                elif stage == "outputs":
                    for j in range(2):
                        name = f"go{h}.{j}"
                        product(name)
                        if h:
                            wait_product(act, f"gosum{h - 1}")
                        nc.scalar.activation(g_o[j][:, h, :], of(name)[:, :], ACT.Copy).then_inc(act_step, 1)
                        nc.scalar.activation(sq[:, j, :], of(name)[:, :], ACT.Square).then_inc(evacuated[JOB[name] % 2], 1)
                elif stage == "sum":
                    deviation(f"gosum{h}", scale=float(KT // 2))
                elif stage == "split":
                    wait_product(act, f"gg{KT - 1}")
                    for j in range(2):
                        act.wait_ge(go_made, 2 * h + j + 1)
                        nc.scalar.activation(h_hi[:, 2 * h + j, :], gsilu[:, 2 * h + j, :], ACT.Copy).then_inc(go_rounded, 1)
            for l in range(DEPTH):
                if l == 1:
                    split_ahead(CHUNK["sq0"])
                    act.wait_ge(late_sum, 1)
                    nc.scalar.activation(root[:, :], late_sum_bank[:, 0:TT], ACT.Sqrt, bias=eps[:, 0:1]).then_inc(root_ready, 1)
                    for j in range(KT):
                        split_ahead(CHUNK[f"sq{j}"])
                        act.wait_ge(swa_biased, j + 1)
                        round_queries("swa0", j, sq_q[:, j, :])
                    for g in range(2):
                        split_ahead(CHUNK[f"sk{g}"])
                        act.wait_ge(swa_biased, KT + 2 + g)
                        nc.scalar.activation(k_swa[0][:, g, :], sk[:, g, :], ACT.Copy).then_inc(k_rounded, 1)
                    move("svT", sv[:, :, :], of("svT")[:, :].rearrange("p (a n) -> p a n", a=TT))
                    attention_stream(act, STREAMS[2], attention_begin, pair_of_heads)
                    concat("scat", 2)
                for j in range(KT):
                    split_ahead(CHUNK[f"mix{l}.{j}"])
                    wait_evacuated(act, f"mix{l}.{j}")
                    square(j, f"mixpost{l}", m[:, j, :])
                deviation(f"sum.mixpost{l}")
                round_gained(f"mlppre{l}", KT * l)
                for half in range(2):
                    up_relu(l, half)
                    down(f"mdown{l}{half}", 2, 2, *((f"mlppost{l}", m) if half else (f"mlppre{l}", x)))
                deviation(f"sum.mlppost{l}")
                if l == 0:
                    round_gained("mixpre1", KT // 2)
                    for k in range(KT):
                        square(k, "mixpre1", x[:, k, :])
                else:
                    for k in range(KT):
                        act.wait_ge(x_added[k % 2], KT * l + KT // 2 + k // 2 + 1)
                        act.dma_start(A["out"][k], x[:, k, :]).then_inc(stored, 16)
            act.wait_ge(stored, 16 * KT)

        @block.vector
        def _(dve):
            steps = [0]

            def step(ins):
                steps[0] += 1
                ins.then_inc(dve_step, 1)
                dve.wait_ge(dve_step, steps[0])

            def zero_sum(name):
                nc.vector.memset(sqacc[:, :], 0.0).then_inc(sq_added, 1)

            def add_square(k, name, n=SEQ, per=0, i=0):
                b = SUMS.index(name)
                dve.wait_ge(sq_done, KT * b + k + 1 + per * i)
                dve.wait_ge(sq_added, 9 * b + k + 1 + per * i)
                nc.vector.tensor_tensor(sqacc[:, 0:n], sqacc[:, 0:n], sq[:, k % 2, 0:n], ALU.add).then_inc(sq_added, 1)

            def roots_on_diagonal(job, n=SEQ):
                a = n // P
                if job[4:] in ROOTED:
                    wait_product(dve, job)
                    nc.vector.tensor_tensor(inv_root[:, :], of(job)[:, 0:TT], eps_out[:, :], ALU.add).then_inc(evacuated[JOB[job] % 2], 1)
                    dve.wait_ge(root_ready, ROOTED.index(job[4:]) + 1)
                wait_evacuated(dve, job)
                step(nc.vector.reciprocal(inv_root[:, 0:a], root[:, 0:a]))
                on_diagonal(inv_root, a)

            def on_diagonal(by_token, a=TT):
                nc.vector.scalar_tensor_tensor(diag[:, 0:a * P].rearrange("p (a n) -> p a n", a=a), ident[:, :].unsqueeze(1).to_broadcast([P, a, P]),
                                               float(D), by_token[:, 0:a].unsqueeze(2).to_broadcast([P, a, P]), ALU.mult, ALU.mult).then_inc(diag_ready, 1)

            def roots_of_two_norms():
                job = "sum.final"
                wait_product(dve, job)
                step(nc.vector.tensor_scalar(mean_sq[:, :], of(job)[:, 0:TT], EPS, None, ALU.add))
                step(nc.vector.reciprocal(mean_sq[:, :], mean_sq[:, :]))
                nc.vector.tensor_copy(oscale[:, 0:TT], of(job)[:, 0:TT])
                nc.vector.tensor_tensor(oscale[:, TT:2 * TT], of(job)[:, TT:2 * TT], mean_sq[:, :], ALU.mult).then_inc(evacuated[JOB[job] % 2], 1)
                dve.wait_ge(root_ready, ROOTED.index("final") + 1)
                step(nc.vector.reciprocal(oscale[:, 0:2 * TT], rinv[:, 0:2 * TT]))
                step(nc.vector.tensor_tensor(mean_sq[:, :], oscale[:, 0:TT], oscale[:, TT:2 * TT], ALU.mult))
                on_diagonal(mean_sq)

            def inverse(job, n=SEQ):
                roots_on_diagonal(job, n)
                wait_product(dve, inverse_of(job))
                return of(inverse_of(job))[:, 0:n]

            def release(job):
                dve.sem_inc(evacuated[JOB[inverse_of(job)] % 2], 1)

            def norm(name, src, hi, lo, rstd, n=SEQ):
                b = NORMS.index(name)

                def whole(k):
                    if k >= 4:
                        dve.wait_ge(h_ready[k % 2], KT // 2 * b + k // 2 - 1)
                    nc.vector.scalar_tensor_tensor(norm_tile(k)[:, 0:n], src[:, k, :], both_gains[:, k:k + 1] if name == "mixpre0" else col(name, k),
                                                   rstd, ALU.mult, ALU.mult).then_inc(h_made, 1)

                if b:
                    for part in range(2):
                        dve.wait_ge(h_ready[part], KT // 2 * b)
                whole(0)
                whole(1)
                for k in range(0, KT, 2):
                    if k + 2 < KT:
                        whole(k + 2)
                    dve.wait_ge(h_rounded, KT * b + k + 1)
                    nc.vector.tensor_tensor(lo[:, k, :], norm_tile(k)[:, 0:n], hi[:, k, :].bitcast(F32), ALU.subtract).then_inc(h_ready[0], 1)
                    if k + 2 < KT:
                        whole(k + 3)
                dve.wait_ge(h_made, KT * (b + 1))

            def rope(name):
                raw, out, t = rope_tile(name)
                wait_evacuated(dve, name)
                if ROPES.index(name):
                    dve.wait_ge(roped, ROPES.index(name))
                nc.vector.tensor_tensor(t[:, 0, :], raw, rope_c[:, :], ALU.mult).then_inc(dve_step, 1)
                steps[0] += 1
                job = f"rope.{name}"
                wait_product(dve, job)
                nc.vector.tensor_tensor(t[:, 1, :], of(job)[:, :], rope_s[:, :], ALU.mult).then_inc(evacuated[JOB[job] % 2], 1)
                dve.wait_ge(dve_step, steps[0])
                wait_evacuated(dve, job)
                nc.vector.tensor_tensor(out, t[:, 0, :], t[:, 1, :], ALU.add).then_inc(roped, 1)

            def index_top(qt):
                n = (qt + 1) * P
                tile = score[:, qt % 2, 0:n]
                if qt:
                    dve.wait_ge(idx_added, qt * IDX_HEADS)
                    for _ in range(TOPK // 8):
                        step(nc.vector.max(top8[:, :], tile))
                        step(nc.vector.match_replace(tile, top8[:, :], tile, -3e38))
                    nc.vector.tensor_scalar(dsa_mask[:, qt, 0:n], tile, -2e38, NEG, ALU.is_gt, ALU.mult).then_inc(dsa_masked, 1)
                else:
                    nc.vector.tensor_copy(dsa_mask[:, 0, 0:P], masks[:, P:2 * P]).then_inc(dsa_masked, 1)

            def rest_of_queries(kind, j, tile):
                dve.wait_ge(q_rounded, 2 * (split_queries(kind)[2] + j) + 2)
                for part, hi, lo in both_heads(kind, j, tile):
                    nc.vector.tensor_tensor(lo, part, hi.bitcast(F32), ALU.subtract).then_inc(q_split, 1)

            def rest_of_keys(n, raw, hi, lo):
                dve.wait_ge(k_rounded, n + 1)
                nc.vector.tensor_tensor(lo, raw, hi.bitcast(F32), ALU.subtract).then_inc(k_split, 1)

            def maximum(kind, pair, u, i):
                _, qt, br = attention_unit(kind, u)
                per, group = PER_PAIR[kind], int(kind[3]) if kind[3:] else 0
                g, s4 = UNIT0[kind] + pair * per + u, slot_of(kind, u)
                dve.wait_ge(scores_ready, g + 1 + per * i)
                if compressed(kind, u):
                    src = score_bank[bank_of(kind, u)][:, 0:P].rearrange("p (a c) -> p a c", a=TT)
                    r0 = 2 * (6 * group + u // 9)
                    nc.vector.tensor_reduce(c_max[:, :, 0], src, AX.X, ALU.max).then_inc(rawmax_ready, 1)
                    dve.wait_ge(rawmax_ready, r0 + 1 + 4 * i)
                    nc.vector.tensor_scalar(c_max[:, :, 0], c_max[:, :, 0], NEG / 10, None, ALU.max).then_inc(rawmax_ready, 1)
                    dve.wait_ge(rawmax_ready, r0 + 2 + 4 * i)
                    nc.vector.tensor_tensor(c_shift[:, :, :], src, c_max[:, :, :].to_broadcast([P, TT, 32]), ALU.subtract).then_inc(max_ready, 1)
                    return
                src = score_bank[bank_of(kind, u)][:, 0:P * len(key_tiles(kind, qt, br))]
                if kind.startswith("swa"):
                    r0 = 24 + g - UNIT0["swa0"]
                    nc.vector.tensor_reduce(rawmax[:, s4:s4 + 1], src, AX.X, ALU.max, negate=True).then_inc(rawmax_ready, 1)
                    dve.wait_ge(rawmax_ready, r0 + 1 + per * i)
                    head = 8 * group + u // 4 + 2 * i
                    nc.vector.tensor_tensor(nmax[:, s4:s4 + 1], rawmax[:, s4:s4 + 1], nsinks[:, bass.ds(head, 1)], ALU.min).then_inc(max_ready, 1)
                    if u % TT == TT - 1:
                        four = slice(s4 - TT + 1, s4 + 1)
                        dve.wait_ge(max_ready, g + 1 + per * i)
                        nc.vector.tensor_scalar(sink_shift[:, four], nmax[:, four], sinks[:, bass.ds(head, 1)], None, ALU.add).then_inc(sink_shifted, 1)
                else:
                    nc.vector.tensor_reduce(nmax[:, s4:s4 + 1], src, AX.X, ALU.max, negate=True).then_inc(max_ready, 1)

            def move_transposed(kind, pair, u, i):
                _, qt, br = attention_unit(kind, u)
                per = PER_PAIR[kind]
                g, n = UNIT0[kind] + pair * per + u, P if compressed(kind, u) else P * len(key_tiles(kind, qt, br))
                dve.wait_ge(transposed, g + 3 + per * i)
                dve.wait_ge(pv_done, g + 1 + per * i)
                nc.vector.tensor_copy(probT[:, g % 2, 0:n], probT_bank[g % 2][:, 0:n]).then_inc(probT_ready[g % 2], 1)

            def output(kind, pair, u, i):
                hh, qt, br = attention_unit(kind, u)
                per, o_tok, group = PER_PAIR[kind], output_of(kind), int(kind[3]) if kind[3:] else 0
                g, s4 = UNIT0[kind] + pair * per + u, slot_of(kind, u)
                nsa, swa = kind.startswith("nsa"), kind.startswith("swa")
                out = o_bank[g // TT % 2] if swa else o_bank[g % 2]
                if kind.startswith("mem"):
                    c = (TOK_HEADS + 2 * pair + hh) * HD
                    of_head = slice(c, c + HD)
                else:
                    of_head = bass.ds(((6 if nsa else 8) * group + hh) * HD + P * i, HD)
                gate, gate2 = (bass.ds((6 * group + hh) * 3 + br + 6 * i, n) for n in (1, 2))
                r1 = g if g < UNIT0["nsa0"] else g - (UNIT0["mem1"] - UNIT0["nsa0"])
                if compressed(kind, u):
                    r0 = 6 * group + u // 9
                    dve.wait_ge(pv_done, g + 3 + per * i)
                    nc.vector.tensor_scalar(c_scale[:, :, 0], out[:, TT * HD:TT * HD + TT], 1e-30, None, ALU.max).then_inc(sum_ready, 1)
                    dve.wait_ge(sum_ready, r0 + 1 + 2 * i)
                    r2 = 10 * (3 * group) + 5 * (u // 9)
                    nc.vector.reciprocal(c_scale[:, :, 0], c_scale[:, :, 0]).then_inc(oscale_ready, 1)
                    dve.wait_ge(oscale_ready, 2 * r2 + 1 + 20 * i)
                    nc.vector.tensor_tensor(c_scale[:, :, :], c_scale[:, :, :], gates[:, :, gate], ALU.mult).then_inc(oscale_ready, 1)
                    dve.wait_ge(oscale_ready, 2 * r2 + 2 + 20 * i)
                    nc.vector.tensor_tensor(o_tok[:, :, of_head], out[:, 0:TT * HD].rearrange("p (a n) -> p a n", a=TT),
                                            c_scale[:, :, :].to_broadcast([P, TT, HD]), ALU.mult).then_inc(o_done, 1)
                    return
                if swa:
                    four = slice(s4 - TT + 2, s4 + 2) if u % TT == TT - 2 else slice(s4 - TT + 1, s4 + 1)
                    head = heads_before(kind, u)
                    if u % TT == TT - 2:
                        dve.wait_ge(sum_ready, 12 + head + 1 + 2 * i)
                        nc.vector.reciprocal(rinv[:, four], oscale[:, four]).then_inc(rinv_ready, 1)
                    if u % TT == TT - 1:
                        dve.wait_ge(rinv_ready, UNIT0["swa0"] - (UNIT0["mem1"] - UNIT0["nsa0"]) + head + 1 + 2 * i)
                        dve.wait_ge(pv_done, g + 3 + per * i)
                        nc.vector.tensor_tensor(o_tok[:, :, of_head], out[:, 0:TT * HD].rearrange("p (a n) -> p a n", a=TT),
                                                rinv[:, four].rearrange("p (a b) -> p a b", b=1).to_broadcast([P, TT, HD]),
                                                ALU.mult).then_inc(o_done, TT)
                    return
                dve.wait_ge(probs_ready, g + 3 + per * i)
                if not nsa:
                    nc.vector.reciprocal(rinv[:, s4:s4 + 1], psum_p[:, s4:s4 + 1]).then_inc(rinv_ready, 1)
                    dve.wait_ge(rinv_ready, r1 + 1 + per * i)
                    factor = rinv[:, s4:s4 + 1]
                else:
                    factor = oscale[:, s4:s4 + 1]
                    if br == 1:
                        r2 = 10 * (3 * group) + 5 * (u // 9) + (u % 9 + 1) // 2
                        dve.wait_ge(probs_ready, g + 4 + per * i)
                        nc.vector.reciprocal(rinv[:, s4:s4 + 2], psum_p[:, s4:s4 + 2]).then_inc(oscale_ready, 1)
                        dve.wait_ge(oscale_ready, 2 * r2 + 1 + 20 * i)
                        nc.vector.tensor_tensor(oscale[:, s4:s4 + 2], rinv[:, s4:s4 + 2], gates[:, qt, gate2], ALU.mult).then_inc(oscale_ready, 1)
                        dve.wait_ge(oscale_ready, 2 * r2 + 2 + 20 * i)
                dve.wait_ge(pv_done, g + 3 + per * i)
                if nsa:
                    dve.wait_ge(o_done, g + 2 + per * i)
                    nc.vector.scalar_tensor_tensor(o_tok[:, qt, of_head], out[:, 0:HD], factor, o_tok[:, qt, of_head], ALU.mult, ALU.add).then_inc(o_done, 1)
                else:
                    nc.vector.tensor_scalar(o_tok[:, qt, of_head], out[:, 0:HD], factor, None, ALU.mult).then_inc(o_done, 1)

            def attention_begin(at):
                for u in range(4):
                    maximum(*at(u))
                if moved_by_vector(at(1)[0], 1):
                    move_transposed(*at(1))

            def pair_of_heads(per, at):
                for u in range(per):
                    if at(u + 4):
                        maximum(*at(u + 4))
                    if at(u + 2) and moved_by_vector(at(u + 2)[0], at(u + 2)[2]):
                        move_transposed(*at(u + 2))
                    output(*at(u))

            def concat(prefix, n):
                for j in range(KT):
                    name = f"{prefix}.{j}"
                    dve.wait_ge(cat_rounded, KT * n + j + 1)
                    nc.vector.tensor_tensor(h_lo[:, j, :], of(name)[:, :], h_hi[:, j, :].bitcast(F32), ALU.subtract).then_inc(evacuated[JOB[name] % 2], 1)

            def up_gated(l):
                n0, t0 = JOB[f"up{l}.0"], CHUNK[f"up{l}.0"]
                with dve.Fori(0, FT // 2) as i:
                    for f in range(2):
                        c = FT * l + f
                        b = n0 + 2 * f + 1
                        dve.wait_ge(chunks_used, t0 + 2 * f + 2 + 4 * i)
                        dve.wait_ge(evacuated[(b - 1) % 2], (b - 1) // 2 + 1 + 2 * i)
                        nc.vector.tensor_tensor(tmp[:, f, :], sq[:, f, :], bank[b % 2][:, :], ALU.mult).then_inc(act_made, 1)
                        dve.wait_ge(act_made, c + 1 + 2 * i)
                        dve.sem_inc(evacuated[b % 2], 1)
                        dve.wait_ge(act_rounded, c + 1 + 2 * i)
                        j = bass.ds(2 * i + f, 1)
                        nc.vector.tensor_tensor(act_lo[:, j, :].rearrange("p a n -> p (a n)"), tmp[:, f, :],
                                                act_hi[:, j, :].rearrange("p a n -> p (a n)").bitcast(F32), ALU.subtract).then_inc(act_ready, 1)

            def up_relu(l, half):
                n0, t0 = JOB[f"mup{l}{half}.0"], CHUNK[f"mup{l}{half}.0"]
                c0, r0 = 2 * FT + HALF_FT * (2 * l + half), HALF_FT * (2 * l + half)
                with dve.Fori(0, HALF_FT // 4) as i:
                    for f in range(4):
                        b = n0 + f
                        dve.wait_ge(relu_done, r0 + f + 1 + 4 * i)
                        nc.vector.tensor_tensor(tmp[:, f % 2, :], sq[:, f % 2, :], bank[b % 2][:, :], ALU.mult).then_inc(act_made, 1)
                        dve.wait_ge(act_made, c0 + f + 1 + 4 * i)
                        dve.sem_inc(evacuated[b % 2], 1)
                        dve.wait_ge(act_rounded, c0 + f + 1 + 4 * i)
                        j = bass.ds(4 * i + f, 1)
                        nc.vector.tensor_tensor(mact_lo[:, j, :].rearrange("p a n -> p (a n)"), tmp[:, f % 2, :],
                                                mact_hi[:, j, :].rearrange("p a n -> p (a n)").bitcast(F32), ALU.subtract).then_inc(act_ready, 1)

            def down(prefix, per_tile, step_, name, dst, add):
                n0, t0 = JOB[f"{prefix}.0"], CHUNK[f"{prefix}.0"]
                zero_sum(name)
                if name == "final":
                    nc.vector.memset(spare[:, :], 0.0).then_inc(gained_sq_added, 2)
                with dve.Fori(0, KT // step_) as i:
                    for j in range(step_):
                        b = bank[(n0 + j) % 2][:, :]
                        d = dst[:, bass.ds(step_ * i + j, 1), :].rearrange("p a n -> p (a n)")
                        dve.wait_ge(chunks_used, t0 + (j + 1) * per_tile + step_ * per_tile * i)
                        ins = nc.vector.tensor_tensor(d, d, b, ALU.add) if add else nc.vector.tensor_copy(d, b)
                        ins.then_inc(evacuated[(n0 + j) % 2], 1)
                        add_square(j, name, per=step_, i=i)
                        if name == "final":
                            dve.wait_ge(gained_sq_done, j + 1 + step_ * i)
                            dve.wait_ge(gained_sq_added, j + 2 + step_ * i)
                            nc.vector.tensor_tensor(spare[:, :], spare[:, :], tmp[:, j % 2, :], ALU.add).then_inc(gained_sq_added, 1)

            dve.sem_inc(o_done, 2)
            dve.sem_inc(probT_ready[1], 1)
            nc.vector.memset(ones[:, :], 1.0 / D)
            nc.vector.memset(eps[:, :], EPS)
            dve.sem_inc(consts_made, 1)
            zero_sum("attn0")
            for k in range(KT):
                add_square(k, "attn0")
            dve.wait_ge(consts_in, 144)
            norm("attn0", x, h_hi, h_lo, inverse("sum.attn0"))
            release("sum.attn0")
            of_final, of_next = (slice(GAINS.index(n) * KT, (GAINS.index(n) + 1) * KT) for n in ("final", "mixpre0"))
            nc.vector.tensor_tensor(both_gains[:, :], cols[:, of_final], cols[:, of_next], ALU.mult)
            nc.vector.tensor_copy(ident_b[:, :], ident[:, :])
            nc.vector.tensor_copy(masks_b[:, :], masks[:, :])
            nc.vector.tensor_scalar(nsinks[:, :], sinks[:, :], -1.0, None, ALU.mult).then_inc(consts_made, 1)
            index_top(0)
            rstd = inverse("ckvsum")
            nc.vector.scalar_tensor_tensor(ckv_n[:, :], ckv[:, :], col("ckv"), rstd, ALU.mult, ALU.mult).then_inc(ckv_normed, 1)
            dve.wait_ge(ckv_normed, 1)
            release("ckvsum")
            rope("kidx")
            zero_sum("mem")
            for k in range(KT):
                add_square(k, "mem", N_MEM)
            roots_on_diagonal("memsum", N_MEM)
            rope("qidx0")
            wait_product(dve, "meminv")
            step(nc.vector.tensor_copy(spare[:, 0:N_MEM], of("meminv")[:, 0:N_MEM]))
            release("memsum")
            for l in range(DEPTH):
                rope(f"qidx{l + 1}")
                dve.wait_ge(roped, ROPES.index(f"qidx{l + 1}") + 1)
                norm(f"mem{l}", memx, mem_hi[l], mem_lo[l], spare[:, 0:N_MEM], N_MEM)
                for part in range(2):
                    dve.wait_ge(h_ready[part], KT // 2 * (NORMS.index(f"mem{l}") + 1))
            for name in ROPES[4:6]:
                rope(name)
            index_top(1)
            rest_of_keys(0, dsa_k[:, :], k_dsa[0][:, :], k_dsa[1][:, :])
            index_top(2)
            for j in range(6):
                rope(f"q0.{j}")
            index_top(3)
            dve.wait_ge(roped, 12)
            attention_stream(dve, STREAMS[0], attention_begin, pair_of_heads)
            for l in range(DEPTH):
                if l == 1:
                    norm("attn1", x, h_hi, h_lo, inverse("sum.attn1"))
                    release("sum.attn1")
                    nc.vector.memset(cmp_hv[:, :, :, N_CMP:32], 0.0)
                    step(nc.vector.memset(v_cmp[:, :, :], 0.0))
                    for a in range(TT):
                        nc.vector.memset(v_cmp[32 * a:32 * a + 32, :, TT * HD + a:TT * HD + a + 1], 1.0)
                    dve.wait_ge(cmp_in, 96)
                    for c, s_ in enumerate("kv"):
                        for g in range(2):
                            name = f"{s_}c{g}"
                            wait_product(dve, name)
                            src = of(name)
                            for half in range(2):
                                rows = slice(HD * half, HD * half + HD)
                                tok = src[rows, half:half + 16 * (N_CMP - 1) + 2 * (CMP_PAIRS - 1) + 1]
                                out = cmp_x[c][rows, :, g, :]
                                pos = cmp_pos[c][rows, :].unsqueeze(2).to_broadcast([HD, CMP_PAIRS, N_CMP])
                                win = bass.AP(tok.tensor, tok.offset, [tok.ap[0], [2, CMP_PAIRS], [16, N_CMP]])
                                ins = nc.vector.tensor_tensor(out, win, pos, ALU.add)
                                ins.then_inc(cmp_built, 1)
                            dve.wait_ge(cmp_built, 4 * c + 2 * g + 2)
                            dve.sem_inc(evacuated[JOB[name] % 2], 1)
                    for name in ROPES[12:16]:
                        rope(name)
                    for n in range(4):
                        rest_of_keys(1 + n, k_raw[:, n, :], k_nsa[0][:, n, :], k_nsa[1][:, n, :])
                    for j in range(6):
                        rope(f"q1.{j}")
                        if j:
                            rest_of_queries("nsa0", j - 1, q1r[:, (j - 1) % 2, :])
                    rest_of_queries("nsa0", 5, q1r[:, 5 % 2, :])
                    wait_evacuated(dve, "gatesT")
                    dve.wait_ge(roped, len(ROPES))
                    attention_stream(dve, STREAMS[1], attention_begin, pair_of_heads)
                concat(f"cat{l}", l)
                zero_sum(f"ffn{l}")
                for j in range(KT):
                    name = f"wo{l}.{j}"
                    wait_product(dve, name)
                    nc.vector.tensor_tensor(x[:, j, :], x[:, j, :], of(name)[:, :], ALU.add).then_inc(evacuated[JOB[name] % 2], 1)
                    add_square(j, f"ffn{l}")
                norm(f"ffn{l}", x, h_hi, h_lo, inverse(f"sum.ffn{l}"))
                release(f"sum.ffn{l}")
                up_gated(l)
                down(f"down{l}", 3, 4, "attn1" if l == 0 else "final", x, True)
            roots_of_two_norms()
            wait_product(dve, "inv.final")
            norm("mixpre0", x, h_hi, h_lo, of("inv.final")[:, :])
            release("sum.final")
            on_diagonal(oscale)
            wait_product(dve, "inv.x")
            for k in range(KT):
                nc.vector.scalar_tensor_tensor(x[:, k, :], x[:, k, :], col("final", k), of("inv.x")[:, :], ALU.mult, ALU.mult).then_inc(x_normed, 1)
            dve.wait_ge(x_normed, KT)
            release("inv.x")
            step(nc.vector.memset(g_reset[:, :], 1.0))
            step(nc.vector.memset(g_reset[:, :].rearrange("p (n c) -> p n c", c=GLA_CHUNK)[:, :, 0:1], 0.0))
            for h in range(4):
                name = f"gz{h}"
                dve.wait_ge(g_absed, h + 1)
                nc.vector.tensor_scalar(g_la[:, :], of(name)[:, :], col(f"gla_b{h}"), 0.0, ALU.add, ALU.min).then_inc(evacuated[JOB[name] % 2], 1)
                wait_evacuated(dve, name)
                dve.wait_ge(g_logged, h + 1)
                nc.vector.tensor_tensor(g_la[:, :], g_la[:, :], g_ab[:, :], ALU.subtract).then_inc(g_cummed, 1)
                dve.wait_ge(g_cummed, 2 * h + 1)
                nc.vector.tensor_tensor_scan(g_cum[:, :], g_reset[:, :], g_la[:, :], 0.0, ALU.mult, ALU.add).then_inc(g_cummed, 1)
                dve.wait_ge(g_cummed, 2 * h + 2)
                cum = g_cum[:, :].rearrange("p (n c) -> p n c", c=GLA_CHUNK)
                last = cum[:, :, GLA_CHUNK - 1:GLA_CHUNK].to_broadcast([P, N_CHUNK, GLA_CHUNK])
                nc.vector.tensor_tensor(g_end[:, :].rearrange("p (n c) -> p n c", c=GLA_CHUNK), last, cum, ALU.subtract).then_inc(g_diffed, 1)
                dve.wait_ge(g_exped, 3 * h + 2)
                wait_evacuated(dve, f"gq{h}")
                nc.vector.tensor_copy(decay[:, h, :], g_exp[:, :].rearrange("p (n c) -> p n c", c=GLA_CHUNK)[:, :, GLA_CHUNK - 1])
                nc.vector.scalar_tensor_tensor(gq[:, h, :], gq[:, h, :], float(P) ** -0.5, g_exp[:, :], ALU.mult, ALU.mult).then_inc(g_gated, 1)
                nc.vector.tensor_tensor(k_inv[:, h, :], gk[:, h, :], g_inv[:, :], ALU.mult).then_inc(g_gated, 1)
                dve.wait_ge(g_exped, 3 * h + 3)
                nc.vector.tensor_tensor(gk[:, h, :], gk[:, h, :], g_end[:, :], ALU.mult).then_inc(g_gated, 1)
            dve.wait_ge(g_gated, 12)
            dve.wait_ge(gla_in, 32)
            step(nc.vector.memset(attT[:, :, :, :], 0.0))

            def gla_scores(h):
                name = f"gatt{h}"
                wait_product(dve, name)
                nc.vector.copy_predicated(attT[:, h % 2, :, :], gla_mask[:, :].unsqueeze(1).to_broadcast([P, TT, P]),
                                          of(name)[:, :].rearrange("p (a n) -> p a n", a=TT)).then_inc(evacuated[JOB[name] % 2], 1)
                for n in range(N_CHUNK - 1):
                    if n < N_CHUNK - 2:
                        dve.wait_ge(gds_ready, (N_CHUNK - 2) * h + n + 1)
                    else:
                        wait_product(dve, f"gds{h}")
                    if n:
                        dve.wait_ge(state_made, (N_CHUNK - 2) * h + n)
                        ins = nc.vector.scalar_tensor_tensor(state[:, h % 2, n + 1, :], state[:, h % 2, n, :], decay[:, h, n:n + 1], state_bank(n),
                                                             ALU.mult, ALU.add)
                    else:
                        ins = nc.vector.tensor_copy(state[:, h % 2, 1, :], state_bank(n))
                    if n < N_CHUNK - 2:
                        ins.then_inc(state_made, 1)
                    else:
                        ins.then_inc(evacuated[JOB[f"gds{h}"] % 2], 1)

            def gla_norm(h):
                wait_product(dve, f"goinv{h}")
                rstd = of(f"goinv{h}")
                for j in range(2):
                    step(nc.vector.scalar_tensor_tensor(tmp[:, j, :], g_o[j][:, h, :], col(f"gla_n{j}"), rstd[:, :], ALU.mult, ALU.mult))
                    if j:
                        release(f"gosum{h}")
                    wait_evacuated(dve, f"gg{2 * h + j}")
                    nc.vector.tensor_tensor(gsilu[:, 2 * h + j, :], tmp[:, j, :], gsilu[:, 2 * h + j, :], ALU.mult).then_inc(go_made, 1)

            def gla_split(h):
                for j in range(2):
                    k = 2 * h + j
                    dve.wait_ge(go_rounded, k + 1)
                    nc.vector.tensor_tensor(h_lo[:, k, :], gsilu[:, k, :], h_hi[:, k, :].bitcast(F32), ALU.subtract).then_inc(go_split, 1)

            for stage, h in GLA_STAGES:
                if stage == "scores":
                    gla_scores(h)
                elif stage == "sum":
                    roots_on_diagonal(f"gosum{h}")
                elif stage == "norm":
                    gla_norm(h)
                elif stage == "split":
                    gla_split(h)
            for l in range(DEPTH):
                if l == 1:
                    zero_sum("mixpre1")
                    for k in range(KT):
                        add_square(k, "mixpre1")
                    dve.wait_ge(root_ready, ROOTED.index("mixpre1") + 1)
                    step(nc.vector.reciprocal(inv_root, root))
                    on_diagonal(inv_root)
                    dve.wait_ge(late_inverse, 1)
                    step(nc.vector.tensor_copy(spare[:, :], late_inverse_bank[:, :]))

                    def projected(name, n, out, bias, *scale):
                        wait_product(dve, name)
                        nc.vector.tensor_tensor(out, of(name)[:, :], spare[:, :], ALU.mult).then_inc(evacuated[JOB[name] % 2], 1)
                        wait_evacuated(dve, name)
                        nc.vector.tensor_scalar(out, out, bias, *(scale or [None]), *([ALU.add] + [ALU.mult] * len(scale))).then_inc(swa_biased, 1)
                        dve.wait_ge(swa_biased, n + 1)

                    for j in range(KT):
                        projected(f"sq{j}", j, sq_q[:, j, :], col("swa_b_q", j), SCALE)
                        if j:
                            rest_of_queries("swa0", j - 1, sq_q[:, j - 1, :])
                    projected("sv", KT, diag[:, :], col("swa_bv"))
                    rest_of_queries("swa0", KT - 1, sq_q[:, KT - 1, :])
                    for g in range(2):
                        projected(f"sk{g}", KT + 1 + g, sk[:, g, :], col(f"swa_bk{g}"))
                        rest_of_keys(5 + g, sk[:, g, :], k_swa[0][:, g, :], k_swa[1][:, g, :])
                    attention_stream(dve, STREAMS[2], attention_begin, pair_of_heads)
                    concat("scat", 2)
                zero_sum(f"mixpost{l}")
                for j in range(KT):
                    name = f"mix{l}.{j}"
                    wait_product(dve, name)
                    if l == 0:
                        ins = nc.vector.tensor_copy(m[:, j, :], of(name)[:, :])
                    else:
                        ins = nc.vector.tensor_scalar(m[:, j, :], of(name)[:, :], col("swa_b_out", j), None, ALU.add)
                    ins.then_inc(evacuated[JOB[name] % 2], 1)
                    add_square(j, f"mixpost{l}")

                def add_normed(name):
                    follow = FOLLOWED.get(name)
                    rstd = inverse(f"sum.{name}")
                    b = SUMMED.index(name)

                    def scaled(k):
                        if b or k >= 2:
                            dve.wait_ge(x_added[k % 2], KT // 2 * b + k // 2)
                        nc.vector.scalar_tensor_tensor(tmp[:, k % 2, :], m[:, k, :], col(name, k), rstd, ALU.mult, ALU.mult).then_inc(m_scaled, 1)

                    def rest_of_gained(k):
                        dve.wait_ge(gain_rounded, KT * GAINED.index(follow) + k + 1)
                        nc.vector.scalar_tensor_tensor(h_lo[:, k, :], x[:, k, :], col(follow, k), h_hi[:, k, :].bitcast(F32),
                                                       ALU.mult, ALU.subtract).then_inc(gain_split[0], 1)

                    scaled(0)
                    for k in range(0, KT, 2):
                        scaled(k + 1)
                        dve.wait_ge(m_scaled, KT * b + k + 1)
                        nc.vector.tensor_tensor(x[:, k, :], x[:, k, :], tmp[:, 0, :], ALU.add).then_inc(x_added[0], 1)
                        if k + 2 < KT:
                            scaled(k + 2)
                        if follow and k:
                            rest_of_gained(k - 2)
                    dve.wait_ge(m_scaled, KT * (b + 1))
                    release(f"sum.{name}")
                    if follow:
                        rest_of_gained(KT - 2)

                add_normed(f"mixpost{l}")
                for half in range(2):
                    up_relu(l, half)
                    if half:
                        wait_product(dve, f"sum.mlppre{l}")
                        nc.vector.tensor_scalar(mean_sq[:, :], of(f"sum.mlppre{l}")[:, 0:TT], EPS, None, ALU.add).then_inc(
                            evacuated[JOB[f"sum.mlppre{l}"] % 2], 1)
                        wait_evacuated(dve, f"sum.mlppre{l}")
                        step(nc.vector.scalar_tensor_tensor(eps_out[:, :], mean_sq[:, :], EPS, mean_sq[:, :], ALU.mult, ALU.mult))
                    down(f"mdown{l}{half}", 2, 2, f"mlppost{l}" if half else f"mlppre{l}", m, half == 1)
                add_normed(f"mlppost{l}")


def by_columns(w):
    k, n = w.shape
    pad = -n % P
    if pad:
        w = np.concatenate([w, np.zeros((k, pad), w.dtype)], 1)
    n = (n + pad) // P
    return w.reshape(k // P, P, n, P).transpose(2, 1, 0, 3).reshape(n, P, k)


def by_rows_of(w, per_tile):
    f, n = w.shape
    pad = per_tile * D - f
    if pad:
        w = np.concatenate([w, np.zeros((pad, n), w.dtype)], 0)
    return w.reshape(per_tile, KT, P, n // P, P).transpose(3, 0, 2, 1, 4).reshape(-1, P, D)


def interleave(a, b):
    return np.stack([a, b], 1).reshape(-1, *a.shape[1:])


def twice(w):
    return np.concatenate([w, w], 1)


def weight_stream(v):
    out = []
    w = v["dsa_w_in"][0]
    q, ckv, k_rope, q_idx, k_idx, w_idx, q_mem = np.split(w, np.cumsum([768, 128, 16, 512, 64, 8]).tolist(), 1)
    gap = np.zeros((D, HD - ROPE), w.dtype)
    out += [by_columns(a) for a in (ckv, twice(k_idx), q_idx, w_idx, twice(np.concatenate([k_rope, gap], 1)), q, v["mem_w_kv"][0], q_mem, v["mem_w_kv"][1])]
    for l in range(DEPTH):
        if l == 1:
            w = v["nsa_w_in"][0]
            q, kc, vc, ks, vs, kw, vw, gates, q_mem = np.split(w, np.cumsum([768] + [128] * 6 + [36]).tolist(), 1)
            for a in (kc, vc, ks, kw):
                out += [by_columns(twice(a[:, 0:HD])), by_columns(twice(a[:, HD:]))]
            out += [by_columns(a) for a in (q, vs, vw, gates, q_mem)]
        out.append(by_columns(v["w_o"][l]))
        gate, upw = np.split(v["ffn_w_in"][l], 2, 1)
        out.append(interleave(by_columns(gate), by_columns(upw)))
        out.append(by_rows_of(v["ffn_w_down"][l], 3))
    w = v["gla_w_in_2"][0]
    q, k, vv, g, glr = np.split(w, np.cumsum([512, 512, 1024, 1024]).tolist(), 1)
    out += [by_columns(a) for a in (glr, k, q, vv, g)]
    for l in range(DEPTH):
        if l == 1:
            w = v["swa_w_in_2"][0]
            q, k, vv = np.split(w, [1024, 1152], 1)
            out += [by_columns(a) for a in (q, vv, twice(k[:, 0:HD]), twice(k[:, HD:]))]
        out.append(by_columns(v["gla_w_out_2"][0] if l == 0 else v["swa_w_out_2"][0]))
        upw, downw = v["mlp_w_up_2"][l], v["mlp_w_down_2"][l]
        for half in range(2):
            f = slice(half * D_FF2 // 2, (half + 1) * D_FF2 // 2)
            out += [by_columns(upw[:, f]), by_rows_of(downw[f], 2)]
    return np.concatenate(out, 0)


def shape_constants():
    inv = 500000.0 ** (-np.arange(0, ROPE, 2, dtype=np.float64) / ROPE)
    ang = np.arange(SEQ, dtype=np.float64)[:, None] * inv[None, :]
    cos, sin = np.cos(ang).astype(np.float32).T, np.sin(ang).astype(np.float32).T
    c, s, perm = np.ones((P, SEQ), np.float32), np.zeros((P, SEQ), np.float32), np.zeros((P, P), np.float32)
    half = ROPE // 2
    for o in (0, HD):
        for d in range(half):
            c[o + d] = c[o + half + d] = cos[d]
            s[o + d] = s[o + half + d] = sin[d]
            perm[o + half + d, o + d] = -1.0
            perm[o + d, o + half + d] = 1.0
    a = np.arange(P)
    prev = np.where(a[None, :] > a[:, None], 0.0, NEG)
    own = np.where(a[None, :] <= a[:, None], 0.0, NEG)
    blocks = np.arange(32)
    cmp_ = [np.where((blocks * 16 + 31)[None, :] <= (t * P + a)[:, None], 0.0, NEG) for t in range(TT)]
    masks = np.concatenate([prev, own] + cmp_, 1).astype(np.float32)
    same = (a[:, None] // GLA_CHUNK == a[None, :] // GLA_CHUNK) & (a[:, None] <= a[None, :])
    return {"ident": np.eye(P, dtype=np.float32), "perm": perm, "rope_c": c, "rope_s": s, "masks": masks, "gla_mask": same.astype(np.int32)}


def lay_out(v):
    f = {n: np.asarray(a) for n, a in v.items()}
    vec = {"final": f["final_norm"], "swa_b_out": f["swa_b_out_2"][0], "swa_b_q": f["swa_b_in_2"][0][0:D]}
    for l in range(DEPTH):
        for name, src in (("attn", "attn_norm"), ("ffn", "ffn_norm"), ("mem", "mem_norm"), ("mixpre", "ln_mix_pre_2"),
                          ("mixpost", "ln_mix_post_2"), ("mlppre", "ln_mlp_pre_2"), ("mlppost", "ln_mlp_post_2")):
            vec[f"{name}{l}"] = f[src][l]
    bk = f["swa_b_in_2"][0][D:D + 2 * HD].reshape(2, HD)
    columns = [vec[n].reshape(KT, P).T for n in GAINS] + [f["dsa_ckv_norm"][0][:, None], f["gla_b_gate_up_2"][0].reshape(4, P).T,
               f["gla_g_norm_2"][0].reshape(2, P).T] + [np.concatenate([b, b])[:, None] for b in bk] + [f["swa_b_in_2"][0][D + 2 * HD:, None]]
    gap = np.zeros((P, ROPE), np.float32)
    uk = f["dsa_w_uk"][0]
    pairs = lambda a: a.reshape(CMP_PAIRS, P, -1).transpose(1, 0, 2)
    out = {
        "weights": weight_stream(f),
        "memT": f["mem"][0].T.reshape(KT, P, N_MEM).transpose(1, 0, 2),
        "xT": f["x"][0].T.reshape(KT, P, SEQ).transpose(1, 0, 2),
        "cols": np.concatenate(columns, 1),
        "w_uk": np.concatenate([gap, uk, gap, uk], 1),
        "w_uv": f["dsa_w_uv"][0],
        "sinks": np.broadcast_to(f["swa_sinks_2"][0][None, :], (P, 16)),
        "cmp_w1": np.stack([pairs(f["nsa_cmp_k_w1"][0]), pairs(f["nsa_cmp_v_w1"][0])]),
        "cmp_pos": np.stack([f[f"nsa_cmp_pos_{c}"][0].reshape(CMP_PAIRS, P).T for c in "kv"]),
        "cmp_w2k": twice(f["nsa_cmp_k_w2"][0]),
        "cmp_w2v": f["nsa_cmp_v_w2"][0],
        "w_gate": f["gla_w_gate_up_2"][0],
    }
    out.update(shape_constants())
    return {"in_" + n: np.ascontiguousarray(a) for n, a in out.items()}


def build(nc, arrays):
    A = {n[3:]: nc.dram_tensor(n, a.shape, mybir.dt.from_np(a.dtype), kind="ExternalInput").ap() for n, a in arrays.items()}
    A["out"] = nc.dram_tensor("out", (KT, P, SEQ), F32, kind="ExternalOutput").ap()
    program(nc, A)


def kernel(**inputs):
    import concourse.bacc as bacc
    from concourse.bass_utils import run_bass_kernel_spmd

    arrays = lay_out(inputs)
    nc = bacc.Bacc("TRN2", target_bir_lowering=False, num_devices=1)
    build(nc, arrays)
    r = run_bass_kernel_spmd(nc, [arrays], core_ids=[0])
    return np.ascontiguousarray(r.results[0]["out"].reshape(D, SEQ).T)[None]
```
